# Optimizing a Trainium2 kernel written in Bass

```python
import functools
import jax
import jax.numpy as jnp
from jax import lax
import numpy as np

D_MODEL = 1024
BATCH = 1
SEQ = 512
DEPTH = 1
DEC_BATCH = 8
DEC_SEQ = 8
PAST_LEN = 4096
PAGE_SIZE = 128

POOL_WIDTH = D_MODEL // 2
POOL_WINDOWS = (2, 4, 8, 16)
N_POOL_GROUPS = len(POOL_WINDOWS)
POOL_GROUP = POOL_WIDTH // N_POOL_GROUPS
POOL_HIST = max(POOL_WINDOWS) - 1
N_HEADS = 8
HEAD_DIM = 64
ATTN_WIDTH = N_HEADS * HEAD_DIM
MOBA_BLOCK = 256
MOBA_TOPK = 3
Q_BLOCK = 128
ATTN_SCALE = HEAD_DIM ** -0.5
MIX_IN = POOL_WIDTH + 3 * ATTN_WIDTH
MIX_WIDTH = POOL_WIDTH + ATTN_WIDTH
N_GROUPS = 4
EXPERTS_PER_GROUP = 8
N_EXPERTS = N_GROUPS * EXPERTS_PER_GROUP
EXPERT_TOPK = 2
D_FF_EXPERT = D_MODEL // 2
ROW_BLOCK = 128
EPS = 1e-6

kernel_name = 'hymba_pool_moba_hmoe_step'

def _rmsnorm(x, g):
    xf = x.astype(jnp.float32)
    y = xf * lax.rsqrt(jnp.mean(xf * xf, axis=-1, keepdims=True) + EPS)
    return (y * g.astype(jnp.float32)).astype(x.dtype)

def _alibi_slopes():
    return jnp.exp2(-8.0 * (jnp.arange(N_HEADS, dtype=jnp.float32) + 1.0) / N_HEADS)

def _pool_mix(u_ext, pos0, w_pool, pool_scale):
    f32 = jnp.float32
    B, Lx, _ = u_ext.shape
    L = Lx - POOL_HIST
    uf = u_ext.astype(f32)
    cz = jnp.concatenate([jnp.zeros((B, 1, POOL_WIDTH), f32), jnp.cumsum(uf, axis=1)], axis=1)
    end = cz[:, POOL_HIST + 1:]
    u = uf[:, POOL_HIST:]
    pos = pos0 + jnp.arange(L)
    groups = []
    for g, w in enumerate(POOL_WINDOWS):
        ch = slice(g * POOL_GROUP, (g + 1) * POOL_GROUP)
        win_sum = end[..., ch] - cz[:, POOL_HIST + 1 - w:POOL_HIST + 1 - w + L, ch]
        count = jnp.minimum(pos + 1, w).astype(f32)[None, :, None]
        groups.append(win_sum / count - u[..., ch])
    pooled = jnp.stack(groups, axis=2)
    y = jnp.einsum('blgc,gcd->blgd', pooled, w_pool.astype(f32)).reshape(B, L, POOL_WIDTH)
    return y * pool_scale.astype(f32)

def _moba_prompt(q, k, v):
    f32 = jnp.float32
    B, T = q.shape[:2]
    S = MOBA_BLOCK
    NB = -(-T // S)
    pad = NB * S - T
    kp = jnp.pad(k.astype(f32), ((0, 0), (0, pad), (0, 0), (0, 0)))
    vp = jnp.pad(v.astype(f32), ((0, 0), (0, pad), (0, 0), (0, 0)))
    kb = kp.reshape(B, NB, S, N_HEADS, HEAD_DIM).transpose(0, 3, 1, 2, 4)
    vb = vp.reshape(B, NB, S, N_HEADS, HEAD_DIM).transpose(0, 3, 1, 2, 4)
    kmean = kb.mean(axis=3)
    ktop = min(MOBA_TOPK, NB - 1)
    slopes = _alibi_slopes()
    nq = T // Q_BLOCK
    qb = q.astype(f32).reshape(B, nq, Q_BLOCK, N_HEADS, HEAD_DIM).transpose(1, 0, 3, 2, 4)
    bi = jnp.arange(B)[:, None, None, None]
    hi = jnp.arange(N_HEADS)[None, :, None, None]
    s_idx = jnp.arange(S)

    def one_block(args):
        qc, c = args
        t = c * Q_BLOCK + jnp.arange(Q_BLOCK)
        cb = (c * Q_BLOCK) // S
        ko = lax.dynamic_index_in_dim(kb, cb, axis=2, keepdims=False)
        vo = lax.dynamic_index_in_dim(vb, cb, axis=2, keepdims=False)
        so = cb * S + s_idx
        lo = jnp.einsum('bhqd,bhsd->bhqs', qc, ko) * ATTN_SCALE - slopes[:, None, None] * (t[:, None] - so[None, :])
        lo = jnp.where(so[None, :] <= t[:, None], lo, -jnp.inf)
        if ktop == 0:
            return jnp.einsum('bhqs,bhsd->bhqd', jax.nn.softmax(lo, axis=-1), vo)
        gate = jnp.einsum('bhqd,bhnd->bhqn', qc, kmean)
        gate = jnp.where(jnp.arange(NB) < cb, gate, -jnp.inf)
        _, sel = lax.top_k(gate, ktop)
        ks = kb[bi, hi, sel]
        vs = vb[bi, hi, sel]
        ps = sel[..., None] * S + s_idx
        ls = jnp.einsum('bhqd,bhqjsd->bhqjs', qc, ks) * ATTN_SCALE - slopes[:, None, None, None] * (t[:, None, None] - ps)
        ls = jnp.where((sel < cb)[..., None], ls, -jnp.inf)
        n_sel = ktop * S
        p = jax.nn.softmax(jnp.concatenate([ls.reshape(B, N_HEADS, Q_BLOCK, n_sel), lo], axis=-1), axis=-1)
        p_sel = p[..., :n_sel].reshape(B, N_HEADS, Q_BLOCK, ktop, S)
        return jnp.einsum('bhqjs,bhqjsd->bhqd', p_sel, vs) + jnp.einsum('bhqs,bhsd->bhqd', p[..., n_sel:], vo)

    out = lax.map(one_block, (qb, jnp.arange(nq)))
    return out.transpose(1, 0, 3, 2, 4).reshape(B, T, ATTN_WIDTH)

def _moba_sample(q, k, v, cache_k, cache_v, page_table, layer):
    f32 = jnp.float32
    B, L = q.shape[:2]
    slopes = _alibi_slopes()
    ppb = MOBA_BLOCK // PAGE_SIZE
    cb = PAST_LEN // MOBA_BLOCK
    n_own = PAST_LEN - cb * MOBA_BLOCK
    ktop = min(MOBA_TOPK, cb)
    t = PAST_LEN + jnp.arange(L)
    qh = q.astype(f32).transpose(0, 2, 1, 3)
    logit_parts, value_parts = [], []
    if ktop > 0:
        past = cache_k[layer, page_table[:, :cb * ppb]].astype(f32)
        kmean = past.reshape(B, cb, MOBA_BLOCK, N_HEADS, HEAD_DIM).mean(axis=2)
        gate = jnp.einsum('bhqd,bnhd->bhqn', qh, kmean)
        _, sel = lax.top_k(gate, ktop)
        bi5 = jnp.arange(B)[:, None, None, None, None]
        hi5 = jnp.arange(N_HEADS)[None, :, None, None, None]
        phys = page_table[bi5, sel[..., None] * ppb + jnp.arange(ppb)]
        n_sel = ktop * MOBA_BLOCK
        ks = cache_k[layer, phys, :, hi5].astype(f32).reshape(B, N_HEADS, L, n_sel, HEAD_DIM)
        vs = cache_v[layer, phys, :, hi5].astype(f32).reshape(B, N_HEADS, L, n_sel, HEAD_DIM)
        ps = (sel[..., None] * MOBA_BLOCK + jnp.arange(MOBA_BLOCK)).reshape(B, N_HEADS, L, n_sel)
        ls = jnp.einsum('bhqd,bhqsd->bhqs', qh, ks) * ATTN_SCALE - slopes[:, None, None] * (t[:, None] - ps)
        logit_parts.append(ls)
        value_parts.append(('bhqs,bhqsd->bhqd', vs))
    if n_own > 0:
        own_pages = page_table[:, cb * ppb:cb * ppb + n_own // PAGE_SIZE]
        ko = cache_k[layer, own_pages].astype(f32).reshape(B, n_own, N_HEADS, HEAD_DIM)
        vo = cache_v[layer, own_pages].astype(f32).reshape(B, n_own, N_HEADS, HEAD_DIM)
        po = cb * MOBA_BLOCK + jnp.arange(n_own)
        lo = jnp.einsum('bhqd,bshd->bhqs', qh, ko) * ATTN_SCALE - slopes[:, None, None] * (t[:, None] - po[None, :])
        logit_parts.append(lo)
        value_parts.append(('bhqs,bshd->bhqd', vo))
    kf = k.astype(f32)
    ln = jnp.einsum('bhqd,bshd->bhqs', qh, kf) * ATTN_SCALE - slopes[:, None, None] * (t[:, None] - t[None, :])
    ln = jnp.where(t[None, :] <= t[:, None], ln, -jnp.inf)
    logit_parts.append(ln)
    value_parts.append(('bhqs,bshd->bhqd', v.astype(f32)))
    p = jax.nn.softmax(jnp.concatenate(logit_parts, axis=-1), axis=-1)
    out = None
    off = 0
    for lp, (eq, val) in zip(logit_parts, value_parts):
        n = lp.shape[-1]
        term = jnp.einsum(eq, p[..., off:off + n], val)
        out = term if out is None else out + term
        off += n
    return out.transpose(0, 2, 1, 3).reshape(B, L, ATTN_WIDTH)

def _routed_experts(x, expert, weight, w_gate, w_up, w_down):
    N, D = x.shape
    A = expert.shape[0]
    token = jnp.arange(A) // EXPERT_TOPK
    order = jnp.argsort(expert)
    e_s, tok_s, w_s = expert[order], token[order], weight[order]
    counts = jnp.zeros((N_EXPERTS,), jnp.int32).at[expert].add(1)
    start = jnp.cumsum(counts) - counts
    padded = (counts + ROW_BLOCK - 1) // ROW_BLOCK * ROW_BLOCK
    pend = jnp.cumsum(padded)
    pstart = pend - padded
    dest = pstart[e_s] + jnp.arange(A) - start[e_s]
    n_blocks = A // ROW_BLOCK + N_EXPERTS
    row_tok = jnp.zeros((n_blocks * ROW_BLOCK,), jnp.int32).at[dest].set(tok_s)
    blk_e = jnp.minimum(jnp.searchsorted(pend, jnp.arange(n_blocks) * ROW_BLOCK, side='right'), N_EXPERTS - 1)
    xr = x[row_tok].reshape(n_blocks, ROW_BLOCK, D)

    def expert_block(args):
        xb, e = args
        return (jax.nn.silu(xb @ w_gate[e]) * (xb @ w_up[e])) @ w_down[e]

    yr = lax.map(expert_block, (xr, blk_e)).reshape(n_blocks * ROW_BLOCK, D)
    contrib = yr[dest].astype(jnp.float32) * w_s[:, None]
    return jax.ops.segment_sum(contrib, tok_s, num_segments=N)

def _hier_moe(h, w_group, b_group, w_expert, b_expert, w_gate, w_up, w_down):
    f32 = jnp.float32
    B, L, D = h.shape
    x = h.reshape(B * L, D)
    xf = x.astype(f32)
    g_prob = jax.nn.softmax(xf @ w_group.astype(f32) + b_group.astype(f32), axis=-1)
    g_w, g_idx = lax.top_k(g_prob, 1)
    e_logits = (xf @ w_expert.astype(f32) + b_expert.astype(f32)).reshape(-1, N_GROUPS, EXPERTS_PER_GROUP)
    e_in = e_logits[jnp.arange(B * L), g_idx[:, 0]]
    e_top, e_loc = lax.top_k(e_in, EXPERT_TOPK)
    weights = jax.nn.softmax(e_top, axis=-1) * g_w
    experts = g_idx * EXPERTS_PER_GROUP + e_loc
    y = _routed_experts(x, experts.reshape(-1), weights.reshape(-1), w_gate, w_up, w_down)
    return y.reshape(B, L, D).astype(h.dtype)

def _layer(x, c, pool_hist, pos0, attend, w_ada, b_ada, g_attn_norm, w_in, g_q, g_k, w_pool, pool_scale,
           w_out, g_ffn_norm, w_group, b_group, w_expert, b_expert, w_gate, w_up, w_down):
    B, L, _ = x.shape
    mod = (jax.nn.silu(c) @ w_ada + b_ada)[:, None, :]
    sh1, sc1, gt1, sh2, sc2, gt2 = jnp.split(mod, 6, axis=-1)
    h = _rmsnorm(x, g_attn_norm) * (1 + sc1) + sh1
    z = h @ w_in
    u, q, k, v = jnp.split(z, [POOL_WIDTH, POOL_WIDTH + ATTN_WIDTH, POOL_WIDTH + 2 * ATTN_WIDTH], axis=-1)
    q = _rmsnorm(q.reshape(B, L, N_HEADS, HEAD_DIM), g_q)
    k = _rmsnorm(k.reshape(B, L, N_HEADS, HEAD_DIM), g_k)
    v = v.reshape(B, L, N_HEADS, HEAD_DIM)
    u_ext = jnp.concatenate([pool_hist.astype(u.dtype), u], axis=1)
    y_pool = _pool_mix(u_ext, pos0, w_pool, pool_scale)
    y_attn = attend(q, k, v)
    mix = jnp.concatenate([y_pool.astype(x.dtype), y_attn.astype(x.dtype)], axis=-1) @ w_out
    x = x + gt1 * mix
    h2 = _rmsnorm(x, g_ffn_norm) * (1 + sc2) + sh2
    x = x + gt2 * _hier_moe(h2, w_group, b_group, w_expert, b_expert, w_gate, w_up, w_down)
    return x, k, v, u_ext[:, -POOL_HIST:]

def setup_inputs(seed: int = 0) -> dict:
    key = jax.random.key(seed)
    ks = jax.random.split(key, 32)
    f32 = jnp.float32
    D = D_MODEL
    n_pages = PAST_LEN // PAGE_SIZE
    n_used = DEC_BATCH * n_pages
    n_phys = n_used + max(1, n_used // 4)

    def nrm(k, shape, scale):
        return jax.random.normal(k, shape, f32) * scale

    return {
        'x_prompt': nrm(ks[0], (BATCH, SEQ, D), 1.0),
        'x_sample': nrm(ks[1], (DEC_BATCH, DEC_SEQ, D), 1.0),
        'cache_k': nrm(ks[2], (DEPTH, n_phys, PAGE_SIZE, N_HEADS, HEAD_DIM), 1.0),
        'cache_v': nrm(ks[3], (DEPTH, n_phys, PAGE_SIZE, N_HEADS, HEAD_DIM), 1.0),
        'state_pool': nrm(ks[4], (DEPTH, DEC_BATCH, POOL_HIST, POOL_WIDTH), 1.0),
        'page_table': jax.random.permutation(ks[5], n_phys)[:n_used].reshape(DEC_BATCH, n_pages).astype(jnp.int32),
        'c_prompt': nrm(ks[6], (BATCH, D), 1.0),
        'c_sample': nrm(ks[7], (DEC_BATCH, D), 1.0),
        'w_ada': nrm(ks[8], (DEPTH, D, 6 * D), 0.5 * D ** -0.5),
        'b_ada': nrm(ks[9], (DEPTH, 6 * D), 0.01),
        'g_attn_norm': 1.0 + nrm(ks[10], (DEPTH, D), 0.02),
        'w_in': nrm(ks[11], (DEPTH, D, MIX_IN), D ** -0.5),
        'g_q': 1.0 + nrm(ks[12], (DEPTH, HEAD_DIM), 0.02),
        'g_k': 1.0 + nrm(ks[13], (DEPTH, HEAD_DIM), 0.02),
        'w_pool': nrm(ks[14], (DEPTH, N_POOL_GROUPS, POOL_GROUP, POOL_GROUP), POOL_GROUP ** -0.5),
        'pool_scale': 1.0 + nrm(ks[15], (DEPTH, POOL_WIDTH), 0.02),
        'w_out': nrm(ks[16], (DEPTH, MIX_WIDTH, D), MIX_WIDTH ** -0.5),
        'g_ffn_norm': 1.0 + nrm(ks[17], (DEPTH, D), 0.02),
        'w_group': nrm(ks[18], (DEPTH, D, N_GROUPS), D ** -0.5),
        'b_group': nrm(ks[19], (DEPTH, N_GROUPS), 0.01),
        'w_expert': nrm(ks[20], (DEPTH, D, N_EXPERTS), D ** -0.5),
        'b_expert': nrm(ks[21], (DEPTH, N_EXPERTS), 0.01),
        'w_gate': nrm(ks[22], (DEPTH, N_EXPERTS, D, D_FF_EXPERT), D ** -0.5),
        'w_up': nrm(ks[23], (DEPTH, N_EXPERTS, D, D_FF_EXPERT), D ** -0.5),
        'w_down': nrm(ks[24], (DEPTH, N_EXPERTS, D_FF_EXPERT, D), D_FF_EXPERT ** -0.5),
    }

def reference(x_prompt, x_sample, cache_k, cache_v, state_pool, page_table, c_prompt, c_sample,
              w_ada, b_ada, g_attn_norm, w_in, g_q, g_k, w_pool, pool_scale, w_out, g_ffn_norm,
              w_group, b_group, w_expert, b_expert, w_gate, w_up, w_down):
    hp, hs = x_prompt, x_sample
    kp_l, vp_l, pp_l, ks_l, vs_l, ps_l = [], [], [], [], [], []
    hist0 = jnp.zeros((x_prompt.shape[0], POOL_HIST, POOL_WIDTH), x_prompt.dtype)
    for l in range(DEPTH):
        lw = (w_ada[l], b_ada[l], g_attn_norm[l], w_in[l], g_q[l], g_k[l], w_pool[l], pool_scale[l],
              w_out[l], g_ffn_norm[l], w_group[l], b_group[l], w_expert[l], b_expert[l],
              w_gate[l], w_up[l], w_down[l])
        hp, kp, vp, pp = _layer(hp, c_prompt, hist0, 0, _moba_prompt, *lw)
        attend_s = functools.partial(_moba_sample, cache_k=cache_k, cache_v=cache_v,
                                     page_table=page_table, layer=l)
        hs, ksm, vsm, psm = _layer(hs, c_sample, state_pool[l], PAST_LEN, attend_s, *lw)
        kp_l.append(kp)
        vp_l.append(vp)
        pp_l.append(pp)
        ks_l.append(ksm)
        vs_l.append(vsm)
        ps_l.append(psm)
    return (hp, hs, jnp.stack(kp_l), jnp.stack(vp_l), jnp.stack(pp_l), jnp.stack(ks_l), jnp.stack(vs_l), jnp.stack(ps_l))


_drawn_inputs = setup_inputs


def setup_inputs(seed=0):
    import zlib

    import numpy as np

    out = dict(_drawn_inputs(seed))
    spreads = {}
    factors = {'cache_v': 3.164,
     'b_ada': 3.716,
     'g_attn_norm': 2.992,
     'g_q': 8.0,
     'g_k': 2.809,
     'pool_scale': 8.0,
     'g_ffn_norm': 5.665,
     'b_group': 8.0,
     'b_expert': 31.433}
    for name, (base, spread) in spreads.items():
        noise = np.random.default_rng([zlib.crc32(name.encode()), seed]).standard_normal(out[name].shape)
        drawn = base * np.exp(spread * noise) if base else spread * noise
        out[name] = jnp.asarray(drawn.astype(out[name].dtype))
    for name, factor in factors.items():
        out[name] = (out[name] * factor).astype(out[name].dtype)
    return out
```

```python
import concourse.bass as bass
from concourse import mybir
from contextlib import ExitStack
import numpy as np

D = 1024
NP, NB, NQ = 512, 8, 8
NS = NB * NQ
NT = NP + NS
KT = D // 128
NSEQ = 1 + NB
PW, AW, HD, NH = 512, 512, 64, 8
HIST = 15
PAST, PAGE, BLK, TOPK = 4096, 128, 256, 3
NBLK = PAST // BLK
CH = 512
NCH = PAST // CH
PPC = CH // PAGE
NE, FF = 32, 512
RB = 64
MAXBLK = NE + 2 * NT // RB
NOV = MAXBLK - NE
TT = (NT + 127) // 128
EPS = 1e-6
OFF = -1e30
U = 4096
US = HIST + NQ
UW = HIST + NP + NB * US


def const_layout():
    at, out = 0, {}
    for name, width in (("ident", 128), ("sel", NSEQ), ("heads", 128), ("before", 128), ("causal", NP),
                        ("jbias", BLK), ("blockoff", NBLK), ("newbias", NB * NS), ("iota", 64),
                        ("share", 4 * 16), ("valid", TT), ("payload", TT * 4), ("thr", 16),
                        ("slopes", NH), ("eps", 1), ("two", 16), ("ovid", NOV), ("half", 1), ("dump", 1)):
        out[name] = (at, width)
        at += width
    return out, at


def build_kernel(nc, d, o):
    f32, i32, u32 = mybir.dt.float32, mybir.dt.int32, mybir.dt.uint32
    ALU, ACT, AX = mybir.AluOpType, mybir.ActivationFunctionType, mybir.AxisListType
    ds = bass.ds
    ctx = ExitStack()
    with ctx:
        def sb(name, shape, dt=f32):
            return ctx.enter_context(nc.sbuf_tensor(name, shape, dt))

        def sem(name):
            return ctx.enter_context(nc.semaphore(name))

        ring = sb("ring", [128, 6 * U])
        xP, xS = sb("xP", [128, KT, NP]), sb("xS", [128, KT, NS])
        hP, hS = sb("hP", [128, KT, NP]), sb("hS", [128, KT, NS])
        mP, mS = hP, hS
        qP, kP = sb("qP", [128, 4, NP]), sb("kP", [128, 4, NP])
        vP = sb("vP", [128, NP // 128, AW])
        qS, kS = sb("qS", [128, 4, NS]), sb("kS", [128, 4, NS])
        vS = sb("vS", [128, AW])
        modT = sb("modT", [128, 6 * KT, NSEQ])
        big = sb("big", [128, PAST + 128 + 33 * 64])
        L = big[:, 0:PAST + 128]
        PT = big[:, PAST + 128:PAST + 128 + 33 * 64].rearrange("p (t c) -> p t c", c=64)
        uX = big[:, 1536:1536 + 4 * UW].rearrange("p (g t) -> p g t", g=4)
        sq = big[:, 0:KT * NT].rearrange("p (k t) -> p k t", t=NT)
        CL, CW = const_layout()
        cst = sb("cst", [128, CW])
        C = {n: cst[:, a:a + w] for n, (a, w) in CL.items()}
        ones = sb("ones", [128, 128])
        cT = ring[:, 4 * U + 512:4 * U + 512 + KT * NSEQ].rearrange("p (k s) -> p k s", s=NSEQ)
        scT = sb("scT", [128, KT, 32])
        part = sb("part", [128, 512])
        coef = part[:, 256:256 + KT * NSEQ].rearrange("p (k s) -> p k s", s=NSEQ)
        gcols = sb("gcols", [128, 2 * KT + 2 + 4])
        g1, g2 = gcols[:, 0:KT], gcols[:, KT:2 * KT]
        gq, gk = gcols[:, 2 * KT:2 * KT + 1], gcols[:, 2 * KT + 1:2 * KT + 2]
        pscale = gcols[:, 2 * KT + 2:2 * KT + 6]
        rstd = sb("rstd", [128, NT])
        qbd = sb("qbd", [128, NB, 4, 32])
        qst = sb("qst", [128, 4, 32])
        pages = sb("pages", [1, NB * PAST // PAGE], i32)
        gsum, bmax, pen, ebias = (sb(n, [128, NBLK]) for n in ("gsum", "bmax", "pen", "ebias"))
        top8, topf = sb("top8", [128, 8]), sb("topf", [128, 8])
        topi = sb("topi", [128, 8], u32)
        st = sb("st", [128, 8])
        nmax, gmax_, negm, tot, rinv = (st[:, i:i + 1] for i in range(5))
        esum = sb("esum", [128, NBLK + 1])
        On = part[:, 0:128]
        wrt = sb("wrt", [128, KT, 36])
        brt = sb("brt", [128, 36])

        bT = ring[:, 5 * U:5 * U + 6 * KT * NSEQ].rearrange("p (c s) -> p c s", s=NSEQ)
        wpool = ring[:, 4 * U:4 * U + 512].rearrange("p (g n) -> p g n", g=4)
        win1, win2 = big[:, 0:UW], big[:, UW:2 * UW]
        pooledP = hP[:, 4:8, :]
        pooledS = qbd[:, :, :, :].rearrange("p b j c -> p (b j c)")[:, 0:4 * NS]\
            .rearrange("p (g t) -> p g t", g=4)

        B = [ctx.enter_context(nc.psum_tensor(f"bank{i}", [128, 512], f32)) for i in range(8)]

        h2d = nc.dram_tensor("h2d", (2 * NT, 512), f32, kind="Internal").ap()
        y2 = nc.dram_tensor("y2", (2 * (2 * NT + RB), 512), f32, kind="Internal").ap()

        s = {n: sem(n) for n in (
            "small", "x_in", "late_in", "zeroed", "silu", "ada_part", "ada_copied", "ada_cols",
            "ada_done", "squared", "sums", "rooted", "h_scaled", "h_ready", "zP", "zS", "zP_out", "zS_out",
            "hsq", "hsum", "hroot", "normed", "qbd_ready", "pooled", "ypool", "ypool_out",
            "q_staged", "new_scored", "new_out", "k_used", "s_out", "exp_bias", "probs", "turned", "turned_out",
            "newT", "newT_out", "v_used", "o_sum", "rinv_ready", "o_scaled", "oT", "oT_out",
            "staged", "p_scores", "p_logits", "p_neg", "p_exp", "p_prob", "p_turned", "p_turned_out", "p_out", "p_stored",
            "wo_full0", "wo_full1", "mixP", "mixS", "res1", "squared2", "sums2", "rooted2", "h_scaled2", "h2_ready", "h2_turn",
            "h2_out", "h2_stored", "route_scores", "g_exp_in", "g_exp", "hot", "ranked", "listed", "lists_summed",
            "n_ready",
            "g_staged", "s_staged", "x_turned", "xT_ready", "gate_up", "silu_ready", "act_ready", "a_turned",
            "aT_ready", "down", "y_out", "w_given", "y_back", "combined", "c_turned", "final", "stored",
            "dve", "dve2", "dve3", "act", "pool", "pool2", "settle", "bank_cleared")}
        w_full = [sem(f"w_full{i}") for i in range(4)]
        k_full = [sem(f"k_full{i}") for i in range(4)]
        v_full = [sem(f"v_full{i}") for i in range(8)]
        gathered = [sem(f"gathered{i}") for i in range(2)]
        y_scat = [sem(f"y_scattered{i}") for i in range(2)]
        e_full = [[sem(f"e_full{p}{i}") for i in range(3)] for p in range(2)]

        slot = [ring[:, i * U:(i + 1) * U].rearrange("p (k n) -> p k n", k=KT) for i in range(6)]
        kslot = [ring[:, i * 2048:(i + 1) * 2048].rearrange("p (g j s) -> p g j s", g=PPC, j=4) for i in range(4)]
        vslot = [ring[:, 2 * U + i * 2048:2 * U + (i + 1) * 2048].rearrange("p (g n) -> p g n", g=PPC)
                 for i in range(8)]
        eslot = [[ring[:, ((3 - 3 * p) + i) * U:((3 - 3 * p) + i + 1) * U] for i in range(3)] for p in range(2)]

        def chain(eng, sm, start=0):
            n = [0]

            def then(ins):
                n[0] += 1
                ins.then_inc(sm, 1)
                eng.wait_ge(sm, start + n[0])
            return then, n

        pq = big[:, 0:512]
        pk = big[:, 512:1024]
        pv = big[:, 1024:1536].rearrange("p (t n) -> p t n", t=4)
        plog = [big[:, 1536 + 512 * i:2048 + 512 * i] for i in range(2)]
        pPT = [big[:, 2560:2560 + 2048].rearrange("p (t q) -> p t q", t=4),
               ring[:, 2 * U:2 * U + 2048].rearrange("p (t q) -> p t q", t=4)]
        pslope = big[:, 4608:4610]
        pst = big[:, 4612:4624]

        h2tok = big[:, 0:TT * D].rearrange("p (t n) -> p t n", t=TT)
        rs = qP[:, :, :].rearrange("p a b -> p (a b)")
        ri = kP[:, :, :].rearrange("p a b -> p (a b)")
        at = [0]

        def cut(n):
            a = at[0]
            at[0] += n
            assert at[0] <= 2048
            return rs[:, a:a + n]
        lg = cut(TT * 36).rearrange("p (t n) -> p t n", t=TT)
        lg8 = cut(TT * 8).rearrange("p (t n) -> p t n", t=TT)
        gtop = cut(TT * 8).rearrange("p (t n) -> p t n", t=TT)
        etop = cut(TT * 8).rearrange("p (t n) -> p t n", t=TT)
        ein = cut(TT * 8).rearrange("p (t n) -> p t n", t=TT)
        gif = cut(TT)
        gexp = cut(TT * 4).rearrange("p (t n) -> p t n", t=TT)
        gw = cut(TT)
        goh = cut(TT * 4).rearrange("p (t n) -> p t n", t=TT)
        gtmp = cut(TT * 32)
        edif = cut(TT)
        eex = cut(TT)
        eden = cut(TT)
        wts = sb("wts", [128, 2, TT])
        ek = cut(TT * 2)
        hot = cut(TT * 2 * 32)
        hotm = cut(TT * 32).rearrange("p (t e) -> p t e", t=TT)
        cum = cut((TT + 1) * 32).rearrange("p (t e) -> p t e", t=TT + 1)
        over, incl, base2 = cut(32), cut(32), cut(32)
        pos, ost, bno, far, blk_ = (cut(TT * 2) for _ in range(5))
        ovt = ri[:, 0:NOV * 32]
        prod = ri[:, 576:576 + TT * 2 * 32]
        past = ri[:, 1400:1400 + TT * 2 * 8]
        ti = ri[:, 1024:1024 + 300].bitcast(u32)
        gidx = ti[:, 0:TT * 8].rearrange("p (t n) -> p t n", t=TT)
        eidx = ti[:, 40:40 + TT * 8].rearrange("p (t n) -> p t n", t=TT)
        oveif = cut(NOV)
        npf = cut(2)
        nint = sb("nint", [1, 3 + NOV], i32)
        rows = vP[:, :, :].rearrange("p a b -> p (a b)")[:, 0:2 * TT * 128].rearrange("p (x h r) -> p x h r", h=2, r=RB)
        blks = ri[:, 0:2 * TT * 3 * MAXBLK].rearrange("p (x c b) -> p x c b", c=3, b=MAXBLK)
        first = sb("first", [1, 4])
        tblS = sb("tblS", [128, 2, MAXBLK + 2], u32)

        o_ = [0]

        def mo(n):
            a = o_[0]
            o_[0] += n
            assert o_[0] <= PAST + 128 + 33 * 64
            return big[:, a:a + n]
        Xg = [mo(512) for _ in range(2)]
        XT = [mo(512) for _ in range(2)]
        gs = [mo(256) for _ in range(2)]
        aa = [mo(256) for _ in range(2)]
        aT = [mo(256) for _ in range(2)]
        Yo = [mo(512) for _ in range(2)]
        gix = [sb(f"gix{i}", [128, 1], u32) for i in range(2)]
        six = [sb(f"six{i}", [128, 1], u32) for i in range(2)]
        yb = [[ring[:, (2 * i + j) * 1024:(2 * i + j + 1) * 1024] for j in range(2)] for i in range(2)]
        yc = [ring[:, (4 + i) * 1024:(5 + i) * 1024] for i in range(2)]

        block = ctx.enter_context(nc.Block())

        @block.sync
        def _(sp):
            sp.sem_inc(s["k_used"], 4)
            sp.sem_inc(s["v_used"], 8)
            sp.dma_start(cT, d["cT"].rearrange("(k p) s -> p k s", p=128)).then_inc(s["small"], 16)
            sp.dma_start(cst[:, :], d["consts"]).then_inc(s["small"], 16)
            sp.dma_start(bT, d["b_ada"]).then_inc(s["small"], 16)
            sp.dma_start(gcols[:, :], d["gcols"]).then_inc(s["small"], 16)
            sp.dma_start(pages[:, :], d["pages"]).then_inc(s["small"], 16)
            w_ada = d["w_ada"].rearrange("(k p) n -> p k n", p=128)
            with sp.Fori(0, 3) as it:
                for u in range(4):
                    sp.wait_ge(s["ada_part"], 4 * it + u + 1)
                    sp.dma_start(slot[u], w_ada[:, :, ds((4 * it + u) * 512, 512)]).then_inc(w_full[u], 16)
            sp.dma_start(xP[:, :, :], d["xT"].rearrange("(k p) t -> p k t", p=128)[:, :, 0:NP]).then_inc(s["x_in"], 16)
            sp.dma_start(xS[:, :, :], d["xT"].rearrange("(k p) t -> p k t", p=128)[:, :, NP:NT]).then_inc(s["x_in"], 16)
            sp.dma_start(wpool, d["w_pool"].rearrange("g p n -> p g n")).then_inc(s["late_in"], 16)
            sp.dma_start(wrt[:, :, :], d["w_route"].rearrange("(k p) n -> p k n", p=128)).then_inc(s["late_in"], 16)
            sp.dma_start(brt[:, :], d["b_route"]).then_inc(s["late_in"], 16)
            w_in = d["w_in"].rearrange("(k p) n -> p k n", p=128)
            for u in range(4):
                sp.wait_ge(s["ada_part"], 4 + 9 + u)
                sp.dma_start(slot[u], w_in[:, :, u * 512:(u + 1) * 512]).then_inc(w_full[u], 16)
            sp.wait_ge(s["small"], 80)
            with sp.Fori(0, NB) as b:
                def chunk_pages(c):
                    return [sp.value_load(pages[0:1, ds(PPC * NCH * b + PPC * c + g, 1)], min_val=0,
                                          max_val=d["v"].shape[0] - 1) for g in range(PPC)]
                for c in range(NCH):
                    at_ = chunk_pages(c)
                    if c == 0:
                        sp.wait_ge(s["zS"], 8)
                    sp.wait_ge(s["k_used"], NCH * b + c + 1)
                    for g, pg in enumerate(at_):
                        sp.dma_start(kslot[c % 4][:, g, :, :], d["kT"][ds(pg, 1), :, :, :].rearrange("a p j s -> (a p) j s"))\
                            .then_inc(k_full[c % 4], 16)
                for c in range(NCH):
                    at_ = chunk_pages(c)
                    if c == 0:
                        sp.wait_ge(s["zP"], 16)
                        sp.wait_ge(s["normed"], 10)
                    sp.wait_ge(s["v_used"], NCH * b + c + 1)
                    for g, pg in enumerate(at_):
                        sp.dma_start(vslot[c][:, g, :], d["v"][ds(pg, 1), :, :].rearrange("a p n -> (a p) n"))\
                            .then_inc(v_full[c], 16)
            w_out = d["w_out"].rearrange("(k p) n -> p k n", p=128)
            sp.wait_ge(s["k_used"], 4 + NB * NCH)
            for u in range(2):
                sp.dma_start(slot[u], w_out[:, :, u * 512:(u + 1) * 512]).then_inc(s[f"wo_full{u}"], 16)
            wg = d["w_gate"].rearrange("e (k p) n -> e p k n", p=128)
            wu = d["w_up"].rearrange("e (k p) n -> e p k n", p=128)
            wd = d["w_down"].rearrange("e (k p) n -> e p k n", p=128)

            def load_expert(e, p):
                for i, (w, k) in enumerate(((wg, KT), (wu, KT), (wd, FF // 128))):
                    sp.dma_start(eslot[p][i].rearrange("q (k n) -> q k n", k=k),
                                 w[ds(e, 1), :, :, :].rearrange("a q k n -> (a q) k n")).then_inc(e_full[p][i], 16)
            sp.wait_ge(s["v_used"], 8 + NB * NCH)
            load_expert(0, 0)
            sp.wait_ge(s["mixS"], 8)
            load_expert(1, 1)
            with sp.Fori(1, NE // 2 - 1) as i:
                for p in range(2):
                    sp.wait_ge(s["down"], 2 * i + p - 1)
                    load_expert(2 * i + p, p)
            sp.wait_ge(s["n_ready"], 1)
            n_pair = sp.value_load(nint[0:1, 0:1], min_val=NE // 2, max_val=MAXBLK // 2)
            with sp.Fori(0, n_pair - (NE // 2 - 1)) as i:
                for p in range(2):
                    e = sp.value_load(nint[0:1, ds(1 + 2 * i + p, 1)], min_val=0, max_val=NE - 1)
                    sp.wait_ge(s["down"], 2 * i + (NE + p - 3))
                    load_expert(e, p)
            for p in range(2):
                sp.wait_ge(y_scat[p], 16 * n_pair + 16)
            for p in range(2):
                sp.wait_ge(gathered[p], 16 * n_pair + 16)
            for t in range(TT):
                r = min(128, NT - 128 * t)
                if t >= 2:
                    sp.wait_ge(s["combined"], t - 1)
                for k in range(2):
                    a = 2 * (k * NT + 128 * t)
                    sp.dma_start(yb[t % 2][k][0:r, :], y2[a:a + 2 * r, :].rearrange("(p h) n -> p (h n)", h=2))\
                        .then_inc(s["y_back"], 16)
                sp.wait_ge(s["y_back"], 32 * (t + 1))
            sp.wait_ge(s["final"], TT * KT)
            sp.dma_start(o["yT"].rearrange("(k p) t -> p k t", p=128)[:, :, 0:NP], xP[:, :, :]).then_inc(s["stored"], 16)
            sp.dma_start(o["yT"].rearrange("(k p) t -> p k t", p=128)[:, :, NP:NT], xS[:, :, :]).then_inc(s["stored"], 16)
            sp.wait_ge(s["stored"], 11 * 16)

        @block.gpsimd
        def _(pool):
            pool.memset(ones[:, :], 1.0).then_inc(s["zeroed"], 1)
            pool.wait_ge(s["zeroed"], 1)
            pool.memset(scT[:, :, :], 0.0).then_inc(s["zeroed"], 1)
            pool.wait_ge(s["zeroed"], 2)
            pool.memset(vS[64:128, :], 0.0).then_inc(s["zeroed"], 1)
            pool.wait_ge(s["zeroed"], 3)
            pool.memset(tblS[:, :, :], 0).then_inc(s["zeroed"], 1)
            pool.wait_ge(s["zeroed"], 4)
            pool.wait_ge(s["sums"], 2)
            pool.memset(uX[:, :, 0:HIST], 0.0).then_inc(s["zeroed"], 1)
            pool.wait_ge(s["zeroed"], 5)
            then, n = chain(pool, s["pool"])
            pool.wait_ge(s["late_in"], 7 * 16)
            pool.wait_ge(s["zP_out"], 4)
            pool.wait_ge(s["zS_out"], 4)
            for g in range(4):
                src = uX[:, g, :]
                for a in range(g + 1):
                    k = 1 << a
                    dst = (win1, win2)[a % 2]
                    lo = 2 * k - 1
                    if a == 0 and g:
                        pool.wait_ge(s["pooled"], g)
                    then(pool.tensor_tensor(dst[:, lo:UW], src[:, lo:UW], src[:, lo - k:UW - k], ALU.add))
                    src = dst
            pool.wait_ge(s["normed"], 10)
            pool.wait_ge(s["turned"], 1 + NB * 8)
            pool.wait_ge(s["newT"], 1 + NB)
            pool.wait_ge(s["o_sum"], 1 + NB)
            pool.wait_ge(s["zP_out"], 16)
            with pool.Fori(0, 4) as j:
                pool.wait_ge(s["p_stored"], j + 1)
                pool.sem_inc(s["settle"], 1)
                for k, (dst, src) in enumerate(((pq, qP[:, ds(j, 1), :].rearrange("p a n -> p (a n)")),
                                                (pk, kP[:, ds(j, 1), :].rearrange("p a n -> p (a n)")),
                                                (pv, vP[:, :, ds(128 * j, 128)]), (pslope, C["slopes"][:, ds(2 * j, 2)]))):
                    pool.tensor_copy(dst, src).then_inc(s["staged"], 1)
                    pool.wait_ge(s["staged"], 4 * j + k + 1)
                    pool.sem_inc(s["settle"], 1)
            pool.wait_ge(s["n_ready"], 1)
            pool.wait_ge(s["h2_stored"], 16 * TT)
            n_pair = pool.value_load(nint[0:1, 0:1], min_val=NE // 2, max_val=MAXBLK // 2)

            def gather(p):
                pool.indirect_dma_start(Xg[p], None, h2d, bass.IndirectOffsetOnAxis(gix[p][:, :], 0)).then_inc(gathered[p], 16)
            pool.wait_ge(s["g_staged"], 2)
            for p in range(2):
                gather(p)
                pool.dma_start(first[:, 2 * p:2 * p + 2], d["consts"][p:p + 1, 0:2]).then_inc(y_scat[p], 16)
            with pool.Fori(0, n_pair) as i:
                for p in range(2):
                    pool.wait_ge(s["g_staged"], 2 * i + p + 3)
                    pool.wait_ge(s["x_turned"], 2 * i + p + 1)
                    pool.sem_inc(s["settle"], 1)
                    gather(p)
                    pool.wait_ge(s["y_out"], 2 * i + p + 3)
                    pool.wait_ge(y_scat[1 - p], 16 * i + 16 * (p + 1))
                    pool.sem_inc(s["settle"], 1)
                    pool.indirect_dma_start(y2, bass.IndirectOffsetOnAxis(six[p][:, :], 0), Yo[p], None)\
                        .then_inc(y_scat[p], 16)

        def norm_act(act, sq_s, sum_s, root_s, scaled_s, ready_s, shift):
            for k in range(KT):
                act.activation(sq[:, k, 0:NP], xP[:, k, :], ACT.Square)
                act.activation(sq[:, k, NP:NT], xS[:, k, :], ACT.Square).then_inc(sq_s, 1)
            act.wait_ge(sum_s, 2)
            act.activation(rstd[:, 0:NP], B[4][:, :], ACT.Sqrt, scale=1.0 / D, bias=C["eps"])
            act.activation(rstd[:, NP:NT], B[5][:, 0:NS], ACT.Sqrt, scale=1.0 / D, bias=C["eps"]).then_inc(root_s, 1)
            for k in range(KT):
                act.wait_ge(scaled_s, 2 * k + 2)
                act.activation(hP[:, k, :], hP[:, k, :], ACT.Identity, bias=modT[:, shift * KT + k, 0:1])\
                    .then_inc(ready_s, 1)

        def norm_pe(pe, sq_s, sum_s):
            for k in range(KT):
                pe.wait_ge(sq_s, k + 1)
                p_ = pe.matmul(B[4][:, :], ones[:, :], sq[:, k, 0:NP], start=k == 0, stop=k == KT - 1)
                s_ = pe.matmul(B[5][:, 0:NS], ones[:, :], sq[:, k, NP:NT], start=k == 0, stop=k == KT - 1)
            p_.then_inc(sum_s, 1)
            s_.then_inc(sum_s, 1)

        def norm_dve(dve, then, root_s, scaled_s, ready_s, gain, g, scale, shift):
            then(dve.scalar_tensor_tensor(coef[:, :, :], modT[:, scale * KT:(scale + 1) * KT, :], 1.0,
                                          g.unsqueeze(2).to_broadcast([128, KT, NSEQ]), ALU.add, ALU.mult))
            dve.wait_ge(root_s, 1)
            then(dve.reciprocal(rstd[:, :], rstd[:, :]))
            for k in range(KT):
                dve.scalar_tensor_tensor(hP[:, k, :], xP[:, k, :], coef[:, k, 0:1], rstd[:, 0:NP],
                                         ALU.mult, ALU.mult).then_inc(scaled_s, 1)
                then(dve.tensor_tensor(hS[:, k, :].rearrange("p (b q) -> p b q", b=NB),
                                       xS[:, k, :].rearrange("p (b q) -> p b q", b=NB),
                                       coef[:, k, 1:NSEQ].unsqueeze(2).to_broadcast([128, NB, NQ]), ALU.mult))
                then(dve.tensor_tensor(hS[:, k, :], hS[:, k, :], rstd[:, NP:NT], ALU.mult))
                dve.tensor_tensor(hS[:, k, :].rearrange("p (b q) -> p b q", b=NB),
                                  hS[:, k, :].rearrange("p (b q) -> p b q", b=NB),
                                  modT[:, shift * KT + k, 1:NSEQ].unsqueeze(2).to_broadcast([128, NB, NQ]),
                                  ALU.add).then_inc(scaled_s, 1)

        uxs = uX[:, :, HIST + NP:UW].rearrange("p g (b t) -> p g b t", b=NB)
        pieces = [(qS[:, :, :].rearrange("p j t -> p (j t)"), 0), (kS[:, :, :].rearrange("p j t -> p (j t)"), 1)]
        pieces += [(qP[:, m, :], 0) for m in range(4)] + [(kP[:, m, :], 1) for m in range(4)]
        hsq = [ring[:, 5 * U + 512 * (i + 1):5 * U + 512 * (i + 2)] for i in range(2)]
        hrt = [ring[:, 5 * U + 512 * (i + 3):5 * U + 512 * (i + 4)] for i in range(2)]
        steps = [(h, i) for i in range(4) for h in range(2)]

        @block.scalar
        def _(act):
            act.wait_ge(s["small"], 80)
            act.wait_ge(s["zeroed"], 4)
            act.activation(scT[:, :, 0:NSEQ], cT, ACT.Silu).then_inc(s["silu"], 1)
            with act.Fori(0, 12) as u:
                act.wait_ge(s["ada_part"], u + 5)
                act.activation(part[:, :], B[0][:, :], ACT.Copy).then_inc(s["ada_copied"], 1)
            act.wait_ge(s["x_in"], 32)
            norm_act(act, s["squared"], s["sums"], s["rooted"], s["h_scaled"], s["h_ready"], 0)
            for g in range(4):
                act.dma_start(uxs[:, g, :, 0:HIST], d["histT"][g * 128:(g + 1) * 128, :, :]).then_inc(s["late_in"], 16)
            for T in range(16):
                act.wait_ge(s["zP"], T + 1)
                n, m = divmod(T, 4)
                dst = (uX[:, m, HIST:HIST + NP], qP[:, m, :], kP[:, m, :], vP[:, m, :])[n]
                act.activation(dst, B[T % 2][:, :], ACT.Copy).then_inc(s["zP_out"], 1)
            for g in range(4):
                act.wait_ge(s["ypool"], g + 1)
                act.activation(mP[:, g, :], B[6][:, :], ACT.Copy, scale=pscale[:, g:g + 1])
                act.activation(mS[:, g, :], B[7][:, 0:NS], ACT.Copy, scale=pscale[:, g:g + 1]).then_inc(s["ypool_out"], 1)
            act.wait_ge(s["zS_out"], 13)
            act.wait_ge(s["zP_out"], 16)
            for i, (x, _) in enumerate(pieces):
                w = x.shape[1]
                if i >= 2:
                    act.wait_ge(s["hsum"], i - 1)
                act.activation(hsq[i % 2][:, 0:w], x, ACT.Square).then_inc(s["hsq"], 1)
                act.wait_ge(s["hsum"], i + 1)
                if i >= 2:
                    act.wait_ge(s["normed"], i - 1)
                act.activation(hrt[i % 2][:, 0:w], B[4 + i % 2][:, 0:w], ACT.Sqrt, scale=1.0 / HD, bias=C["eps"])\
                    .then_inc(s["hroot"], 1)
            act.wait_ge(s["normed"], 10)
            act.dma_start(o["kT"].rearrange("(j p) t -> p j t", p=128)[:, :, 0:NP], kP[:, :, :]).then_inc(s["stored"], 16)
            act.dma_start(o["kT"].rearrange("(j p) t -> p j t", p=128)[:, :, NP:NT], kS[:, :, :]).then_inc(s["stored"], 16)
            act.wait_ge(s["zP_out"], 16)
            act.wait_ge(s["zS_out"], 13)
            act.dma_start(o["v"][0:NP, :].rearrange("(r p) n -> p r n", p=128), vP[:, :, :]).then_inc(s["stored"], 16)
            act.dma_start(o["v"][NP:NT, :], vS[0:NS, :]).then_inc(s["stored"], 16)
            act.dma_start(o["poolT"].rearrange("(g p) b t -> p g b t", p=128)[:, :, 0, :],
                         uX[:, :, NP:NP + HIST]).then_inc(s["stored"], 16)
            for g in range(4):
                act.dma_start(o["poolT"][g * 128:(g + 1) * 128, 1:NSEQ, :], uxs[:, g, :, NQ:US]).then_inc(s["stored"], 16)
            with act.Fori(0, NB) as b:
                act.wait_ge(s["exp_bias"], b + 1)
                for n in range(NBLK):
                    act.activation(L[:, BLK * n:BLK * (n + 1)], L[:, BLK * n:BLK * (n + 1)], ACT.Exp,
                                   bias=ebias[:, n:n + 1], accum_out=esum[:, n:n + 1]).then_inc(s["probs"], 1)
                act.activation(L[:, PAST:PAST + NS], L[:, PAST:PAST + NS], ACT.Exp, bias=negm,
                               accum_out=esum[:, NBLK:NBLK + 1]).then_inc(s["probs"], 1)
                act.wait_ge(s["o_sum"], b + 1)
                for g in range(8):
                    act.wait_ge(s["turned"], 8 * b + g + 2)
                    act.activation(PT[:, 4 * g:4 * g + 4, :].rearrange("p t (j c) -> p (t j) c", j=4),
                                   B[3 + g % 2][:, :].rearrange("p (x c) -> p x c", c=32)[:, :, 0:16],
                                   ACT.Copy).then_inc(s["turned_out"], 1)
                act.wait_ge(s["newT"], b + 2)
                act.activation(PT[:, 32, :].rearrange("p (j c) -> p j c", j=4),
                               B[2][:, 128:256].rearrange("p (x c) -> p x c", c=32)[:, :, 0:16],
                               ACT.Copy).then_inc(s["newT_out"], 1)
                act.wait_ge(s["o_sum"], b + 2)
                act.wait_ge(s["rinv_ready"], b + 1)
                act.activation(On, B[5][:, 0:128], ACT.Copy, scale=rinv).then_inc(s["o_scaled"], 1)
                act.wait_ge(s["oT"], b + 1)
                act.sem_inc(s["settle"], 1)
                oT = B[6][:, 0:128].rearrange("p (j c) -> p j c", j=4)
                for h in range(2):
                    act.activation(mS[64 * h:64 * h + 64, 4:8, ds(NQ * b, NQ)],
                                   oT[64 * h:64 * h + 64, :, NQ * h:NQ * h + NQ], ACT.Copy).then_inc(s["oT_out"], 1)
            with act.Fori(0, 4) as j:
                def p_evac(e):
                    h, i = steps[e]
                    act.wait_ge(s["p_turned"], 8 * j + e + 1)
                    act.activation(pPT[h][:, 0:i + 1, 128 * i:128 * i + 128],
                                   B[2 + e % 2][:, 0:128 * (i + 1)].rearrange("p (t q) -> p t q", q=128), ACT.Copy)\
                        .then_inc(s["p_turned_out"], 1)
                for e, (h, i) in enumerate(steps):
                    act.wait_ge(s["p_neg"], 8 * j + e + 1)
                    act.activation(plog[h][:, 0:128 * (i + 1)], plog[h][:, 0:128 * (i + 1)], ACT.Exp,
                                   bias=pst[:, h:h + 1], accum_out=pst[:, 2 + h:3 + h]).then_inc(s["p_exp"], 1)
                    if e:
                        p_evac(e - 1)
                p_evac(7)
            act.wait_ge(s["res1"], 2 * KT)
            norm_act(act, s["squared2"], s["sums2"], s["rooted2"], s["h_scaled2"], s["h2_ready"], 3)
            for t in range(2 * TT):
                r = min(128, NT - 128 * (t // 2))
                act.wait_ge(s["h2_turn"], t + 1)
                act.activation(h2tok[0:r, t // 2, 512 * (t % 2):512 * (t % 2) + 512], B[t % 2][0:r, :], ACT.Copy)\
                    .then_inc(s["h2_out"], 1)
            for t in range(TT):
                r = min(128, NT - 128 * t)
                act.wait_ge(s["h2_out"], 2 * t + 2)
                act.dma_start(h2d[256 * t:256 * t + 2 * r, :].rearrange("(p h) n -> p (h n)", h=2),
                              h2tok[0:r, t, :]).then_inc(s["h2_stored"], 16)
            act.wait_ge(s["g_exp_in"], 1)
            act.activation(gexp, gexp, ACT.Exp).then_inc(s["g_exp"], 1)
            act.wait_ge(s["g_exp_in"], 2)
            act.activation(eex, edif, ACT.Exp).then_inc(s["g_exp"], 1)
            act.wait_ge(s["n_ready"], 1)
            n_pair = act.value_load(nint[0:1, 0:1], min_val=NE // 2, max_val=MAXBLK // 2)
            with act.Fori(0, n_pair) as i:
                for p in range(2):
                    act.wait_ge(s["x_turned"], 2 * i + p + 1)
                    act.activation(XT[p], B[0][:, :], ACT.Copy).then_inc(s["xT_ready"], 1)
                    act.wait_ge(s["gate_up"], 2 * i + p + 1)
                    act.activation(gs[p], B[1][:, 0:256], ACT.Silu).then_inc(s["silu_ready"], 1)
                    act.wait_ge(s["a_turned"], 2 * i + p + 1)
                    act.activation(aT[p], B[3][:, 0:256], ACT.Copy).then_inc(s["aT_ready"], 1)

        @block.vector
        def _(dve):
            then, n = chain(dve, s["dve"])
            dve.wait_ge(s["small"], 80)
            with dve.Fori(0, 12) as u:
                dve.wait_ge(s["ada_cols"], u + 1)
                dve.tensor_tensor(modT[:, ds(4 * u, 4), :], B[1][:, 0:4 * NSEQ].rearrange("p (c s) -> p c s", s=NSEQ),
                                  bT[:, ds(4 * u, 4), :], ALU.add).then_inc(s["ada_done"], 1)
            dve.wait_ge(s["ada_done"], 12)
            norm_dve(dve, then, s["rooted"], s["h_scaled"], s["h_ready"], None, g1, 1, 0)
            dve.wait_ge(s["late_in"], 7 * 16)
            for T in range(13):
                dve.wait_ge(s["zS"], T + 1)
                n_, m = divmod(T, 4)
                src = B[2 + T % 2][:, 0:NS]
                if n_ == 0:
                    ins = dve.tensor_copy(uxs[:, m, :, HIST:US], src.rearrange("p (b q) -> p b q", b=NB))
                elif n_ < 3:
                    ins = dve.tensor_copy((qS, kS)[n_ - 1][:, m, :], src)
                else:
                    ins = dve.tensor_copy(vS[0:NS, :], B[2 + T % 2][0:NS, :])
                ins.then_inc(s["zS_out"], 1)
            dve.wait_ge(s["zP"], 16)
            for g in range(4):
                w = 2 << g
                src = (win1, win2)[g % 2]
                dve.wait_ge(s["pool"], sum(range(1, g + 2)))
                dve.scalar_tensor_tensor(pooledP[:, g, :], src[:, HIST:HIST + NP], 1.0 / w, uX[:, g, HIST:HIST + NP],
                                         ALU.mult, ALU.subtract)
                then(dve.tensor_tensor(part[:, 0:16], src[:, HIST:HIST + 16], C["share"][:, 16 * g:16 * g + 16], ALU.mult))
                then(dve.tensor_tensor(pooledP[:, g, 0:16], part[:, 0:16], uX[:, g, HIST:HIST + 16], ALU.subtract))
                sw = src[:, HIST + NP:UW].rearrange("p (b t) -> p b t", b=NB)
                dve.scalar_tensor_tensor(pooledS[:, g, :].rearrange("p (b q) -> p b q", b=NB), sw[:, :, HIST:US], 1.0 / w,
                                         uxs[:, g, :, HIST:US], ALU.mult, ALU.subtract).then_inc(s["pooled"], 1)
            then(dve.tensor_scalar(gq, gq, HD ** -0.5, None, ALU.mult))
            for i, (x, which) in enumerate(pieces):
                w = x.shape[1]
                r = hrt[i % 2][:, 0:w]
                dve.wait_ge(s["hroot"], i + 1)
                then(dve.reciprocal(r, r))
                dve.scalar_tensor_tensor(x, x, (gq, gk)[which], r, ALU.mult, ALU.mult).then_inc(s["normed"], 1)
            dve.wait_ge(s["normed"], 10)
            dve.wait_ge(s["ypool"], 4)
            then(dve.memset(qbd[:, :, :, :], 0.0))
            for h in range(2):
                for j in range(4):
                    ins = dve.tensor_copy(qbd[64 * h:64 * h + 64, :, j, NQ * h:NQ * h + NQ],
                                          qS[64 * h:64 * h + 64, j, :].rearrange("p (b q) -> p b q", b=NB))
                    then(ins)
            dve.wait_ge(s["stored"], 9 * 16)
            then(dve.memset(L[:, PAST:PAST + 128], 0.0))
            jb = C["jbias"].unsqueeze(1).to_broadcast([128, CH // BLK, BLK])
            PER = 12
            nb = C["newbias"].rearrange("p (b t) -> p b t", b=NB)
            with dve.Fori(0, NB) as b:
                then2, n2 = chain(dve, s["dve2"], PER * b)
                dve.wait_ge(s["k_used"], NCH * b + 4)
                dve.tensor_scalar(qst[:, :, :], qbd[:, ds(b, 1), :, :].rearrange("p a j c -> p (a j) c"), 1.0, None, ALU.mult)\
                    .then_inc(s["q_staged"], 1)
                dve.wait_ge(s["new_scored"], b + 1)
                dve.wait_ge(s["newT"], b + 1)
                dve.wait_ge(s["turned"], 8 * b + 1)
                dve.tensor_tensor(L[:, PAST:PAST + NS], B[2][:, 0:NS], nb[:, ds(b, 1), :].rearrange("p a t -> p (a t)"),
                                  ALU.add).then_inc(s["new_out"], 1)
                dve.wait_ge(s["new_out"], b + 1)
                dve.tensor_reduce(nmax, L[:, PAST:PAST + NS], AX.X, ALU.max)
                for c in range(NCH):
                    dve.wait_ge(s["k_used"], NCH * b + c + 5)
                    sc = B[c % 2][:, :].rearrange("p (n k) -> p n k", n=2)
                    dve.tensor_reduce(gsum[:, 2 * c:2 * c + 2], sc, AX.X, ALU.add)
                    dve.tensor_tensor(L[:, CH * c:CH * (c + 1)].rearrange("p (n k) -> p n k", n=2), sc, jb, ALU.add)\
                        .then_inc(s["s_out"], 1)
                    dve.wait_ge(s["s_out"], NCH * b + c + 3)
                    ins = dve.tensor_reduce(bmax[:, 2 * c:2 * c + 2], L[:, CH * c:CH * (c + 1)].rearrange("p (n k) -> p n k", n=2),
                                            AX.X, ALU.max)
                then2(ins)
                dve.sem_inc(s["settle"], 1)
                then2(dve.max(top8[:, :], gsum[:, :]))
                dve.sem_inc(s["settle"], 1)
                then2(dve.max_index(topi[:, :], top8[:, :], gsum[:, :]))
                then2(dve.tensor_scalar(topf[:, :], topi[:, :], 1.0, None, ALU.mult))
                io = C["iota"][:, 0:NBLK]
                then2(dve.tensor_scalar(pen[:, :], io, topf[:, 0:1], None, ALU.is_equal))
                then2(dve.scalar_tensor_tensor(pen[:, :], io, topf[:, 1:2], pen[:, :], ALU.is_equal, ALU.add))
                then2(dve.scalar_tensor_tensor(pen[:, :], io, topf[:, 2:3], pen[:, :], ALU.is_equal, ALU.add))
                then2(dve.tensor_scalar(pen[:, :], pen[:, :], -1.0, -OFF, ALU.add, ALU.mult))
                then2(dve.tensor_tensor(pen[:, :], pen[:, :], C["blockoff"], ALU.add))
                then2(dve.tensor_tensor(bmax[:, :], bmax[:, :], pen[:, :], ALU.add))
                then2(dve.tensor_reduce(gmax_, bmax[:, :], AX.X, ALU.max))
                then2(dve.tensor_scalar(negm, gmax_, nmax, -1.0, ALU.max, ALU.mult))
                assert n2[0] == PER
                dve.tensor_scalar(ebias[:, :], pen[:, :], negm, None, ALU.add).then_inc(s["exp_bias"], 1)
                dve.wait_ge(s["probs"], 17 * b + 17)
                dve.tensor_reduce(tot, esum[:, :], AX.X, ALU.add).then_inc(s["dve3"], 1)
                dve.wait_ge(s["dve3"], b + 1)
                dve.wait_ge(s["o_scaled"], b + 1)
                dve.reciprocal(rinv, tot).then_inc(s["rinv_ready"], 1)
            with dve.Fori(0, 4) as j:
                dve.wait_ge(s["staged"], 4 * j + 4)

                def p_scale(e):
                    h, i = steps[e]
                    dve.wait_ge(s["p_exp"], 8 * j + e + 1)
                    dve.reciprocal(pst[:, 4 + h:5 + h], pst[:, 2 + h:3 + h]).then_inc(s["p_out"], 1)
                    dve.wait_ge(s["p_out"], 8 * j + e + 1)
                    dve.tensor_scalar(plog[h][:, 0:128 * (i + 1)], plog[h][:, 0:128 * (i + 1)], pst[:, 4 + h:5 + h], None,
                                      ALU.mult).then_inc(s["p_prob"], 1)
                for e, (h, i) in enumerate(steps):
                    w = 128 * (i + 1)
                    dve.wait_ge(s["p_scores"], 8 * j + e + 1)
                    if e > 1:
                        dve.wait_ge(s["p_turned"], 8 * j + e - 1)
                    dve.scalar_tensor_tensor(plog[h][:, 0:w], C["causal"][:, NP - w:NP], pslope[:, h:h + 1], B[e % 2][:, 0:w],
                                             ALU.mult, ALU.add).then_inc(s["p_logits"], 1)
                    dve.wait_ge(s["p_logits"], 8 * j + e + 3)
                    dve.tensor_reduce(pst[:, h:h + 1], plog[h][:, 0:w], AX.X, ALU.max, negate=True).then_inc(s["p_neg"], 1)
                    if e:
                        p_scale(e - 1)
                p_scale(7)
                dve.wait_ge(s["mixP"], j + 1)
                dve.tensor_scalar(mP[:, ds(4 + j, 1), :].rearrange("p a t -> p (a t)"), B[4][:, :], 1.0, None, ALU.mult)\
                    .then_inc(s["p_stored"], 1)
            for m in range(KT):
                dve.wait_ge(s["mixP"], 4 + m + 1)
                dve.scalar_tensor_tensor(xP[:, m, :], B[m % 2][:, :], modT[:, 2 * KT + m, 0:1], xP[:, m, :], ALU.mult, ALU.add)\
                    .then_inc(s["res1"], 1)
                dve.wait_ge(s["mixS"], m + 1)
                if m:
                    dve.wait_ge(s["res1"], 2 * m)
                then(dve.tensor_tensor(part[:, 0:NS].rearrange("p (b q) -> p b q", b=NB),
                                       B[2 + m % 2][:, 0:NS].rearrange("p (b q) -> p b q", b=NB),
                                       modT[:, 2 * KT + m, 1:NSEQ].unsqueeze(2).to_broadcast([128, NB, NQ]), ALU.mult))
                dve.tensor_tensor(xS[:, m, :], xS[:, m, :], part[:, 0:NS], ALU.add).then_inc(s["res1"], 1)
            dve.memset(B[6][:, :], 0.0).then_inc(s["bank_cleared"], 1)
            norm_dve(dve, then, s["rooted2"], s["h_scaled2"], s["h2_ready"], None, g2, 4, 3)

            dve.wait_ge(s["stored"], 9 * 16)
            then(dve.memset(lg8, OFF))
            dve.wait_ge(s["route_scores"], 1)
            then(dve.tensor_tensor(lg, B[6][:, 0:TT * 36].rearrange("p (t n) -> p t n", t=TT),
                                   brt[:, :].unsqueeze(1).to_broadcast([128, TT, 36]), ALU.add))
            then(dve.tensor_copy(lg8[:, :, 0:4], lg[:, :, 0:4]))
            for t in range(TT):
                then(dve.max(gtop[:, t, :], lg8[:, t, :]))
                then(dve.max_index(gidx[:, t, :], gtop[:, t, :], lg8[:, t, :]))
            then(dve.tensor_copy(gif, gidx[:, :, 0]))
            dve.tensor_tensor(gexp, lg[:, :, 0:4], gtop[:, :, 0:1].to_broadcast([128, TT, 4]), ALU.subtract)\
                .then_inc(s["g_exp_in"], 1)
            then(dve.tensor_tensor(goh, C["iota"][:, 0:4].unsqueeze(1).to_broadcast([128, TT, 4]),
                                   gif.unsqueeze(2).to_broadcast([128, TT, 4]), ALU.is_equal))
            g4 = gtmp.rearrange("p (t g e) -> p t g e", t=TT, g=4)
            then(dve.tensor_tensor(g4, lg[:, :, 4:36].rearrange("p t (g e) -> p t g e", g=4),
                                   goh.unsqueeze(3).to_broadcast([128, TT, 4, 8]), ALU.mult))
            then(dve.tensor_reduce(ein, g4.rearrange("p t g e -> p t e g"), AX.X, ALU.add))
            for t in range(TT):
                then(dve.max(etop[:, t, :], ein[:, t, :]))
                then(dve.max_index(eidx[:, t, :], etop[:, t, :], ein[:, t, :]))
            dve.tensor_tensor(edif, etop[:, :, 1], etop[:, :, 0], ALU.subtract).then_inc(s["g_exp_in"], 1)
            ek2 = ek.rearrange("p (t k) -> p t k", k=2)
            then(dve.tensor_copy(ek2, eidx[:, :, 0:2]))
            then(dve.scalar_tensor_tensor(ek2, gif.unsqueeze(2).to_broadcast([128, TT, 2]), 8.0, ek2, ALU.mult, ALU.add))
            hotv = hot.rearrange("p (x e) -> p x e", e=32)
            then(dve.tensor_tensor(hotv, C["iota"][:, 0:NE].unsqueeze(1).to_broadcast([128, 2 * TT, 32]),
                                   ek.unsqueeze(2).to_broadcast([128, 2 * TT, 32]), ALU.is_equal))
            h4 = hot.rearrange("p (t k e) -> p t k e", t=TT, k=2)
            then(dve.tensor_tensor(hotm, h4[:, :, 0, :], h4[:, :, 1, :], ALU.add))
            then(dve.tensor_tensor(hotm, hotm, C["valid"].unsqueeze(2).to_broadcast([128, TT, 32]), ALU.mult))
            dve.sem_inc(s["hot"], 1)
            dve.wait_ge(s["g_exp"], 1)
            then(dve.tensor_reduce(gw, gexp, AX.X, ALU.add))
            dve.wait_ge(s["g_exp"], 2)
            then(dve.scalar_tensor_tensor(eden, eex, 1.0, gw, ALU.add, ALU.mult))
            then(dve.reciprocal(wts[:, 0, :], eden))
            then(dve.tensor_tensor(wts[:, 1, :], wts[:, 0, :], eex, ALU.mult))
            dve.wait_ge(s["ranked"], 1)
            then(dve.tensor_copy(cum, B[7][:, 0:(TT + 1) * 32].rearrange("p (t e) -> p t e", t=TT + 1)))
            NTH = 9
            ovv = ovt[:, 0:32 * NTH].rearrange("p (e i) -> p e i", i=NTH)
            then(dve.tensor_tensor(ovv, cum[:, TT, :].unsqueeze(2).to_broadcast([128, 32, NTH]),
                                   C["thr"][:, 0:NTH].unsqueeze(1).to_broadcast([128, 32, NTH]), ALU.is_gt))
            then(dve.tensor_reduce(over, ovv, AX.X, ALU.add))
            then(dve.tensor_tensor_scan(incl, ones[:, 0:32], over, 0.0, ALU.mult, ALU.add))
            then(dve.tensor_tensor(base2, incl, over, ALU.subtract))
            then(dve.tensor_scalar(base2, base2, float(NE - 1), None, ALU.add))
            pr = prod.rearrange("p (t k e) -> p t k e", t=TT, k=2)
            then(dve.tensor_tensor(pr, h4, cum[:, 0:TT, :].unsqueeze(2).to_broadcast([128, TT, 2, 32]), ALU.mult))
            prv = prod.rearrange("p (x e) -> p x e", e=32)
            then(dve.tensor_reduce(pos, prv, AX.X, ALU.add))
            then(dve.tensor_tensor(prv, hotv, base2.unsqueeze(1).to_broadcast([128, 2 * TT, 32]), ALU.mult))
            then(dve.tensor_reduce(ost, prv, AX.X, ALU.add))
            pv8 = past.rearrange("p (x i) -> p x i", i=8)
            then(dve.tensor_tensor(pv8, pos.unsqueeze(2).to_broadcast([128, 2 * TT, 8]),
                                   C["thr"][:, 0:8].unsqueeze(1).to_broadcast([128, 2 * TT, 8]), ALU.is_ge))
            then(dve.tensor_reduce(bno, pv8, AX.X, ALU.add))
            then(dve.scalar_tensor_tensor(pos, bno, -float(RB), pos, ALU.mult, ALU.add))
            then(dve.tensor_scalar(far, bno, 1.0, None, ALU.is_ge))
            then(dve.tensor_tensor(ost, ost, bno, ALU.add))
            then(dve.tensor_tensor(ost, ost, ek, ALU.subtract))
            then(dve.tensor_tensor(ost, ost, far, ALU.mult))
            then(dve.tensor_tensor(blk_, ost, ek, ALU.add))
            nv = ovt[0:1, 0:NOV * 32].rearrange("p (o e) -> p o e", e=32)
            then(dve.tensor_tensor(nv, C["ovid"][0:1, :].unsqueeze(2).to_broadcast([1, NOV, 32]),
                                   incl[0:1, :].unsqueeze(1).to_broadcast([1, NOV, 32]), ALU.is_ge))
            then(dve.tensor_reduce(oveif[0:1, :], nv, AX.X, ALU.add))
            then(dve.tensor_scalar(oveif[0:1, :], oveif[0:1, :], float(NE - 1), None, ALU.min))
            then(dve.tensor_scalar(ovt[0:1, 0:NOV // 2], C["two"][0:1, 0:NOV // 2], incl[0:1, 31:32], None, ALU.is_lt))
            then(dve.tensor_reduce(npf[0:1, 1:2], ovt[0:1, 0:NOV // 2], AX.X, ALU.add))
            then(dve.tensor_scalar(nint[0:1, 0:1], npf[0:1, 1:2], float(NE // 2), None, ALU.add))
            then(dve.tensor_copy(nint[0:1, 1:3], C["iota"][0:1, NE - 2:NE]))
            then(dve.tensor_copy(nint[0:1, 3:3 + NOV], oveif[0:1, :]))
            then(dve.tensor_tensor(rows, C["iota"].unsqueeze(1).unsqueeze(1).to_broadcast([128, 2 * TT, 2, RB]),
                                   pos.unsqueeze(2).unsqueeze(2).to_broadcast([128, 2 * TT, 2, RB]), ALU.is_equal))
            then(dve.tensor_tensor(blks[:, :, 0, :], C["iota"][:, 0:MAXBLK].unsqueeze(1).to_broadcast([128, 2 * TT, MAXBLK]),
                                   blk_.unsqueeze(2).to_broadcast([128, 2 * TT, MAXBLK]), ALU.is_equal))
            b0 = blks[:, :, 0, :].rearrange("p (t k) b -> p t k b", k=2)
            then(dve.tensor_tensor(b0, b0, C["valid"].unsqueeze(2).unsqueeze(3).to_broadcast([128, TT, 2, MAXBLK]), ALU.mult))
            pay = C["payload"].rearrange("p (x c) -> p x c", c=2)
            for c in range(2):
                ins = dve.tensor_tensor(blks[:, :, 1 + c, :], blks[:, :, 0, :],
                                        pay[:, :, c:c + 1].to_broadcast([128, 2 * TT, MAXBLK]), ALU.mult)
                ins.then_inc(s["listed"], 1)
            dve.wait_ge(s["lists_summed"], 1)
            dve.wait_ge(s["zeroed"], 4)
            ls = B[5][:, 0:3 * MAXBLK].rearrange("p (c b) -> p c b", c=3)
            free = ovt[:, 0:MAXBLK]
            then(dve.tensor_scalar(free, ls[:, 0, :], -1.0, 1.0, ALU.mult, ALU.add))
            then(dve.scalar_tensor_tensor(free, free, C["dump"], ls[:, 2, :], ALU.mult, ALU.add))
            then(dve.tensor_scalar(tblS[:, 0, 0:MAXBLK], ls[:, 1, :], C["half"], None, ALU.add))
            then(dve.tensor_scalar(tblS[:, 1, 0:MAXBLK], free, C["half"], None, ALU.add))
            dve.sem_inc(s["n_ready"], 1)

            n_pair = dve.value_load(nint[0:1, 0:1], min_val=NE // 2, max_val=MAXBLK // 2)
            for p in range(2):
                dve.tensor_copy(gix[p][:, :], tblS[:, 0, p:p + 1]).then_inc(s["g_staged"], 1)
            with dve.Fori(0, n_pair) as i:
                for p in range(2):
                    dve.wait_ge(gathered[p], 16 * i + 16)
                    dve.tensor_scalar(gix[p][:, :], tblS[:, 0, ds(2 * i + (2 + p), 1)], 0, None, ALU.add).then_inc(s["g_staged"], 1)
                    dve.wait_ge(y_scat[p], 16 * i + 16)
                    dve.tensor_scalar(six[p][:, :], tblS[:, 1, ds(2 * i + p, 1)], 0, None, ALU.add).then_inc(s["s_staged"], 1)
                    dve.wait_ge(s["silu_ready"], 2 * i + p + 1)
                    dve.tensor_tensor(aa[p], gs[p], B[2][:, 0:256], ALU.mult).then_inc(s["act_ready"], 1)
                    dve.wait_ge(s["down"], 2 * i + p + 1)
                    dve.tensor_copy(Yo[p], B[4 + p][:, :]).then_inc(s["y_out"], 1)
            for t in range(TT):
                r = min(128, NT - 128 * t)
                dve.wait_ge(s["y_back"], 32 * (t + 1))
                if t >= 2:
                    dve.wait_ge(s["c_turned"], 2 * t - 2)
                then(dve.tensor_scalar(yc[t % 2][0:r, :], yb[t % 2][0][0:r, :], wts[0:r, 0, t:t + 1], None, ALU.mult))
                dve.scalar_tensor_tensor(yc[t % 2][0:r, :], yb[t % 2][1][0:r, :], wts[0:r, 1, t:t + 1], yc[t % 2][0:r, :],
                                         ALU.mult, ALU.add).then_inc(s["combined"], 1)
                for k in range(KT):
                    if k % 4 == 0:
                        dve.wait_ge(s["c_turned"], 2 * t + k // 4 + 1)
                    src = B[k // 4][:, (k % 4) * 128:(k % 4) * 128 + r]
                    if t < TT - 1:
                        x = xP[:, k, 128 * t:128 * t + 128]
                        dve.scalar_tensor_tensor(x, src, modT[:, 5 * KT + k, 0:1], x, ALU.mult, ALU.add)\
                            .then_inc(s["final"], 1)
                    else:
                        then(dve.tensor_tensor(part[:, 0:NS].rearrange("p (b q) -> p b q", b=NB),
                                               src.rearrange("p (b q) -> p b q", b=NB),
                                               modT[:, 5 * KT + k, 1:NSEQ].unsqueeze(2).to_broadcast([128, NB, NQ]), ALU.mult))
                        dve.tensor_tensor(xS[:, k, :], xS[:, k, :], part[:, 0:NS], ALU.add).then_inc(s["final"], 1)
                        dve.wait_ge(s["final"], t * KT + k + 1)

        @block.tensor
        def _(pe):
            pe.sem_inc(s["ada_part"], 4)
            pe.sem_inc(s["s_out"], 2)
            pe.sem_inc(s["turned_out"], 2)
            pe.sem_inc(s["o_scaled"], 1)
            pe.sem_inc(s["oT_out"], 1)
            pe.sem_inc(s["p_logits"], 2)
            pe.sem_inc(s["p_turned_out"], 2)
            pe.sem_inc(s["y_out"], 2)
            pe.sem_inc(s["turned"], 1)
            pe.sem_inc(s["newT"], 1)
            pe.sem_inc(s["o_sum"], 1)
            pe.sem_inc(s["p_stored"], 1)
            pe.wait_ge(s["zeroed"], 4)
            pe.wait_ge(s["silu"], 1)
            with pe.Fori(0, 3) as it:
                for u in range(4):
                    pe.wait_ge(w_full[u], 16 * it + 16)
                    for k in range(KT):
                        j = k % 4
                        last = pe.matmul(B[0][32 * j:32 * j + 32, :], scT[:, k, :], slot[u][:, k, :], start=k < 4, stop=k >= 4)
                    last.then_inc(s["ada_part"], 1)
                    pe.wait_ge(s["ada_copied"], 4 * it + u + 1)
                    for c in range(4):
                        last = pe.matmul(B[1][:, NSEQ * c:NSEQ * (c + 1)], part[:, 128 * c:128 * c + 128], C["sel"],
                                         start=True, stop=True)
                    last.then_inc(s["ada_cols"], 1)
                    pe.wait_ge(s["ada_done"], 4 * it + u + 1)
            norm_pe(pe, s["squared"], s["sums"])
            pe.wait_ge(s["h_ready"], KT)
            pe.wait_ge(s["h_scaled"], 2 * KT)
            for T in range(16):
                n, m = divmod(T, 4)
                if m == 0:
                    pe.wait_ge(w_full[n], 16 * 4)
                if T >= 2:
                    pe.wait_ge(s["zP_out"], T - 1)
                    pe.wait_ge(s["zS_out"], min(T - 1, 12))
                sample = n < 3 or m == 0
                for k in range(KT):
                    w = slot[n][:, k, 128 * m:128 * m + 128]
                    if n < 3:
                        a = pe.matmul(B[T % 2][:, :], w, hP[:, k, :], start=k == 0, stop=k == KT - 1)
                        b_ = pe.matmul(B[2 + T % 2][:, 0:NS], w, hS[:, k, :], start=k == 0, stop=k == KT - 1)
                    else:
                        a = pe.matmul(B[T % 2][:, :], hP[:, k, 128 * m:128 * m + 128], slot[n][:, k, :],
                                      start=k == 0, stop=k == KT - 1)
                        if m == 0:
                            b_ = pe.matmul(B[2 + T % 2][0:NS, :], hS[:, k, :], slot[n][:, k, :], start=k == 0, stop=k == KT - 1)
                a.then_inc(s["zP"], 1)
                if sample:
                    b_.then_inc(s["zS"], 1)
            for g in range(4):
                pe.wait_ge(s["pooled"], g + 1)
                if g:
                    pe.wait_ge(s["ypool_out"], g)
                pe.matmul(B[6][:, :], wpool[:, g, :], pooledP[:, g, :], start=True, stop=True)
                pe.matmul(B[7][:, 0:NS], wpool[:, g, :], pooledS[:, g, :], start=True, stop=True).then_inc(s["ypool"], 1)
            for i, (x, _) in enumerate(pieces):
                w = x.shape[1]
                pe.wait_ge(s["hsq"], i + 1)
                if i >= 2:
                    pe.wait_ge(s["hroot"], i - 1)
                pe.matmul(B[4 + i % 2][:, 0:w], C["heads"], hsq[i % 2][:, 0:w], start=True, stop=True).then_inc(s["hsum"], 1)
            pe.wait_ge(s["hroot"], 10)
            with pe.Fori(0, NB) as b:
                pe.wait_ge(s["q_staged"], b + 1)
                pe.wait_ge(s["newT"], b + 1)
                for j in range(4):
                    last = pe.matmul(B[2][32 * j:32 * j + 32, 0:NS], qst[:, j, :], kS[:, j, :], start=True, stop=True)
                last.then_inc(s["new_scored"], 1)
                for c in range(NCH):
                    pe.wait_ge(k_full[c % 4], 16 * PPC * (2 * b + c // 4 + 1))
                    pe.wait_ge(s["s_out"], NCH * b + c + 1)
                    for j in range(4):
                        last = pe.matmul(B[c % 2][32 * j:32 * j + 32, :], qst[:, j, :], kslot[c % 4][:, :, j, :],
                                         start=True, stop=True)
                    last.then_inc(s["k_used"], 1)
                for g in range(8):
                    pe.wait_ge(s["probs"], 17 * b + 2 * g + 2)
                    pe.wait_ge(s["turned_out"], 8 * b + g + 1)
                    for t in range(4):
                        a = (4 * g + t) * 128
                        last = pe.transpose(B[3 + g % 2][:, 128 * t:128 * t + 128], L[:, a:a + 128], C["ident"])
                    last.then_inc(s["turned"], 1)
                pe.wait_ge(s["probs"], 17 * b + 17)
                pe.transpose(B[2][:, 128:256], L[:, PAST:PAST + 128], C["ident"]).then_inc(s["newT"], 1)
                pe.wait_ge(s["o_scaled"], b + 1)
                for t in range(33):
                    if t < 32 and t % 4 == 0:
                        pe.wait_ge(s["turned_out"], 8 * b + t // 4 + 3)
                        pe.wait_ge(v_full[t // 4], 16 * PPC * (b + 1))
                    if t == 32:
                        pe.wait_ge(s["newT_out"], b + 1)
                    for j in range(4):
                        rhs = vslot[t // 4][:, t % 4, 128 * j:128 * j + 128] if t < 32 else vS[:, 128 * j:128 * j + 128]
                        last = pe.matmul(B[5][32 * j:32 * j + 16, 0:128], PT[:, t, 16 * j:16 * j + 16], rhs,
                                         start=t == 0, stop=t == 32)
                    if t < 32 and t % 4 == 3:
                        last.then_inc(s["v_used"], 1)
                last.then_inc(s["o_sum"], 1)
                pe.wait_ge(s["o_scaled"], b + 2)
                pe.wait_ge(s["oT_out"], 2 * b + 1)
                pe.transpose(B[6][:, 0:128], On, C["ident"]).then_inc(s["oT"], 1)
            with pe.Fori(0, 4) as j:
                pe.wait_ge(s["staged"], 4 * j + 4)

                def p_turn(e):
                    h, i = steps[e]
                    pe.wait_ge(s["p_prob"], 8 * j + e + 1)
                    pe.wait_ge(s["p_turned_out"], 8 * j + e + 1)
                    for t in range(i + 1):
                        last = pe.transpose(B[2 + e % 2][:, 128 * t:128 * t + 128], plog[h][:, 128 * t:128 * t + 128], C["ident"])
                    last.then_inc(s["p_turned"], 1)
                for e, (h, i) in enumerate(steps):
                    pe.wait_ge(s["p_logits"], 8 * j + e + 1)
                    pe.matmul(B[e % 2][:, 0:128 * (i + 1)], pq[64 * h:64 * h + 64, 128 * i:128 * i + 128],
                              pk[64 * h:64 * h + 64, 0:128 * (i + 1)], start=True, stop=True).then_inc(s["p_scores"], 1)
                    if e:
                        p_turn(e - 1)
                p_turn(7)
                pe.wait_ge(s["p_turned_out"], 8 * j + 10)
                for t in range(4):
                    for h in range(2):
                        last = pe.matmul(B[4][64 * h:64 * h + 64, 128 * t:NP], pv[:, t, 64 * h:64 * h + 64],
                                         pPT[h][:, t, 128 * t:NP], start=t == 0, stop=t == 3)
                last.then_inc(s["mixP"], 1)
            pe.wait_ge(s["p_stored"], 5)
            for m in range(KT):
                if m % 4 == 0:
                    pe.wait_ge(s[f"wo_full{m // 4}"], 16)
                if m >= 2:
                    pe.wait_ge(s["res1"], 2 * (m - 1))
                for k in range(KT):
                    w = slot[m // 4][:, k, 128 * (m % 4):128 * (m % 4) + 128]
                    a = pe.matmul(B[m % 2][:, :], w, mP[:, k, :], start=k == 0, stop=k == KT - 1)
                    b_ = pe.matmul(B[2 + m % 2][:, 0:NS], w, mS[:, k, :], start=k == 0, stop=k == KT - 1)
                a.then_inc(s["mixP"], 1)
                b_.then_inc(s["mixS"], 1)
            norm_pe(pe, s["squared2"], s["sums2"])
            pe.wait_ge(s["h2_ready"], KT)
            pe.wait_ge(s["h_scaled2"], 2 * KT)
            pe.wait_ge(s["bank_cleared"], 1)

            def tok(k, t):
                return hP[:, k, 128 * t:128 * t + 128] if t < 4 else hS[:, k, :]
            for t in range(TT):
                r = min(128, NT - 128 * t)
                for k in range(KT):
                    last = pe.matmul(B[6][0:r, 36 * t:36 * t + 36], tok(k, t), wrt[:, k, :], start=k == 0, stop=k == KT - 1)
            last.then_inc(s["route_scores"], 1)
            for t in range(2 * TT):
                r = min(128, NT - 128 * (t // 2))
                if t >= 2:
                    pe.wait_ge(s["h2_out"], t - 1)
                for k in range(4):
                    last = pe.transpose(B[t % 2][0:r, 128 * k:128 * k + 128], tok(4 * (t % 2) + k, t // 2), C["ident"])
                last.then_inc(s["h2_turn"], 1)
            pe.wait_ge(s["hot"], 1)
            for t in range(TT):
                for a in range(t + 1):
                    pe.matmul(B[7][:, 32 * t:32 * t + 32], C["before"] if a == t else ones[:, :], hotm[:, a, :],
                              start=a == 0, stop=a == t)
            for a in range(TT):
                last = pe.matmul(B[7][:, 32 * TT:32 * TT + 32], ones[:, :], hotm[:, a, :], start=a == 0, stop=a == TT - 1)
            last.then_inc(s["ranked"], 1)
            pe.wait_ge(s["listed"], 2)
            for x in range(2 * TT):
                last = pe.matmul(B[5][:, 0:3 * MAXBLK], rows[:, x, :, :].rearrange("p h r -> p (h r)"),
                                 blks[:, x, :, :].rearrange("p c b -> p (c b)"), start=x == 0, stop=x == 2 * TT - 1)
            last.then_inc(s["lists_summed"], 1)
            pe.wait_ge(s["n_ready"], 1)
            n_pair = pe.value_load(nint[0:1, 0:1], min_val=NE // 2, max_val=MAXBLK // 2)
            with pe.Fori(0, n_pair) as i:
                for p in range(2):
                    pe.wait_ge(gathered[p], 16 * i + 16)
                    for c in range(4):
                        last = pe.transpose(B[0][:, 128 * c:128 * c + 128], Xg[p][:, 128 * c:128 * c + 128], C["ident"])
                    last.then_inc(s["x_turned"], 1)
                    xv = XT[p].rearrange("q (c h r) -> q c h r", c=4, h=2)
                    pe.wait_ge(s["xT_ready"], 2 * i + p + 1)
                    for w in range(2):
                        pe.wait_ge(e_full[p][w], 16 * i + 16)
                        wv = eslot[p][w].rearrange("q (k n) -> q k n", k=KT)
                        for k in range(KT):
                            h, c = divmod(k, 4)
                            for f in range(2):
                                last = pe.matmul(B[1 + w][64 * f:64 * f + 64, 0:256], xv[:, c, h, :],
                                                 wv[:, k, 256 * f:256 * f + 256], start=k == 0, stop=k == KT - 1)
                    last.then_inc(s["gate_up"], 1)
                    pe.wait_ge(s["act_ready"], 2 * i + p + 1)
                    for c in range(2):
                        last = pe.transpose(B[3][:, 128 * c:128 * c + 128], aa[p][:, 128 * c:128 * c + 128], C["ident"])
                    last.then_inc(s["a_turned"], 1)
                    pe.wait_ge(s["aT_ready"], 2 * i + p + 1)
                    pe.wait_ge(e_full[p][2], 16 * i + 16)
                    pe.wait_ge(s["y_out"], 2 * i + p + 1)
                    av = aT[p].rearrange("q (c f r) -> q c f r", c=2, f=2)
                    wv = eslot[p][2].rearrange("q (k n) -> q k n", k=FF // 128)
                    for k in range(FF // 128):
                        f, c = divmod(k, 2)
                        for h in range(2):
                            last = pe.matmul(B[4 + p][64 * h:64 * h + 64, :], av[:, c, f, :], wv[:, k, 512 * h:512 * h + 512],
                                             start=k == 0, stop=k == FF // 128 - 1)
                    last.then_inc(s["down"], 1)
            for t in range(TT):
                r = min(128, NT - 128 * t)
                pe.wait_ge(s["combined"], t + 1)
                if t:
                    pe.wait_ge(s["final"], KT * t)
                for k in range(KT):
                    last = pe.transpose(B[k // 4][:, 128 * (k % 4):128 * (k % 4) + r], yc[t % 2][0:r, 128 * k:128 * k + 128],
                                        C["ident"][0:r, 0:r])
                    if k % 4 == 3:
                        last.then_inc(s["c_turned"], 1)


def constants():
    lay, width = const_layout()
    c = np.zeros((128, width), np.float32)

    def put(name, a):
        at, w = lay[name]
        c[:a.shape[0], at:at + w] = a.reshape(a.shape[0], -1)
    p = np.arange(128)
    put("ident", np.eye(128))
    put("sel", (p[:, None] % 32 == np.arange(NSEQ)[None]) * 1.0)
    put("heads", (p[:, None] // 64 == p[None] // 64) * 1.0)
    put("before", (p[:, None] < p[None]) * 1.0)
    rel = (np.arange(NP) - (NP - 128))[None] - p[:, None]
    put("causal", np.where(rel <= 0, rel, -1e32))
    r = p % 32
    live = r < 2 * NQ
    head = 2 * (p // 32) + r // NQ
    slope = np.where(live, 2.0 ** -(head + 1.0), 0.0)[:, None]
    q = (r % NQ)[:, None]
    put("jbias", slope * np.arange(BLK)[None])
    put("blockoff", slope * (BLK * np.arange(NBLK)[None] - PAST - q))
    sb_, si = np.arange(NS) // NQ, np.arange(NS) % NQ
    ok = (sb_[None, None] == np.arange(NB)[None, :, None]) & (si[None, None] <= q[:, :, None])
    nbias = np.where(ok, slope[:, :, None] * (si[None, None] - q[:, :, None]), OFF)
    put("newbias", np.where(live[:, None, None], nbias, 0.0))
    put("iota", np.tile(np.arange(64), (128, 1)))
    t = np.arange(16)
    put("share", np.tile(np.concatenate([1.0 / np.minimum(t + 1, 2 << g) for g in range(4)]), (128, 1)))
    tok = 128 * np.arange(TT)[None] + p[:, None]
    put("valid", (tok < NT) * 1.0)
    put("payload", np.stack([np.stack([2 * tok, 2 * (k * NT + tok)], -1) for k in range(2)], 2))
    put("thr", np.tile(RB * (np.arange(16) + 1), (128, 1)))
    put("slopes", np.tile(2.0 ** -(np.arange(NH) + 1.0), (128, 1)))
    put("eps", np.full((128, 1), EPS))
    put("two", np.tile(2 * np.arange(16), (128, 1)))
    put("half", p[:, None] // RB)
    put("dump", 2 * (2 * NT + p[:, None] % RB))
    put("ovid", np.tile(np.arange(NOV), (128, 1)))
    return c


def kernel(**inputs):
    import numpy as _np
    import concourse.bacc as _bacc
    from concourse import mybir as _mybir
    from concourse.bass_utils import run_bass_kernel_spmd as _run

    a = {k: _np.asarray(v) for k, v in inputs.items()}
    cc = _np.ascontiguousarray
    cols = lambda v: v.reshape(-1, 128).T
    x = _np.concatenate([a["x_prompt"].reshape(NP, D), a["x_sample"].reshape(NS, D)])
    c9 = _np.concatenate([a["c_prompt"], a["c_sample"]])
    nph = a["cache_k"].shape[1]
    gq, gk = (_np.concatenate([a[n][0], a[n][0]])[:, None] for n in ("g_q", "g_k"))
    arr = {
        "xT": cc(x.T), "cT": cc(c9.T), "consts": constants(), "pages": a["page_table"].reshape(1, -1),
        "b_ada": cc(_np.broadcast_to(cols(a["b_ada"][0])[:, :, None], (128, 6 * KT, NSEQ))),
        "gcols": cc(_np.concatenate([cols(a["g_attn_norm"][0]), cols(a["g_ffn_norm"][0]), gq, gk, cols(a["pool_scale"][0])], 1)),
        "w_ada": a["w_ada"][0], "w_in": a["w_in"][0], "w_out": a["w_out"][0], "w_pool": a["w_pool"][0],
        "histT": cc(a["state_pool"][0].transpose(2, 0, 1)),
        "kT": cc(a["cache_k"][0].reshape(nph, PAGE, 4, 128).transpose(0, 3, 2, 1)),
        "v": a["cache_v"][0].reshape(nph, PAGE, AW),
        "w_route": cc(_np.concatenate([a["w_group"][0], a["w_expert"][0]], 1)),
        "b_route": cc(_np.broadcast_to(_np.concatenate([a["b_group"][0], a["b_expert"][0]])[None], (128, 36))),
        "w_gate": a["w_gate"][0], "w_up": a["w_up"][0], "w_down": a["w_down"][0],
    }
    outs = {"yT": (D, NT), "kT": (AW, NT), "v": (NT, AW), "poolT": (PW, NSEQ, HIST)}
    nc = _bacc.Bacc("TRN2", target_bir_lowering=False, num_devices=1)
    d = {n: nc.dram_tensor(f"in_{n}", v.shape, _mybir.dt.from_np(v.dtype), kind="ExternalInput").ap() for n, v in arr.items()}
    o = {n: nc.dram_tensor(f"out_{n}", sh, _mybir.dt.float32, kind="ExternalOutput").ap() for n, sh in outs.items()}
    build_kernel(nc, d, o)
    r = _run(nc, [{f"in_{n}": cc(v) for n, v in arr.items()}], core_ids=[0]).results[0]
    y, k, v, pl = (_np.asarray(r[f"out_{n}"]) for n in ("yT", "kT", "v", "poolT"))
    y, k, pl = y.T, k.T, pl.transpose(1, 2, 0)
    return (cc(y[:NP]).reshape(1, NP, D), cc(y[NP:]).reshape(NB, NQ, D),
            cc(k[:NP]).reshape(1, 1, NP, NH, HD), cc(v[:NP]).reshape(1, 1, NP, NH, HD), cc(pl[:1]).reshape(1, 1, HIST, PW),
            cc(k[NP:]).reshape(1, NB, NQ, NH, HD), cc(v[NP:]).reshape(1, NB, NQ, NH, HD), cc(pl[1:]).reshape(1, NB, HIST, PW))
```

```python
import concourse.bass as bass
from concourse import mybir
from contextlib import ExitStack
import numpy as np

D = 1024
NP, NB, NQ = 512, 8, 8
NS = NB * NQ
NT = NP + NS
KT = D // 128
NSEQ = 1 + NB
PW, AW, HD, NH = 512, 512, 64, 8
HIST = 15
PAST, PAGE, BLK, TOPK = 4096, 128, 256, 3
NBLK = PAST // BLK
CH = 512
NCH = PAST // CH
PPC = CH // PAGE
NE, FF = 32, 512
RB = 64
MAXBLK = NE + 2 * NT // RB
NOV = MAXBLK - NE
TT = (NT + 127) // 128
EPS = 1e-6
OFF = -1e30
U = 4096
US = HIST + NQ
UW = HIST + NP + NB * US


def const_layout():
    at, out = 0, {}
    for name, width in (("ident", 128), ("sel", NSEQ), ("heads", 128), ("before", 128), ("causal", NP),
                        ("jbias", BLK), ("blockoff", NBLK), ("newbias", NB * NS), ("iota", 64),
                        ("share", 4 * 16), ("valid", TT), ("payload", TT * 4), ("thr", 16),
                        ("slopes", NH), ("eps", 1), ("two", 16), ("ovid", NOV), ("half", 1), ("dump", 1)):
        out[name] = (at, width)
        at += width
    return out, at


def build_kernel(nc, d, o):
    f32, i32, u32 = mybir.dt.float32, mybir.dt.int32, mybir.dt.uint32
    ALU, ACT, AX = mybir.AluOpType, mybir.ActivationFunctionType, mybir.AxisListType
    ds = bass.ds
    ctx = ExitStack()
    with ctx:
        def sb(name, shape, dt=f32):
            return ctx.enter_context(nc.sbuf_tensor(name, shape, dt))

        def sem(name):
            return ctx.enter_context(nc.semaphore(name))

        ring = sb("ring", [128, 6 * U])
        wbuf = sb("wbuf", [128, U])
        xP = wbuf[:, :].rearrange("p (k t) -> p k t", k=KT)
        uxr = sb("uxr", [128, 4 * UW])
        uX = uxr[:, :].rearrange("p (g t) -> p g t", g=4)
        rstd = uxr[:, 0:NT]
        xS = uxr[:, NT:NT + KT * NS].rearrange("p (k t) -> p k t", k=KT)
        hP, hS = sb("hP", [128, KT, NP]), sb("hS", [128, KT, NS])
        mP, mS = hP, hS
        qP, kP = sb("qP", [128, 4, NP]), sb("kP", [128, 4, NP])
        vP = sb("vP", [128, NP // 128, AW])
        qS, kS = sb("qS", [128, 4, NS]), sb("kS", [128, 4, NS])
        vS = sb("vS", [128, AW])
        modT = sb("modT", [128, 6 * KT, NSEQ])
        big = sb("big", [128, PAST + 128 + 33 * 64])
        L = big[:, 0:PAST + 128]
        PT = big[:, PAST + 128:PAST + 128 + 33 * 64].rearrange("p (t c) -> p t c", c=64)
        sq = big[:, 0:KT * NT].rearrange("p (k t) -> p k t", t=NT)
        CL, CW = const_layout()
        cst = sb("cst", [128, CW])
        C = {n: cst[:, a:a + w] for n, (a, w) in CL.items()}
        ones = sb("ones", [128, 128])
        cT = ring[:, 4 * U + 512:4 * U + 512 + KT * NSEQ].rearrange("p (k s) -> p k s", s=NSEQ)
        scT = qS[:, :, :].rearrange("p j t -> p (j t)").rearrange("p (k c) -> p k c", k=KT)
        part = sb("part", [128, 512])
        coef = part[:, 256:256 + KT * NSEQ].rearrange("p (k s) -> p k s", s=NSEQ)
        gcols = sb("gcols", [128, 2 * KT + 2 + 4])
        g1, g2 = gcols[:, 0:KT], gcols[:, KT:2 * KT]
        gq, gk = gcols[:, 2 * KT:2 * KT + 1], gcols[:, 2 * KT + 1:2 * KT + 2]
        pscale = gcols[:, 2 * KT + 2:2 * KT + 6]
        pages = sb("pages", [1, NB * PAST // PAGE], i32)
        gsum, bmax, pen, ebias = (sb(n, [128, NBLK]) for n in ("gsum", "bmax", "pen", "ebias"))
        top8, topf = sb("top8", [128, 8]), sb("topf", [128, 8])
        topi = sb("topi", [128, 8], u32)
        st = sb("st", [128, 8])
        nmax, gmax_, negm, tot, rinv = (st[:, i:i + 1] for i in range(5))
        esum = sb("esum", [128, NBLK + 1])
        On = part[:, 0:128]
        qst = part[:, 128:256].rearrange("p (j c) -> p j c", j=4)
        wrt = uxr[:, 1536:1536 + KT * 36].rearrange("p (k n) -> p k n", k=KT)
        brt = uxr[:, 2048:2084]

        bT = ring[:, 5 * U:5 * U + 6 * KT * NSEQ].rearrange("p (c s) -> p c s", s=NSEQ)
        wpool = hP[:, 4, :].rearrange("p (g n) -> p g n", g=4)
        win1, win2 = (vP[:, :, :].rearrange("p a b -> p (a b)")[:, i * UW:(i + 1) * UW] for i in range(2))
        part2 = big[:, 5 * 1024:5 * 1024 + 512]

        B = [ctx.enter_context(nc.psum_tensor(f"bank{i}", [128, 512], f32)) for i in range(8)]

        h2d = nc.dram_tensor("h2d", (2 * NT, 512), f32, kind="Internal").ap()
        y2 = nc.dram_tensor("y2", (2 * (2 * NT + RB), 512), f32, kind="Internal").ap()

        s = {n: sem(n) for n in (
            "small", "x_in", "late_in", "wpool_in", "zeroed", "silu", "ada_part", "ada_copied", "ada_cols",
            "ada_done", "squared", "sums", "rooted", "h_scaled", "h_ready", "zP", "zS", "zP_out", "zS_out",
            "hsq", "hsum", "hroot", "normed", "qbd_ready", "pooled", "ypool", "ypool_out",
            "q_staged", "new_scored", "new_out", "k_used", "s_out", "exp_bias", "probs", "turned", "turned_out",
            "newT", "newT_out", "v_used", "o_sum", "rinv_ready", "o_scaled", "oT", "oT_out", "w2_full", "x_back",
            "staged", "p_scores", "p_logits", "p_neg", "p_exp", "p_prob", "p_turned", "p_turned_out", "p_out", "p_stored",
            "wo_full0", "wo_full1", "mixP", "mixS", "res1", "squared2", "sums2", "rooted2", "h_scaled2", "h2_ready", "h2_turn",
            "h2_out", "h2_stored", "route_scores", "g_exp_in", "g_exp", "hot", "ranked", "listed", "lists_summed",
            "n_ready",
            "g_staged", "s_staged", "x_turned", "xT_ready", "gate_up", "silu_ready", "act_ready", "a_turned",
            "aT_ready", "down", "y_out", "w_given", "y_back", "combined", "c_turned", "final", "stored",
            "dve", "dve2", "dve3", "act", "pool", "pool2", "settle", "bank_cleared")}
        w_full = [sem(f"w_full{i}") for i in range(4)]
        k_full = [sem(f"k_full{i}") for i in range(4)]
        v_full = [sem(f"v_full{i}") for i in range(8)]
        gathered = [sem(f"gathered{i}") for i in range(2)]
        y_scat = [sem(f"y_scattered{i}") for i in range(2)]
        e_full = [[sem(f"e_full{p}{i}") for i in range(3)] for p in range(2)]

        slot = [ring[:, i * U:(i + 1) * U].rearrange("p (k n) -> p k n", k=KT) for i in range(6)]
        kslot = [ring[:, i * 2048:(i + 1) * 2048].rearrange("p (g j s) -> p g j s", g=PPC, j=4) for i in range(4)]
        vslot = [ring[:, 2 * U + i * 2048:2 * U + (i + 1) * 2048].rearrange("p (g n) -> p g n", g=PPC)
                 for i in range(8)]
        eslot = [[ring[:, ((3 - 3 * p) + i) * U:((3 - 3 * p) + i + 1) * U] for i in range(3)] for p in range(2)]

        def chain(eng, sm, start=0):
            n = [0]

            def then(ins):
                n[0] += 1
                ins.then_inc(sm, 1)
                eng.wait_ge(sm, start + n[0])
            return then, n

        pq, pk = uxr[:, 0:512], uxr[:, 512:1024]
        pv = uxr[:, 1024:1536].rearrange("p (t n) -> p t n", t=4)
        plog = [uxr[:, 1536 + 512 * i:2048 + 512 * i] for i in range(2)]
        pslope, pst = uxr[:, 2560:2562], uxr[:, 2564:2572]
        pPT = [wbuf[:, 2048 * i:2048 * (i + 1)].rearrange("p (t q) -> p t q", t=4) for i in range(2)]
        w2 = wbuf[:, :].rearrange("p (k n) -> p k n", k=KT)

        h2tok = big[:, 0:TT * D].rearrange("p (t n) -> p t n", t=TT)
        rs = qP[:, :, :].rearrange("p a b -> p (a b)")
        ri = kP[:, :, :].rearrange("p a b -> p (a b)")
        at = [0]

        def cut(n):
            a = at[0]
            at[0] += n
            assert at[0] <= 2048
            return rs[:, a:a + n]
        lg = cut(TT * 36).rearrange("p (t n) -> p t n", t=TT)
        lg8 = cut(TT * 8).rearrange("p (t n) -> p t n", t=TT)
        gtop = cut(TT * 8).rearrange("p (t n) -> p t n", t=TT)
        etop = cut(TT * 8).rearrange("p (t n) -> p t n", t=TT)
        ein = cut(TT * 8).rearrange("p (t n) -> p t n", t=TT)
        gif = cut(TT)
        gexp = cut(TT * 4).rearrange("p (t n) -> p t n", t=TT)
        gw = cut(TT)
        goh = cut(TT * 4).rearrange("p (t n) -> p t n", t=TT)
        gtmp = cut(TT * 32)
        edif = cut(TT)
        eex = cut(TT)
        eden = cut(TT)
        wts = sb("wts", [128, 2, TT])
        ek = cut(TT * 2)
        hot = cut(TT * 2 * 32)
        hotm = cut(TT * 32).rearrange("p (t e) -> p t e", t=TT)
        cum = cut((TT + 1) * 32).rearrange("p (t e) -> p t e", t=TT + 1)
        over, incl, base2 = cut(32), cut(32), cut(32)
        pos, ost, bno, far, blk_ = (cut(TT * 2) for _ in range(5))
        ovt = ri[:, 0:NOV * 32]
        prod = ri[:, 576:576 + TT * 2 * 32]
        past = ri[:, 1400:1400 + TT * 2 * 8]
        ti = ri[:, 1024:1024 + 300].bitcast(u32)
        gidx = ti[:, 0:TT * 8].rearrange("p (t n) -> p t n", t=TT)
        eidx = ti[:, 40:40 + TT * 8].rearrange("p (t n) -> p t n", t=TT)
        oveif = cut(NOV)
        npf = cut(2)
        nint = sb("nint", [1, 3 + NOV], i32)
        rows = vP[:, :, :].rearrange("p a b -> p (a b)")[:, 0:2 * TT * 128].rearrange("p (x h r) -> p x h r", h=2, r=RB)
        blks = ri[:, 0:2 * TT * 3 * MAXBLK].rearrange("p (x c b) -> p x c b", c=3, b=MAXBLK)
        first = sb("first", [1, 4])
        tblS = sb("tblS", [128, 2, MAXBLK + 2], u32)

        o_ = [0]

        def mo(n):
            a = o_[0]
            o_[0] += n
            assert o_[0] <= PAST + 128 + 33 * 64
            return big[:, a:a + n]
        Xg = [mo(512) for _ in range(2)]
        XT = [mo(512) for _ in range(2)]
        gs = [mo(256) for _ in range(2)]
        aa = [mo(256) for _ in range(2)]
        aT = [mo(256) for _ in range(2)]
        Yo = [mo(512) for _ in range(2)]
        gix = [sb(f"gix{i}", [128, 1], u32) for i in range(2)]
        six = [sb(f"six{i}", [128, 1], u32) for i in range(2)]
        yb = [[ring[:, (2 * i + j) * 1024:(2 * i + j + 1) * 1024] for j in range(2)] for i in range(2)]
        yc = [ring[:, (4 + i) * 1024:(5 + i) * 1024] for i in range(2)]

        def sp_pages(ap):
            return nc.values_load_multi_w_load_instructions(
                ap, engines=(mybir.EngineType.SP,), min_val=0, max_val=d["v"].shape[0] - 1,
                skip_runtime_bounds_check_because="a page table names pages of the pool")[1]

        block = ctx.enter_context(nc.Block())

        @block.sync
        def _(sp):
            sp.sem_inc(s["k_used"], 4)
            sp.sem_inc(s["v_used"], 8)
            sp.dma_start(cT, d["cT"].rearrange("(k p) s -> p k s", p=128)).then_inc(s["small"], 16)
            sp.dma_start(cst[:, :], d["consts"]).then_inc(s["small"], 16)
            sp.dma_start(bT, d["b_ada"]).then_inc(s["small"], 16)
            sp.dma_start(gcols[:, :], d["gcols"]).then_inc(s["small"], 16)
            sp.dma_start(pages[:, :], d["pages"]).then_inc(s["small"], 16)
            xT = d["xT"].rearrange("(k p) t -> p k t", p=128)
            sp.dma_start(xP[:, :, :], xT[:, :, 0:NP]).then_inc(s["x_in"], 16)
            sp.dma_start(xS[:, :, :], xT[:, :, NP:NT]).then_inc(s["x_in"], 16)
            w_ada = d["w_ada"].rearrange("(k p) n -> p k n", p=128)
            with sp.Fori(0, 3) as it:
                for u in range(4):
                    sp.wait_ge(s["ada_part"], 4 * it + u + 1)
                    sp.dma_start(slot[u], w_ada[:, :, ds((4 * it + u) * 512, 512)]).then_inc(w_full[u], 16)
            w_in = d["w_in"].rearrange("(k p) n -> p k n", p=128)
            for u in range(4):
                sp.wait_ge(s["ada_part"], 4 + 9 + u)
                sp.dma_start(slot[u], w_in[:, :, u * 512:(u + 1) * 512]).then_inc(w_full[u], 16)
            sp.wait_ge(s["small"], 80)

            def batch_loads(b, unit):
                def chunk_pages(c):
                    return sp_pages(pages[0:1, ds(PPC * NCH * b + PPC * c, PPC)])
                for c in range(NCH):
                    at_ = chunk_pages(c)
                    if unit == 0 and c == 0:
                        sp.wait_ge(s["zS"], 8)
                    sp.wait_ge(s["k_used"], NCH * b + c + 1)
                    for g, pg in enumerate(at_):
                        sp.dma_start(kslot[c % 4][:, g, :, :], d["kT"][ds(pg, 1), :, :, :].rearrange("a p j s -> (a p) j s"))\
                            .then_inc(k_full[c % 4], 16)
                    if unit is not None and c == 3:
                        if unit == 0:
                            sp.wait_ge(s["h_scaled"], 1 + KT)
                            sp.wait_ge(s["normed"], 2)
                        else:
                            sp.wait_ge(s["zP"], 4 * unit)
                        sp.dma_start(w2, w_in[:, :, unit * 512:(unit + 1) * 512]).then_inc(s["w2_full"], 16)
                for c in range(NCH):
                    at_ = chunk_pages(c)
                    if unit == 0 and c == 0:
                        sp.wait_ge(s["zS"], 13)
                    sp.wait_ge(s["v_used"], NCH * b + c + 1)
                    for g, pg in enumerate(at_):
                        sp.dma_start(vslot[c][:, g, :], d["v"][ds(pg, 1), :, :].rearrange("a p n -> (a p) n"))\
                            .then_inc(v_full[c], 16)
            for b in range(4):
                batch_loads(b, b)
            sp.wait_ge(s["zP"], 16)
            sp.dma_start(wpool, d["w_pool"].rearrange("g p n -> p g n")).then_inc(s["wpool_in"], 16)
            with sp.Fori(4, NB) as b:
                batch_loads(b, None)
            w_out = d["w_out"].rearrange("(k p) n -> p k n", p=128)
            sp.wait_ge(s["k_used"], 4 + NB * NCH)
            for u in range(2):
                sp.dma_start(slot[u], w_out[:, :, u * 512:(u + 1) * 512]).then_inc(s[f"wo_full{u}"], 16)
            sp.wait_ge(s["mixP"], 1 + 4)
            sp.wait_ge(s["p_stored"], 1 + 4)
            sp.dma_start(xP[:, :, :], xT[:, :, 0:NP]).then_inc(s["x_back"], 16)
            sp.dma_start(xS[:, :, :], xT[:, :, NP:NT]).then_inc(s["x_back"], 16)
            sp.dma_start(wrt, d["w_route"].rearrange("(k p) n -> p k n", p=128)).then_inc(s["x_back"], 16)
            sp.dma_start(brt, d["b_route"]).then_inc(s["x_back"], 16)
            wg = d["w_gate"].rearrange("e (k p) n -> e p k n", p=128)
            wu = d["w_up"].rearrange("e (k p) n -> e p k n", p=128)
            wd = d["w_down"].rearrange("e (k p) n -> e p k n", p=128)

            def load_expert(e, p):
                for i, (w, k) in enumerate(((wg, KT), (wu, KT), (wd, FF // 128))):
                    sp.dma_start(eslot[p][i].rearrange("q (k n) -> q k n", k=k),
                                 w[ds(e, 1), :, :, :].rearrange("a q k n -> (a q) k n")).then_inc(e_full[p][i], 16)
            sp.wait_ge(s["v_used"], 8 + NB * NCH)
            load_expert(0, 0)
            sp.wait_ge(s["mixS"], 8)
            load_expert(1, 1)
            with sp.Fori(1, NE // 2 - 1) as i:
                for p in range(2):
                    sp.wait_ge(s["down"], 2 * i + p - 1)
                    load_expert(2 * i + p, p)
            sp.wait_ge(s["n_ready"], 1)
            n_pair = sp.value_load(nint[0:1, 0:1], min_val=NE // 2, max_val=MAXBLK // 2)
            with sp.Fori(0, n_pair - (NE // 2 - 1)) as i:
                for p in range(2):
                    e = sp.value_load(nint[0:1, ds(1 + 2 * i + p, 1)], min_val=0, max_val=NE - 1)
                    sp.wait_ge(s["down"], 2 * i + (NE + p - 3))
                    load_expert(e, p)
            for p in range(2):
                sp.wait_ge(y_scat[p], 16 * n_pair + 16)
            for p in range(2):
                sp.wait_ge(gathered[p], 16 * n_pair + 16)
            for t in range(TT):
                r = min(128, NT - 128 * t)
                if t >= 2:
                    sp.wait_ge(s["combined"], t - 1)
                for k in range(2):
                    a = 2 * (k * NT + 128 * t)
                    sp.dma_start(yb[t % 2][k][0:r, :], y2[a:a + 2 * r, :].rearrange("(p h) n -> p (h n)", h=2))\
                        .then_inc(s["y_back"], 16)
                sp.wait_ge(s["y_back"], 32 * (t + 1))
            sp.wait_ge(s["final"], TT * KT)
            sp.dma_start(o["yT"].rearrange("(k p) t -> p k t", p=128)[:, :, 0:NP], xP[:, :, :]).then_inc(s["stored"], 16)
            sp.dma_start(o["yT"].rearrange("(k p) t -> p k t", p=128)[:, :, NP:NT], xS[:, :, :]).then_inc(s["stored"], 16)
            sp.wait_ge(s["stored"], 11 * 16)

        @block.gpsimd
        def _(pool):
            pool.memset(ones[:, :], 1.0).then_inc(s["zeroed"], 1)
            pool.wait_ge(s["zeroed"], 1)
            pool.memset(scT[:, :, :], 0.0).then_inc(s["zeroed"], 1)
            pool.wait_ge(s["zeroed"], 2)
            pool.memset(vS[64:128, :], 0.0).then_inc(s["zeroed"], 1)
            pool.wait_ge(s["zeroed"], 3)
            pool.memset(tblS[:, :, :], 0).then_inc(s["zeroed"], 1)
            pool.wait_ge(s["zeroed"], 4)
            pool.wait_ge(s["h_scaled"], 1 + KT)
            pool.memset(uX[:, :, 0:HIST], 0.0).then_inc(s["zeroed"], 1)
            pool.wait_ge(s["zeroed"], 5)
            then, n = chain(pool, s["pool"])
            pool.wait_ge(s["late_in"], 4 * 16)
            pool.wait_ge(s["zP_out"], 4)
            pool.wait_ge(s["zS_out"], 4)
            for g in range(4):
                src = uX[:, g, :]
                for a in range(g + 1):
                    k = 1 << a
                    dst = (win1, win2)[a % 2]
                    lo = 2 * k - 1
                    if a == 0 and g:
                        pool.wait_ge(s["pooled"], g)
                    then(pool.tensor_tensor(dst[:, lo:UW], src[:, lo:UW], src[:, lo - k:UW - k], ALU.add))
                    src = dst
            pool.wait_ge(s["normed"], 10)
            pool.wait_ge(s["zP_out"], 16)
            pool.wait_ge(s["ypool"], 4)
            with pool.Fori(0, 4) as j:
                pool.wait_ge(s["mixP"], j + 1)
                pool.wait_ge(s["p_stored"], j + 1)
                pool.sem_inc(s["settle"], 1)
                for k, (dst, src) in enumerate(((pq, qP[:, ds(j, 1), :].rearrange("p a n -> p (a n)")),
                                                (pk, kP[:, ds(j, 1), :].rearrange("p a n -> p (a n)")),
                                                (pv, vP[:, :, ds(128 * j, 128)]), (pslope, C["slopes"][:, ds(2 * j, 2)]))):
                    pool.tensor_copy(dst, src).then_inc(s["staged"], 1)
                    pool.wait_ge(s["staged"], 4 * j + k + 1)
                    pool.sem_inc(s["settle"], 1)
            pool.wait_ge(s["n_ready"], 1)
            pool.wait_ge(s["h2_stored"], 16 * TT)
            n_pair = pool.value_load(nint[0:1, 0:1], min_val=NE // 2, max_val=MAXBLK // 2)

            def gather(p):
                pool.indirect_dma_start(Xg[p], None, h2d, bass.IndirectOffsetOnAxis(gix[p][:, :], 0)).then_inc(gathered[p], 16)
            pool.wait_ge(s["g_staged"], 2)
            for p in range(2):
                gather(p)
                pool.dma_start(first[:, 2 * p:2 * p + 2], d["consts"][p:p + 1, 0:2]).then_inc(y_scat[p], 16)
            with pool.Fori(0, n_pair) as i:
                for p in range(2):
                    pool.wait_ge(s["g_staged"], 2 * i + p + 3)
                    pool.wait_ge(s["x_turned"], 2 * i + p + 1)
                    pool.sem_inc(s["settle"], 1)
                    gather(p)
                    pool.wait_ge(s["y_out"], 2 * i + p + 3)
                    pool.wait_ge(y_scat[1 - p], 16 * i + 16 * (p + 1))
                    pool.sem_inc(s["settle"], 1)
                    pool.indirect_dma_start(y2, bass.IndirectOffsetOnAxis(six[p][:, :], 0), Yo[p], None)\
                        .then_inc(y_scat[p], 16)

        def norm_roots(act, sq_s, sum_s, root_s):
            for k in range(KT):
                act.activation(sq[:, k, 0:NP], xP[:, k, :], ACT.Square)
                act.activation(sq[:, k, NP:NT], xS[:, k, :], ACT.Square).then_inc(sq_s, 1)
            act.wait_ge(sum_s, 2)
            act.activation(rstd[:, 0:NP], B[4][:, :], ACT.Sqrt, scale=1.0 / D, bias=C["eps"])
            act.activation(rstd[:, NP:NT], B[5][:, 0:NS], ACT.Sqrt, scale=1.0 / D, bias=C["eps"]).then_inc(root_s, 1)

        def norm_shift(act, scaled_s, ready_s, shift):
            for k in range(KT):
                act.wait_ge(scaled_s, k + 2)
                act.activation(hP[:, k, :], hP[:, k, :], ACT.Identity, bias=modT[:, shift * KT + k, 0:1])\
                    .then_inc(ready_s, 1)

        def norm_pe(pe, sq_s, sum_s):
            for k in range(KT):
                pe.wait_ge(sq_s, k + 1)
                p_ = pe.matmul(B[4][:, :], ones[:, :], sq[:, k, 0:NP], start=k == 0, stop=k == KT - 1)
                s_ = pe.matmul(B[5][:, 0:NS], ones[:, :], sq[:, k, NP:NT], start=k == 0, stop=k == KT - 1)
            p_.then_inc(sum_s, 1)
            s_.then_inc(sum_s, 1)

        def norm_scale(dve, then, scaled_s, g, scale, shift):
            then(dve.scalar_tensor_tensor(coef, modT[:, scale * KT:(scale + 1) * KT, :], 1.0,
                                          g.unsqueeze(2).to_broadcast([128, KT, NSEQ]), ALU.add, ALU.mult))
            h4_ = hS[:, :, :].rearrange("p k (b q) -> p k b q", b=NB)
            then(dve.tensor_tensor(h4_, xS.rearrange("p k (b q) -> p k b q", b=NB),
                                   coef[:, :, 1:NSEQ].unsqueeze(3).to_broadcast([128, KT, NB, NQ]), ALU.mult))
            then(dve.tensor_tensor(hS[:, :, :], hS[:, :, :], rstd[:, NP:NT].unsqueeze(1).to_broadcast([128, KT, NS]), ALU.mult))
            dve.tensor_tensor(h4_, h4_, modT[:, shift * KT:(shift + 1) * KT, 1:NSEQ].unsqueeze(3)
                              .to_broadcast([128, KT, NB, NQ]), ALU.add).then_inc(scaled_s, 1)
            for k in range(KT):
                dve.scalar_tensor_tensor(hP[:, k, :], xP[:, k, :], coef[:, k, 0:1], rstd[:, 0:NP],
                                         ALU.mult, ALU.mult).then_inc(scaled_s, 1)

        uxs = uX[:, :, HIST + NP:UW].rearrange("p g (b t) -> p g b t", b=NB)
        pieces = [(qS[:, :, :].rearrange("p j t -> p (j t)"), 0), (kS[:, :, :].rearrange("p j t -> p (j t)"), 1)]
        pieces += [(qP[:, m, :], 0) for m in range(4)] + [(kP[:, m, :], 1) for m in range(4)]
        hsq = [wbuf[:, 512 * i:512 * (i + 1)] for i in range(2)]
        hrt = [wbuf[:, 512 * (i + 2):512 * (i + 3)] for i in range(2)]
        hbank = [B[5], B[6]]
        steps = [(h, i) for i in range(4) for h in range(2)]
        zbank = [B[5], B[6], B[7], B[5]]
        z_at = {("q", 5): (0,), ("q", 7): (1, 2), ("v", 3): (3,)}
        z_out_at = {("q", 5): (0,), ("s", 0): (1, 2), ("v", 3): (3,)}
        p_at = {(kind, c): e for e, (kind, c) in enumerate([("q", 1), ("q", 3), ("q", 5), ("q", 7),
                                                             ("v", 1), ("v", 3), ("v", 5), ("v", 7), ("e", 0)])}

        @block.scalar
        def _(act):
            act.wait_ge(s["small"], 80)
            act.wait_ge(s["zeroed"], 4)
            act.activation(scT[:, :, 0:NSEQ], cT, ACT.Silu).then_inc(s["silu"], 1)
            act.wait_ge(s["x_in"], 32)
            norm_roots(act, s["squared"], s["sums"], s["rooted"])
            with act.Fori(0, 6) as u:
                for i in range(2):
                    act.wait_ge(s["ada_part"], 2 * u + i + 5)
                    act.activation((part[:, :], part2)[i], B[i][:, :], ACT.Copy).then_inc(s["ada_copied"], 1)
            norm_shift(act, s["h_scaled"], s["h_ready"], 0)
            for g in range(4):
                act.dma_start(uxs[:, g, :, 0:HIST], d["histT"][g * 128:(g + 1) * 128, :, :]).then_inc(s["late_in"], 16)

            def head_roots(first, last):
                for i in range(first, last):
                    x = pieces[i][0]
                    w = x.shape[1]
                    act.activation(hsq[i % 2][:, 0:w], x, ACT.Square).then_inc(s["hsq"], 1)
                    if i > first:
                        root(i - 1)
                root(last - 1)

            def root(i):
                w = pieces[i][0].shape[1]
                act.wait_ge(s["hsum"], i + 1)
                if i >= 2:
                    act.wait_ge(s["normed"], i - 1)
                act.activation(hrt[i % 2][:, 0:w], hbank[i % 2][:, 0:w], ACT.Sqrt, scale=1.0 / HD, bias=C["eps"])\
                    .then_inc(s["hroot"], 1)
            act.wait_ge(s["zS_out"], 13)
            head_roots(0, 2)
            act.wait_ge(s["normed"], 2)
            act.dma_start(o["kT"].rearrange("(j p) t -> p j t", p=128)[:, :, NP:NT], kS[:, :, :]).then_inc(s["stored"], 16)
            act.dma_start(o["v"][NP:NT, :], vS[0:NS, :]).then_inc(s["stored"], 16)

            def act_batch(b, extra):
                for c in range(NCH):
                    extra("q", c)
                act.wait_ge(s["exp_bias"], b + 1)
                for n in range(NBLK):
                    act.activation(L[:, BLK * n:BLK * (n + 1)], L[:, BLK * n:BLK * (n + 1)], ACT.Exp,
                                   bias=ebias[:, n:n + 1], accum_out=esum[:, n:n + 1]).then_inc(s["probs"], 1)
                act.activation(L[:, PAST:PAST + NS], L[:, PAST:PAST + NS], ACT.Exp, bias=negm,
                               accum_out=esum[:, NBLK:NBLK + 1]).then_inc(s["probs"], 1)
                act.wait_ge(s["o_sum"], b + 1)
                for g in range(8):
                    act.wait_ge(s["turned"], 8 * b + g + 2)
                    act.activation(PT[:, 4 * g:4 * g + 4, :].rearrange("p t (j c) -> p (t j) c", j=4),
                                   B[3][:, :].rearrange("p (x c) -> p x c", c=32)[:, :, 0:16],
                                   ACT.Copy).then_inc(s["turned_out"], 1)
                    if g == 0:
                        extra("s", 0)
                    else:
                        extra("v", g - 1)
                act.wait_ge(s["newT"], b + 2)
                act.activation(PT[:, 32, :].rearrange("p (j c) -> p j c", j=4),
                               B[2][:, 128:256].rearrange("p (x c) -> p x c", c=32)[:, :, 0:16],
                               ACT.Copy).then_inc(s["newT_out"], 1)
                extra("v", 7)
                act.wait_ge(s["o_sum"], b + 2)
                act.wait_ge(s["rinv_ready"], b + 1)
                act.activation(On, B[4][:, 0:128], ACT.Copy, scale=rinv).then_inc(s["o_scaled"], 1)
                extra("e", 0)
                act.wait_ge(s["oT"], b + 1)
                act.sem_inc(s["settle"], 1)
                oT = B[2][:, 256:384].rearrange("p (j c) -> p j c", j=4)
                for h in range(2):
                    act.activation(mS[64 * h:64 * h + 64, 4:8, ds(NQ * b, NQ)],
                                   oT[64 * h:64 * h + 64, :, NQ * h:NQ * h + NQ], ACT.Copy).then_inc(s["oT_out"], 1)

            for b in range(4):
                def tiles_out(kind, c):
                    for m in z_out_at.get((kind, c), ()):
                        act.wait_ge(s["zP"], 4 * b + m + 1)
                        if b == 3 and m == 0:
                            act.wait_ge(s["pooled"], 4)
                        dst = (uX[:, m, HIST:HIST + NP], qP[:, m, :], kP[:, m, :], vP[:, m, :])[b]
                        act.activation(dst, zbank[m][:, :], ACT.Copy).then_inc(s["zP_out"], 1)
                act_batch(b, tiles_out)
                if b == 0:
                    act.wait_ge(s["zP_out"], 4)
                    act.wait_ge(s["zS_out"], 4)
                    act.wait_ge(s["late_in"], 4 * 16)
                    act.dma_start(o["poolT"].rearrange("(g p) b t -> p g b t", p=128)[:, :, 0, :],
                                  uX[:, :, NP:NP + HIST]).then_inc(s["stored"], 16)
                    for g in range(4):
                        act.dma_start(o["poolT"][g * 128:(g + 1) * 128, 1:NSEQ, :], uxs[:, g, :, NQ:US])\
                            .then_inc(s["stored"], 16)
            for g in range(4):
                act.wait_ge(s["ypool"], g + 1)
                act.activation(mP[:, g, :], B[5 + g % 2][:, :], ACT.Copy, scale=pscale[:, g:g + 1])
                act.activation(mS[:, g, :], B[g % 2][:, 0:NS], ACT.Copy, scale=pscale[:, g:g + 1])\
                    .then_inc(s["ypool_out"], 1)
            act.wait_ge(s["zP_out"], 16)
            head_roots(2, 10)
            act.wait_ge(s["normed"], 10)
            act.dma_start(o["kT"].rearrange("(j p) t -> p j t", p=128)[:, :, 0:NP], kP[:, :, :]).then_inc(s["stored"], 16)
            act.dma_start(o["v"][0:NP, :].rearrange("(r p) n -> p r n", p=128), vP[:, :, :]).then_inc(s["stored"], 16)
            with act.Fori(4, NB) as b:
                def p_turned_out(n, e):
                    h, i = steps[e]
                    act.wait_ge(s["p_turned"], n + e + 1)
                    act.activation(pPT[h][:, 0:i + 1, 128 * i:128 * i + 128],
                                   B[6][:, 0:128 * (i + 1)].rearrange("p (t q) -> p t q", q=128), ACT.Copy)\
                        .then_inc(s["p_turned_out"], 1)

                def prompt_step(kind, c):
                    if (kind, c) not in p_at:
                        return
                    e = p_at[kind, c]
                    n = 8 * (b - 4)
                    if e:
                        p_turned_out(n, e - 1)
                    if e < 8:
                        h, i = steps[e]
                        act.wait_ge(s["p_neg"], n + e + 1)
                        act.activation(plog[h][:, 0:128 * (i + 1)], plog[h][:, 0:128 * (i + 1)], ACT.Exp,
                                       bias=pst[:, h:h + 1], accum_out=pst[:, 2 + h:3 + h]).then_inc(s["p_exp"], 1)
                act_batch(b, prompt_step)
            act.wait_ge(s["res1"], 2 * KT)
            norm_roots(act, s["squared2"], s["sums2"], s["rooted2"])
            norm_shift(act, s["h_scaled2"], s["h2_ready"], 3)
            for t in range(2 * TT):
                r = min(128, NT - 128 * (t // 2))
                act.wait_ge(s["h2_turn"], t + 1)
                act.activation(h2tok[0:r, t // 2, 512 * (t % 2):512 * (t % 2) + 512], B[t % 2][0:r, :], ACT.Copy)\
                    .then_inc(s["h2_out"], 1)
            for t in range(TT):
                r = min(128, NT - 128 * t)
                act.wait_ge(s["h2_out"], 2 * t + 2)
                act.dma_start(h2d[256 * t:256 * t + 2 * r, :].rearrange("(p h) n -> p (h n)", h=2),
                              h2tok[0:r, t, :]).then_inc(s["h2_stored"], 16)
            act.wait_ge(s["g_exp_in"], 1)
            act.activation(gexp, gexp, ACT.Exp).then_inc(s["g_exp"], 1)
            act.wait_ge(s["g_exp_in"], 2)
            act.activation(eex, edif, ACT.Exp).then_inc(s["g_exp"], 1)
            act.wait_ge(s["n_ready"], 1)
            n_pair = act.value_load(nint[0:1, 0:1], min_val=NE // 2, max_val=MAXBLK // 2)
            with act.Fori(0, n_pair) as i:
                for p in range(2):
                    act.wait_ge(s["x_turned"], 2 * i + p + 1)
                    act.activation(XT[p], B[0][:, :], ACT.Copy).then_inc(s["xT_ready"], 1)
                    act.wait_ge(s["gate_up"], 2 * i + p + 1)
                    act.activation(gs[p], B[1][:, 0:256], ACT.Silu).then_inc(s["silu_ready"], 1)
                    act.wait_ge(s["a_turned"], 2 * i + p + 1)
                    act.activation(aT[p], B[3][:, 0:256], ACT.Copy).then_inc(s["aT_ready"], 1)

        @block.vector
        def _(dve):
            then, n = chain(dve, s["dve"])
            dve.wait_ge(s["small"], 80)
            dve.wait_ge(s["rooted"], 1)
            then(dve.reciprocal(rstd, rstd))
            with dve.Fori(0, 6) as u:
                for i in range(2):
                    dve.wait_ge(s["ada_cols"], 2 * u + i + 1)
                    dve.tensor_tensor(modT[:, ds(8 * u + 4 * i, 4), :],
                                      B[2 + i][:, 0:4 * NSEQ].rearrange("p (c s) -> p c s", s=NSEQ),
                                      bT[:, ds(8 * u + 4 * i, 4), :], ALU.add).then_inc(s["ada_done"], 1)
            dve.wait_ge(s["ada_done"], 14)
            norm_scale(dve, then, s["h_scaled"], g1, 1, 0)
            dve.wait_ge(s["h_scaled"], 1 + KT)
            for T in range(13):
                dve.wait_ge(s["zS"], T + 1)
                n_, m = divmod(T, 4)
                src = B[5 + T % 2][:, 0:NS]
                if n_ == 0:
                    ins = dve.tensor_copy(uxs[:, m, :, HIST:US], src.rearrange("p (b q) -> p b q", b=NB))
                elif n_ < 3:
                    ins = dve.tensor_copy((qS, kS)[n_ - 1][:, m, :], src)
                else:
                    ins = dve.tensor_copy(vS[0:NS, :], B[5 + T % 2][0:NS, :])
                ins.then_inc(s["zS_out"], 1)
            then(dve.tensor_scalar(gq, gq, HD ** -0.5, None, ALU.mult))

            def head_norms(first, last):
                for i in range(first, last):
                    x, which = pieces[i]
                    r = hrt[i % 2][:, 0:x.shape[1]]
                    dve.wait_ge(s["hroot"], i + 1)
                    then(dve.reciprocal(r, r))
                    dve.scalar_tensor_tensor(x, x, (gq, gk)[which], r, ALU.mult, ALU.mult).then_inc(s["normed"], 1)
            head_norms(0, 2)
            then(dve.memset(qst, 0.0))
            then(dve.memset(L[:, PAST:PAST + 128], 0.0))
            dve.wait_ge(s["normed"], 2)
            jb = C["jbias"].unsqueeze(1).to_broadcast([128, CH // BLK, BLK])
            PER = 12
            nb = C["newbias"].rearrange("p (b t) -> p b t", b=NB)

            def dve_batch(b, extra):
                then2, n2 = chain(dve, s["dve2"], PER * b)
                dve.wait_ge(s["k_used"], NCH * b + 4)
                for h in range(2):
                    ins = dve.tensor_scalar(qst[64 * h:64 * h + 64, :, NQ * h:NQ * h + NQ],
                                            qS[64 * h:64 * h + 64, :, ds(NQ * b, NQ)], 1.0, None, ALU.mult)
                ins.then_inc(s["q_staged"], 1)
                dve.wait_ge(s["new_scored"], b + 1)
                dve.wait_ge(s["newT"], b + 1)
                dve.wait_ge(s["turned"], 8 * b + 1)
                dve.tensor_tensor(L[:, PAST:PAST + NS], B[2][:, 0:NS], nb[:, ds(b, 1), :].rearrange("p a t -> p (a t)"),
                                  ALU.add).then_inc(s["new_out"], 1)
                dve.wait_ge(s["new_out"], b + 1)
                dve.tensor_reduce(nmax, L[:, PAST:PAST + NS], AX.X, ALU.max)
                for c in range(NCH):
                    dve.wait_ge(s["k_used"], NCH * b + c + 5)
                    sc = B[c % 2][:, :].rearrange("p (n k) -> p n k", n=2)
                    dve.tensor_reduce(gsum[:, 2 * c:2 * c + 2], sc, AX.X, ALU.add)
                    dve.tensor_tensor(L[:, CH * c:CH * (c + 1)].rearrange("p (n k) -> p n k", n=2), sc, jb, ALU.add)\
                        .then_inc(s["s_out"], 1)
                    dve.wait_ge(s["s_out"], NCH * b + c + 3)
                    ins = dve.tensor_reduce(bmax[:, 2 * c:2 * c + 2], L[:, CH * c:CH * (c + 1)].rearrange("p (n k) -> p n k", n=2),
                                            AX.X, ALU.max)
                    if c < NCH - 1:
                        extra("q", c)
                then2(ins)
                dve.sem_inc(s["settle"], 1)
                then2(dve.max(top8[:, :], gsum[:, :]))
                dve.sem_inc(s["settle"], 1)
                then2(dve.max_index(topi[:, :], top8[:, :], gsum[:, :]))
                then2(dve.tensor_scalar(topf[:, :], topi[:, :], 1.0, None, ALU.mult))
                io = C["iota"][:, 0:NBLK]
                then2(dve.tensor_scalar(pen[:, :], io, topf[:, 0:1], None, ALU.is_equal))
                then2(dve.scalar_tensor_tensor(pen[:, :], io, topf[:, 1:2], pen[:, :], ALU.is_equal, ALU.add))
                then2(dve.scalar_tensor_tensor(pen[:, :], io, topf[:, 2:3], pen[:, :], ALU.is_equal, ALU.add))
                then2(dve.tensor_scalar(pen[:, :], pen[:, :], -1.0, -OFF, ALU.add, ALU.mult))
                then2(dve.tensor_tensor(pen[:, :], pen[:, :], C["blockoff"], ALU.add))
                then2(dve.tensor_tensor(bmax[:, :], bmax[:, :], pen[:, :], ALU.add))
                then2(dve.tensor_reduce(gmax_, bmax[:, :], AX.X, ALU.max))
                then2(dve.tensor_scalar(negm, gmax_, nmax, -1.0, ALU.max, ALU.mult))
                assert n2[0] == PER
                dve.tensor_scalar(ebias[:, :], pen[:, :], negm, None, ALU.add).then_inc(s["exp_bias"], 1)
                extra("q", NCH - 1)
                dve.wait_ge(s["probs"], 17 * b + 17)
                dve.tensor_reduce(tot, esum[:, :], AX.X, ALU.add).then_inc(s["dve3"], 1)
                dve.wait_ge(s["dve3"], b + 1)
                dve.wait_ge(s["o_scaled"], b + 1)
                dve.reciprocal(rinv, tot).then_inc(s["rinv_ready"], 1)
                for c in range(NCH):
                    extra("v", c)
                extra("e", 0)

            for b in range(4):
                dve_batch(b, lambda kind, c: None)
                if b == 1:
                    dve.wait_ge(s["stored"], 7 * 16)
                    for g in range(4):
                        w = 2 << g
                        src = (win1, win2)[g % 2]
                        dve.wait_ge(s["pool"], sum(range(1, g + 2)))
                        start = part[:, 384:400]
                        then(dve.tensor_tensor(start, src[:, HIST:HIST + 16], C["share"][:, 16 * g:16 * g + 16], ALU.mult))
                        then(dve.tensor_tensor(start, start, uX[:, g, HIST:HIST + 16], ALU.subtract))
                        then(dve.scalar_tensor_tensor(uX[:, g, HIST:HIST + NP], src[:, HIST:HIST + NP], 1.0 / w,
                                                      uX[:, g, HIST:HIST + NP], ALU.mult, ALU.subtract))
                        then(dve.tensor_copy(uX[:, g, HIST:HIST + 16], start))
                        sw = src[:, HIST + NP:UW].rearrange("p (b t) -> p b t", b=NB)
                        dve.scalar_tensor_tensor(uxs[:, g, :, HIST:US], sw[:, :, HIST:US], 1.0 / w,
                                                 uxs[:, g, :, HIST:US], ALU.mult, ALU.subtract).then_inc(s["pooled"], 1)
            head_norms(2, 10)
            with dve.Fori(4, NB) as b:
                def p_scale(n, e):
                    h, i = steps[e]
                    dve.wait_ge(s["p_exp"], n + e + 1)
                    dve.reciprocal(pst[:, 4 + h:5 + h], pst[:, 2 + h:3 + h]).then_inc(s["p_out"], 1)
                    dve.wait_ge(s["p_out"], n + e + 1)
                    dve.tensor_scalar(plog[h][:, 0:128 * (i + 1)], plog[h][:, 0:128 * (i + 1)], pst[:, 4 + h:5 + h], None,
                                      ALU.mult).then_inc(s["p_prob"], 1)

                def prompt_step(kind, c):
                    if (kind, c) not in p_at:
                        return
                    e = p_at[kind, c]
                    n = 8 * (b - 4)
                    if e:
                        p_scale(n, e - 1)
                    if e < 8:
                        h, i = steps[e]
                        w = 128 * (i + 1)
                        dve.wait_ge(s["p_scores"], n + e + 1)
                        if e > 1:
                            dve.wait_ge(s["p_turned"], n + e - 1)
                        dve.scalar_tensor_tensor(plog[h][:, 0:w], C["causal"][:, NP - w:NP], pslope[:, h:h + 1], B[5][:, 0:w],
                                                 ALU.mult, ALU.add).then_inc(s["p_logits"], 1)
                        dve.wait_ge(s["p_logits"], n + e + 2)
                        dve.tensor_reduce(pst[:, h:h + 1], plog[h][:, 0:w], AX.X, ALU.max, negate=True).then_inc(s["p_neg"], 1)
                    else:
                        dve.wait_ge(s["mixP"], b - 4 + 2)
                        dve.tensor_scalar(mP[:, ds(b, 1), :].rearrange("p a t -> p (a t)"), B[7][:, :], 1.0, None, ALU.mult)\
                            .then_inc(s["p_stored"], 1)
                dve_batch(b, prompt_step)
            dve.wait_ge(s["x_back"], 64)
            for m in range(KT):
                dve.wait_ge(s["mixP"], 5 + m + 1)
                dve.scalar_tensor_tensor(xP[:, m, :], B[m % 2][:, :], modT[:, 2 * KT + m, 0:1], xP[:, m, :], ALU.mult, ALU.add)\
                    .then_inc(s["res1"], 1)
                dve.wait_ge(s["mixS"], m + 1)
                if m:
                    dve.wait_ge(s["res1"], 2 * m)
                then(dve.tensor_tensor(part[:, 0:NS].rearrange("p (b q) -> p b q", b=NB),
                                       B[2 + m % 2][:, 0:NS].rearrange("p (b q) -> p b q", b=NB),
                                       modT[:, 2 * KT + m, 1:NSEQ].unsqueeze(2).to_broadcast([128, NB, NQ]), ALU.mult))
                dve.tensor_tensor(xS[:, m, :], xS[:, m, :], part[:, 0:NS], ALU.add).then_inc(s["res1"], 1)
            dve.memset(B[6][:, :], 0.0).then_inc(s["bank_cleared"], 1)
            dve.wait_ge(s["rooted2"], 1)
            then(dve.reciprocal(rstd, rstd))
            norm_scale(dve, then, s["h_scaled2"], g2, 4, 3)

            dve.wait_ge(s["stored"], 9 * 16)
            then(dve.memset(lg8, OFF))
            dve.wait_ge(s["route_scores"], 1)
            then(dve.tensor_tensor(lg, B[6][:, 0:TT * 36].rearrange("p (t n) -> p t n", t=TT),
                                   brt[:, :].unsqueeze(1).to_broadcast([128, TT, 36]), ALU.add))
            then(dve.tensor_copy(lg8[:, :, 0:4], lg[:, :, 0:4]))
            for t in range(TT):
                then(dve.max(gtop[:, t, :], lg8[:, t, :]))
                then(dve.max_index(gidx[:, t, :], gtop[:, t, :], lg8[:, t, :]))
            then(dve.tensor_copy(gif, gidx[:, :, 0]))
            dve.tensor_tensor(gexp, lg[:, :, 0:4], gtop[:, :, 0:1].to_broadcast([128, TT, 4]), ALU.subtract)\
                .then_inc(s["g_exp_in"], 1)
            then(dve.tensor_tensor(goh, C["iota"][:, 0:4].unsqueeze(1).to_broadcast([128, TT, 4]),
                                   gif.unsqueeze(2).to_broadcast([128, TT, 4]), ALU.is_equal))
            g4 = gtmp.rearrange("p (t g e) -> p t g e", t=TT, g=4)
            then(dve.tensor_tensor(g4, lg[:, :, 4:36].rearrange("p t (g e) -> p t g e", g=4),
                                   goh.unsqueeze(3).to_broadcast([128, TT, 4, 8]), ALU.mult))
            then(dve.tensor_reduce(ein, g4.rearrange("p t g e -> p t e g"), AX.X, ALU.add))
            for t in range(TT):
                then(dve.max(etop[:, t, :], ein[:, t, :]))
                then(dve.max_index(eidx[:, t, :], etop[:, t, :], ein[:, t, :]))
            dve.tensor_tensor(edif, etop[:, :, 1], etop[:, :, 0], ALU.subtract).then_inc(s["g_exp_in"], 1)
            ek2 = ek.rearrange("p (t k) -> p t k", k=2)
            then(dve.tensor_copy(ek2, eidx[:, :, 0:2]))
            then(dve.scalar_tensor_tensor(ek2, gif.unsqueeze(2).to_broadcast([128, TT, 2]), 8.0, ek2, ALU.mult, ALU.add))
            hotv = hot.rearrange("p (x e) -> p x e", e=32)
            then(dve.tensor_tensor(hotv, C["iota"][:, 0:NE].unsqueeze(1).to_broadcast([128, 2 * TT, 32]),
                                   ek.unsqueeze(2).to_broadcast([128, 2 * TT, 32]), ALU.is_equal))
            h4 = hot.rearrange("p (t k e) -> p t k e", t=TT, k=2)
            then(dve.tensor_tensor(hotm, h4[:, :, 0, :], h4[:, :, 1, :], ALU.add))
            then(dve.tensor_tensor(hotm, hotm, C["valid"].unsqueeze(2).to_broadcast([128, TT, 32]), ALU.mult))
            dve.sem_inc(s["hot"], 1)
            dve.wait_ge(s["g_exp"], 1)
            then(dve.tensor_reduce(gw, gexp, AX.X, ALU.add))
            dve.wait_ge(s["g_exp"], 2)
            then(dve.scalar_tensor_tensor(eden, eex, 1.0, gw, ALU.add, ALU.mult))
            then(dve.reciprocal(wts[:, 0, :], eden))
            then(dve.tensor_tensor(wts[:, 1, :], wts[:, 0, :], eex, ALU.mult))
            dve.wait_ge(s["ranked"], 1)
            then(dve.tensor_copy(cum, B[7][:, 0:(TT + 1) * 32].rearrange("p (t e) -> p t e", t=TT + 1)))
            NTH = 9
            ovv = ovt[:, 0:32 * NTH].rearrange("p (e i) -> p e i", i=NTH)
            then(dve.tensor_tensor(ovv, cum[:, TT, :].unsqueeze(2).to_broadcast([128, 32, NTH]),
                                   C["thr"][:, 0:NTH].unsqueeze(1).to_broadcast([128, 32, NTH]), ALU.is_gt))
            then(dve.tensor_reduce(over, ovv, AX.X, ALU.add))
            then(dve.tensor_tensor_scan(incl, ones[:, 0:32], over, 0.0, ALU.mult, ALU.add))
            then(dve.tensor_tensor(base2, incl, over, ALU.subtract))
            then(dve.tensor_scalar(base2, base2, float(NE - 1), None, ALU.add))
            pr = prod.rearrange("p (t k e) -> p t k e", t=TT, k=2)
            then(dve.tensor_tensor(pr, h4, cum[:, 0:TT, :].unsqueeze(2).to_broadcast([128, TT, 2, 32]), ALU.mult))
            prv = prod.rearrange("p (x e) -> p x e", e=32)
            then(dve.tensor_reduce(pos, prv, AX.X, ALU.add))
            then(dve.tensor_tensor(prv, hotv, base2.unsqueeze(1).to_broadcast([128, 2 * TT, 32]), ALU.mult))
            then(dve.tensor_reduce(ost, prv, AX.X, ALU.add))
            pv8 = past.rearrange("p (x i) -> p x i", i=8)
            then(dve.tensor_tensor(pv8, pos.unsqueeze(2).to_broadcast([128, 2 * TT, 8]),
                                   C["thr"][:, 0:8].unsqueeze(1).to_broadcast([128, 2 * TT, 8]), ALU.is_ge))
            then(dve.tensor_reduce(bno, pv8, AX.X, ALU.add))
            then(dve.scalar_tensor_tensor(pos, bno, -float(RB), pos, ALU.mult, ALU.add))
            then(dve.tensor_scalar(far, bno, 1.0, None, ALU.is_ge))
            then(dve.tensor_tensor(ost, ost, bno, ALU.add))
            then(dve.tensor_tensor(ost, ost, ek, ALU.subtract))
            then(dve.tensor_tensor(ost, ost, far, ALU.mult))
            then(dve.tensor_tensor(blk_, ost, ek, ALU.add))
            nv = ovt[0:1, 0:NOV * 32].rearrange("p (o e) -> p o e", e=32)
            then(dve.tensor_tensor(nv, C["ovid"][0:1, :].unsqueeze(2).to_broadcast([1, NOV, 32]),
                                   incl[0:1, :].unsqueeze(1).to_broadcast([1, NOV, 32]), ALU.is_ge))
            then(dve.tensor_reduce(oveif[0:1, :], nv, AX.X, ALU.add))
            then(dve.tensor_scalar(oveif[0:1, :], oveif[0:1, :], float(NE - 1), None, ALU.min))
            then(dve.tensor_scalar(ovt[0:1, 0:NOV // 2], C["two"][0:1, 0:NOV // 2], incl[0:1, 31:32], None, ALU.is_lt))
            then(dve.tensor_reduce(npf[0:1, 1:2], ovt[0:1, 0:NOV // 2], AX.X, ALU.add))
            then(dve.tensor_scalar(nint[0:1, 0:1], npf[0:1, 1:2], float(NE // 2), None, ALU.add))
            then(dve.tensor_copy(nint[0:1, 1:3], C["iota"][0:1, NE - 2:NE]))
            then(dve.tensor_copy(nint[0:1, 3:3 + NOV], oveif[0:1, :]))
            then(dve.tensor_tensor(rows, C["iota"].unsqueeze(1).unsqueeze(1).to_broadcast([128, 2 * TT, 2, RB]),
                                   pos.unsqueeze(2).unsqueeze(2).to_broadcast([128, 2 * TT, 2, RB]), ALU.is_equal))
            then(dve.tensor_tensor(blks[:, :, 0, :], C["iota"][:, 0:MAXBLK].unsqueeze(1).to_broadcast([128, 2 * TT, MAXBLK]),
                                   blk_.unsqueeze(2).to_broadcast([128, 2 * TT, MAXBLK]), ALU.is_equal))
            b0 = blks[:, :, 0, :].rearrange("p (t k) b -> p t k b", k=2)
            then(dve.tensor_tensor(b0, b0, C["valid"].unsqueeze(2).unsqueeze(3).to_broadcast([128, TT, 2, MAXBLK]), ALU.mult))
            pay = C["payload"].rearrange("p (x c) -> p x c", c=2)
            for c in range(2):
                ins = dve.tensor_tensor(blks[:, :, 1 + c, :], blks[:, :, 0, :],
                                        pay[:, :, c:c + 1].to_broadcast([128, 2 * TT, MAXBLK]), ALU.mult)
                ins.then_inc(s["listed"], 1)
            dve.wait_ge(s["lists_summed"], 1)
            dve.wait_ge(s["zeroed"], 4)
            ls = B[5][:, 0:3 * MAXBLK].rearrange("p (c b) -> p c b", c=3)
            free = ovt[:, 0:MAXBLK]
            then(dve.tensor_scalar(free, ls[:, 0, :], -1.0, 1.0, ALU.mult, ALU.add))
            then(dve.scalar_tensor_tensor(free, free, C["dump"], ls[:, 2, :], ALU.mult, ALU.add))
            then(dve.tensor_scalar(tblS[:, 0, 0:MAXBLK], ls[:, 1, :], C["half"], None, ALU.add))
            then(dve.tensor_scalar(tblS[:, 1, 0:MAXBLK], free, C["half"], None, ALU.add))
            dve.sem_inc(s["n_ready"], 1)

            n_pair = dve.value_load(nint[0:1, 0:1], min_val=NE // 2, max_val=MAXBLK // 2)
            for p in range(2):
                dve.tensor_copy(gix[p][:, :], tblS[:, 0, p:p + 1]).then_inc(s["g_staged"], 1)
            with dve.Fori(0, n_pair) as i:
                for p in range(2):
                    dve.wait_ge(gathered[p], 16 * i + 16)
                    dve.tensor_scalar(gix[p][:, :], tblS[:, 0, ds(2 * i + (2 + p), 1)], 0, None, ALU.add).then_inc(s["g_staged"], 1)
                    dve.wait_ge(y_scat[p], 16 * i + 16)
                    dve.tensor_scalar(six[p][:, :], tblS[:, 1, ds(2 * i + p, 1)], 0, None, ALU.add).then_inc(s["s_staged"], 1)
                    dve.wait_ge(s["silu_ready"], 2 * i + p + 1)
                    dve.tensor_tensor(aa[p], gs[p], B[2][:, 0:256], ALU.mult).then_inc(s["act_ready"], 1)
                    dve.wait_ge(s["down"], 2 * i + p + 1)
                    dve.tensor_copy(Yo[p], B[4 + p][:, :]).then_inc(s["y_out"], 1)
            for t in range(TT):
                r = min(128, NT - 128 * t)
                dve.wait_ge(s["y_back"], 32 * (t + 1))
                if t >= 2:
                    dve.wait_ge(s["c_turned"], 2 * t - 2)
                then(dve.tensor_scalar(yc[t % 2][0:r, :], yb[t % 2][0][0:r, :], wts[0:r, 0, t:t + 1], None, ALU.mult))
                dve.scalar_tensor_tensor(yc[t % 2][0:r, :], yb[t % 2][1][0:r, :], wts[0:r, 1, t:t + 1], yc[t % 2][0:r, :],
                                         ALU.mult, ALU.add).then_inc(s["combined"], 1)
                for k in range(KT):
                    if k % 4 == 0:
                        dve.wait_ge(s["c_turned"], 2 * t + k // 4 + 1)
                    src = B[k // 4][:, (k % 4) * 128:(k % 4) * 128 + r]
                    if t < TT - 1:
                        x = xP[:, k, 128 * t:128 * t + 128]
                        dve.scalar_tensor_tensor(x, src, modT[:, 5 * KT + k, 0:1], x, ALU.mult, ALU.add)\
                            .then_inc(s["final"], 1)
                    else:
                        then(dve.tensor_tensor(part[:, 0:NS].rearrange("p (b q) -> p b q", b=NB),
                                               src.rearrange("p (b q) -> p b q", b=NB),
                                               modT[:, 5 * KT + k, 1:NSEQ].unsqueeze(2).to_broadcast([128, NB, NQ]), ALU.mult))
                        dve.tensor_tensor(xS[:, k, :], xS[:, k, :], part[:, 0:NS], ALU.add).then_inc(s["final"], 1)
                        dve.wait_ge(s["final"], t * KT + k + 1)

        @block.tensor
        def _(pe):
            pe.sem_inc(s["ada_part"], 4)
            pe.sem_inc(s["ada_done"], 2)
            pe.sem_inc(s["s_out"], 2)
            pe.sem_inc(s["turned"], 1)
            pe.sem_inc(s["turned_out"], 1)
            pe.sem_inc(s["newT"], 1)
            pe.sem_inc(s["o_sum"], 1)
            pe.sem_inc(s["o_scaled"], 1)
            pe.sem_inc(s["oT_out"], 1)
            pe.sem_inc(s["mixP"], 1)
            pe.sem_inc(s["p_stored"], 1)
            pe.sem_inc(s["p_logits"], 1)
            pe.sem_inc(s["p_turned_out"], 1)
            pe.sem_inc(s["y_out"], 2)
            pe.wait_ge(s["zeroed"], 4)
            pe.wait_ge(s["silu"], 1)
            norm_pe(pe, s["squared"], s["sums"])
            with pe.Fori(0, 3) as it:
                def columns(u):
                    pe.wait_ge(s["ada_copied"], 4 * it + u + 1)
                    pe.wait_ge(s["ada_done"], 4 * it + u + 1)
                    for c in range(4):
                        last = pe.matmul(B[2 + u % 2][:, NSEQ * c:NSEQ * (c + 1)], (part[:, :], part2)[u % 2][:, 128 * c:128 * c + 128],
                                         C["sel"], start=True, stop=True)
                    last.then_inc(s["ada_cols"], 1)
                for u in range(4):
                    pe.wait_ge(w_full[u], 16 * it + 16)
                    for k in range(KT):
                        j = k % 4
                        last = pe.matmul(B[u % 2][32 * j:32 * j + 32, :], scT[:, k, :], slot[u][:, k, :], start=k < 4, stop=k >= 4)
                    last.then_inc(s["ada_part"], 1)
                    if u:
                        columns(u - 1)
                columns(3)
            pe.wait_ge(s["h_scaled"], 1)
            for T in range(13):
                n, m = divmod(T, 4)
                if m == 0:
                    pe.wait_ge(w_full[n], 16 * 4)
                if T >= 2:
                    pe.wait_ge(s["zS_out"], T - 1)
                for k in range(KT):
                    if n < 3:
                        last = pe.matmul(B[5 + T % 2][:, 0:NS], slot[n][:, k, 128 * m:128 * m + 128], hS[:, k, :],
                                         start=k == 0, stop=k == KT - 1)
                    else:
                        last = pe.matmul(B[5 + T % 2][0:NS, :], hS[:, k, :], slot[n][:, k, :], start=k == 0, stop=k == KT - 1)
                last.then_inc(s["zS"], 1)
            pe.wait_ge(s["zS_out"], 13)

            def head_sums(first, last):
                for i in range(first, last):
                    w = pieces[i][0].shape[1]
                    pe.wait_ge(s["hsq"], i + 1)
                    if i >= 2:
                        pe.wait_ge(s["hroot"], i - 1)
                    pe.matmul(hbank[i % 2][:, 0:w], C["heads"], hsq[i % 2][:, 0:w], start=True, stop=True).then_inc(s["hsum"], 1)
            head_sums(0, 2)
            pe.wait_ge(s["hroot"], 2)

            def pe_batch(b, extra):
                pe.wait_ge(s["q_staged"], b + 1)
                pe.wait_ge(s["oT_out"], 2 * b + 1)
                for j in range(4):
                    last = pe.matmul(B[2][32 * j:32 * j + 32, 0:NS], qst[:, j, :], kS[:, j, :], start=True, stop=True)
                last.then_inc(s["new_scored"], 1)
                for c in range(NCH):
                    pe.wait_ge(k_full[c % 4], 16 * PPC * (2 * b + c // 4 + 1))
                    pe.wait_ge(s["s_out"], NCH * b + c + 1)
                    for j in range(4):
                        last = pe.matmul(B[c % 2][32 * j:32 * j + 32, :], qst[:, j, :], kslot[c % 4][:, :, j, :],
                                         start=True, stop=True)
                    last.then_inc(s["k_used"], 1)
                    extra("q", c)

                def values(t):
                    for j in range(4):
                        rhs = vslot[t // 4][:, t % 4, 128 * j:128 * j + 128] if t < 32 else vS[:, 128 * j:128 * j + 128]
                        last = pe.matmul(B[4][32 * j:32 * j + 16, 0:128], PT[:, t, 16 * j:16 * j + 16], rhs,
                                         start=t == 0, stop=t == 32)
                    return last

                def chunk_values(g):
                    if g == 0:
                        pe.wait_ge(s["o_scaled"], b + 1)
                    pe.wait_ge(s["turned_out"], 8 * b + g + 2)
                    pe.wait_ge(v_full[g], 16 * PPC * (b + 1))
                    for t in range(4 * g, 4 * g + 4):
                        last = values(t)
                    last.then_inc(s["v_used"], 1)
                    extra("v", g)
                for g in range(8):
                    pe.wait_ge(s["probs"], 17 * b + 2 * g + 2)
                    pe.wait_ge(s["turned_out"], 8 * b + g + 1)
                    for t in range(4):
                        a = (4 * g + t) * 128
                        last = pe.transpose(B[3][:, 128 * t:128 * t + 128], L[:, a:a + 128], C["ident"])
                    last.then_inc(s["turned"], 1)
                    if g:
                        chunk_values(g - 1)
                pe.wait_ge(s["probs"], 17 * b + 17)
                pe.transpose(B[2][:, 128:256], L[:, PAST:PAST + 128], C["ident"]).then_inc(s["newT"], 1)
                chunk_values(7)
                pe.wait_ge(s["newT_out"], b + 1)
                values(32).then_inc(s["o_sum"], 1)
                extra("e", 0)
                pe.wait_ge(s["o_scaled"], b + 2)
                pe.transpose(B[2][:, 256:384], On, C["ident"]).then_inc(s["oT"], 1)

            pe.wait_ge(s["h_ready"], KT)
            for b in range(4):
                def tiles(kind, c):
                    for m in z_at.get((kind, c), ()):
                        if m == 0:
                            pe.wait_ge(s["w2_full"], 16 * (b + 1))
                            if b:
                                pe.wait_ge(s["zP_out"], 4 * b)
                        if m == 3:
                            pe.wait_ge(s["zP_out"], 4 * b + 1)
                        for k in range(KT):
                            if b < 3:
                                last = pe.matmul(zbank[m][:, :], w2[:, k, 128 * m:128 * m + 128], hP[:, k, :],
                                                 start=k == 0, stop=k == KT - 1)
                            else:
                                last = pe.matmul(zbank[m][:, :], hP[:, k, 128 * m:128 * m + 128], w2[:, k, :],
                                                 start=k == 0, stop=k == KT - 1)
                        last.then_inc(s["zP"], 1)
                pe_batch(b, tiles)
            pe.wait_ge(s["pooled"], 4)
            pe.wait_ge(s["zP_out"], 16)
            pe.wait_ge(s["wpool_in"], 16)
            for g in range(4):
                if g >= 2:
                    pe.wait_ge(s["ypool_out"], g - 1)
                pe.matmul(B[5 + g % 2][:, :], wpool[:, g, :], uX[:, g, HIST:HIST + NP], start=True, stop=True)
                pe.matmul(B[g % 2][:, 0:NS], wpool[:, g, :], uxs[:, g, :, HIST:US], start=True, stop=True)\
                    .then_inc(s["ypool"], 1)
            pe.wait_ge(s["ypool_out"], 4)
            head_sums(2, 10)
            pe.wait_ge(s["hroot"], 10)
            with pe.Fori(4, NB) as b:
                def p_turn(n, e):
                    h, i = steps[e]
                    pe.wait_ge(s["p_prob"], n + e + 1)
                    pe.wait_ge(s["p_turned_out"], n + e + 1)
                    for t in range(i + 1):
                        last = pe.transpose(B[6][:, 128 * t:128 * t + 128], plog[h][:, 128 * t:128 * t + 128], C["ident"])
                    last.then_inc(s["p_turned"], 1)

                def prompt_step(kind, c):
                    if (kind, c) not in p_at:
                        return
                    e = p_at[kind, c]
                    n = 8 * (b - 4)
                    if e:
                        p_turn(n, e - 1)
                    else:
                        pe.wait_ge(s["staged"], 4 * (b - 4) + 4)
                    if e < 8:
                        h, i = steps[e]
                        pe.wait_ge(s["p_logits"], n + e + 1)
                        pe.matmul(B[5][:, 0:128 * (i + 1)], pq[64 * h:64 * h + 64, 128 * i:128 * i + 128],
                                  pk[64 * h:64 * h + 64, 0:128 * (i + 1)], start=True, stop=True).then_inc(s["p_scores"], 1)
                    else:
                        pe.wait_ge(s["p_turned_out"], n + 9)
                        pe.wait_ge(s["p_stored"], b - 4 + 1)
                        for t in range(4):
                            for h in range(2):
                                last = pe.matmul(B[7][64 * h:64 * h + 64, 128 * t:NP], pv[:, t, 64 * h:64 * h + 64],
                                                 pPT[h][:, t, 128 * t:NP], start=t == 0, stop=t == 3)
                        last.then_inc(s["mixP"], 1)
                pe_batch(b, prompt_step)
            pe.wait_ge(s["oT_out"], 1 + 2 * NB)
            pe.wait_ge(s["p_stored"], 5)
            for m in range(KT):
                if m % 4 == 0:
                    pe.wait_ge(s[f"wo_full{m // 4}"], 16)
                if m >= 2:
                    pe.wait_ge(s["res1"], 2 * (m - 1))
                for k in range(KT):
                    w = slot[m // 4][:, k, 128 * (m % 4):128 * (m % 4) + 128]
                    a = pe.matmul(B[m % 2][:, :], w, mP[:, k, :], start=k == 0, stop=k == KT - 1)
                    b_ = pe.matmul(B[2 + m % 2][:, 0:NS], w, mS[:, k, :], start=k == 0, stop=k == KT - 1)
                a.then_inc(s["mixP"], 1)
                b_.then_inc(s["mixS"], 1)
            norm_pe(pe, s["squared2"], s["sums2"])
            pe.wait_ge(s["h2_ready"], KT)
            pe.wait_ge(s["h_scaled2"], 1)
            pe.wait_ge(s["bank_cleared"], 1)

            def tok(k, t):
                return hP[:, k, 128 * t:128 * t + 128] if t < 4 else hS[:, k, :]
            for t in range(TT):
                r = min(128, NT - 128 * t)
                for k in range(KT):
                    last = pe.matmul(B[6][0:r, 36 * t:36 * t + 36], tok(k, t), wrt[:, k, :], start=k == 0, stop=k == KT - 1)
            last.then_inc(s["route_scores"], 1)
            for t in range(2 * TT):
                r = min(128, NT - 128 * (t // 2))
                if t >= 2:
                    pe.wait_ge(s["h2_out"], t - 1)
                for k in range(4):
                    last = pe.transpose(B[t % 2][0:r, 128 * k:128 * k + 128], tok(4 * (t % 2) + k, t // 2), C["ident"])
                last.then_inc(s["h2_turn"], 1)
            pe.wait_ge(s["hot"], 1)
            for t in range(TT):
                for a in range(t + 1):
                    pe.matmul(B[7][:, 32 * t:32 * t + 32], C["before"] if a == t else ones[:, :], hotm[:, a, :],
                              start=a == 0, stop=a == t)
            for a in range(TT):
                last = pe.matmul(B[7][:, 32 * TT:32 * TT + 32], ones[:, :], hotm[:, a, :], start=a == 0, stop=a == TT - 1)
            last.then_inc(s["ranked"], 1)
            pe.wait_ge(s["listed"], 2)
            for x in range(2 * TT):
                last = pe.matmul(B[5][:, 0:3 * MAXBLK], rows[:, x, :, :].rearrange("p h r -> p (h r)"),
                                 blks[:, x, :, :].rearrange("p c b -> p (c b)"), start=x == 0, stop=x == 2 * TT - 1)
            last.then_inc(s["lists_summed"], 1)
            pe.wait_ge(s["n_ready"], 1)
            n_pair = pe.value_load(nint[0:1, 0:1], min_val=NE // 2, max_val=MAXBLK // 2)
            with pe.Fori(0, n_pair) as i:
                for p in range(2):
                    pe.wait_ge(gathered[p], 16 * i + 16)
                    for c in range(4):
                        last = pe.transpose(B[0][:, 128 * c:128 * c + 128], Xg[p][:, 128 * c:128 * c + 128], C["ident"])
                    last.then_inc(s["x_turned"], 1)
                    xv = XT[p].rearrange("q (c h r) -> q c h r", c=4, h=2)
                    pe.wait_ge(s["xT_ready"], 2 * i + p + 1)
                    for w in range(2):
                        pe.wait_ge(e_full[p][w], 16 * i + 16)
                        wv = eslot[p][w].rearrange("q (k n) -> q k n", k=KT)
                        for k in range(KT):
                            h, c = divmod(k, 4)
                            for f in range(2):
                                last = pe.matmul(B[1 + w][64 * f:64 * f + 64, 0:256], xv[:, c, h, :],
                                                 wv[:, k, 256 * f:256 * f + 256], start=k == 0, stop=k == KT - 1)
                    last.then_inc(s["gate_up"], 1)
                    pe.wait_ge(s["act_ready"], 2 * i + p + 1)
                    for c in range(2):
                        last = pe.transpose(B[3][:, 128 * c:128 * c + 128], aa[p][:, 128 * c:128 * c + 128], C["ident"])
                    last.then_inc(s["a_turned"], 1)
                    pe.wait_ge(s["aT_ready"], 2 * i + p + 1)
                    pe.wait_ge(e_full[p][2], 16 * i + 16)
                    pe.wait_ge(s["y_out"], 2 * i + p + 1)
                    av = aT[p].rearrange("q (c f r) -> q c f r", c=2, f=2)
                    wv = eslot[p][2].rearrange("q (k n) -> q k n", k=FF // 128)
                    for k in range(FF // 128):
                        f, c = divmod(k, 2)
                        for h in range(2):
                            last = pe.matmul(B[4 + p][64 * h:64 * h + 64, :], av[:, c, f, :], wv[:, k, 512 * h:512 * h + 512],
                                             start=k == 0, stop=k == FF // 128 - 1)
                    last.then_inc(s["down"], 1)
            for t in range(TT):
                r = min(128, NT - 128 * t)
                pe.wait_ge(s["combined"], t + 1)
                if t:
                    pe.wait_ge(s["final"], KT * t)
                for k in range(KT):
                    last = pe.transpose(B[k // 4][:, 128 * (k % 4):128 * (k % 4) + r], yc[t % 2][0:r, 128 * k:128 * k + 128],
                                        C["ident"][0:r, 0:r])
                    if k % 4 == 3:
                        last.then_inc(s["c_turned"], 1)


def constants():
    lay, width = const_layout()
    c = np.zeros((128, width), np.float32)

    def put(name, a):
        at, w = lay[name]
        c[:a.shape[0], at:at + w] = a.reshape(a.shape[0], -1)
    p = np.arange(128)
    put("ident", np.eye(128))
    put("sel", (p[:, None] % 32 == np.arange(NSEQ)[None]) * 1.0)
    put("heads", (p[:, None] // 64 == p[None] // 64) * 1.0)
    put("before", (p[:, None] < p[None]) * 1.0)
    rel = (np.arange(NP) - (NP - 128))[None] - p[:, None]
    put("causal", np.where(rel <= 0, rel, -1e32))
    r = p % 32
    live = r < 2 * NQ
    head = 2 * (p // 32) + r // NQ
    slope = np.where(live, 2.0 ** -(head + 1.0), 0.0)[:, None]
    q = (r % NQ)[:, None]
    put("jbias", slope * np.arange(BLK)[None])
    put("blockoff", slope * (BLK * np.arange(NBLK)[None] - PAST - q))
    sb_, si = np.arange(NS) // NQ, np.arange(NS) % NQ
    ok = (sb_[None, None] == np.arange(NB)[None, :, None]) & (si[None, None] <= q[:, :, None])
    nbias = np.where(ok, slope[:, :, None] * (si[None, None] - q[:, :, None]), OFF)
    put("newbias", np.where(live[:, None, None], nbias, 0.0))
    put("iota", np.tile(np.arange(64), (128, 1)))
    t = np.arange(16)
    put("share", np.tile(np.concatenate([1.0 / np.minimum(t + 1, 2 << g) for g in range(4)]), (128, 1)))
    tok = 128 * np.arange(TT)[None] + p[:, None]
    put("valid", (tok < NT) * 1.0)
    put("payload", np.stack([np.stack([2 * tok, 2 * (k * NT + tok)], -1) for k in range(2)], 2))
    put("thr", np.tile(RB * (np.arange(16) + 1), (128, 1)))
    put("slopes", np.tile(2.0 ** -(np.arange(NH) + 1.0), (128, 1)))
    put("eps", np.full((128, 1), EPS))
    put("two", np.tile(2 * np.arange(16), (128, 1)))
    put("half", p[:, None] // RB)
    put("dump", 2 * (2 * NT + p[:, None] % RB))
    put("ovid", np.tile(np.arange(NOV), (128, 1)))
    return c


def kernel(**inputs):
    import numpy as _np
    import concourse.bacc as _bacc
    from concourse import mybir as _mybir
    from concourse.bass_utils import run_bass_kernel_spmd as _run

    a = {k: _np.asarray(v) for k, v in inputs.items()}
    cc = _np.ascontiguousarray
    cols = lambda v: v.reshape(-1, 128).T
    x = _np.concatenate([a["x_prompt"].reshape(NP, D), a["x_sample"].reshape(NS, D)])
    c9 = _np.concatenate([a["c_prompt"], a["c_sample"]])
    nph = a["cache_k"].shape[1]
    gq, gk = (_np.concatenate([a[n][0], a[n][0]])[:, None] for n in ("g_q", "g_k"))
    arr = {
        "xT": cc(x.T), "cT": cc(c9.T), "consts": constants(), "pages": a["page_table"].reshape(1, -1),
        "b_ada": cc(_np.broadcast_to(cols(a["b_ada"][0])[:, :, None], (128, 6 * KT, NSEQ))),
        "gcols": cc(_np.concatenate([cols(a["g_attn_norm"][0]), cols(a["g_ffn_norm"][0]), gq, gk, cols(a["pool_scale"][0])], 1)),
        "w_ada": a["w_ada"][0], "w_in": a["w_in"][0], "w_out": a["w_out"][0], "w_pool": a["w_pool"][0],
        "histT": cc(a["state_pool"][0].transpose(2, 0, 1)),
        "kT": cc(a["cache_k"][0].reshape(nph, PAGE, 4, 128).transpose(0, 3, 2, 1)),
        "v": a["cache_v"][0].reshape(nph, PAGE, AW),
        "w_route": cc(_np.concatenate([a["w_group"][0], a["w_expert"][0]], 1)),
        "b_route": cc(_np.broadcast_to(_np.concatenate([a["b_group"][0], a["b_expert"][0]])[None], (128, 36))),
        "w_gate": a["w_gate"][0], "w_up": a["w_up"][0], "w_down": a["w_down"][0],
    }
    outs = {"yT": (D, NT), "kT": (AW, NT), "v": (NT, AW), "poolT": (PW, NSEQ, HIST)}
    nc = _bacc.Bacc("TRN2", target_bir_lowering=False, num_devices=1)
    d = {n: nc.dram_tensor(f"in_{n}", v.shape, _mybir.dt.from_np(v.dtype), kind="ExternalInput").ap() for n, v in arr.items()}
    o = {n: nc.dram_tensor(f"out_{n}", sh, _mybir.dt.float32, kind="ExternalOutput").ap() for n, sh in outs.items()}
    build_kernel(nc, d, o)
    r = _run(nc, [{f"in_{n}": cc(v) for n, v in arr.items()}], core_ids=[0]).results[0]
    y, k, v, pl = (_np.asarray(r[f"out_{n}"]) for n in ("yT", "kT", "v", "poolT"))
    y, k, pl = y.T, k.T, pl.transpose(1, 2, 0)
    return (cc(y[:NP]).reshape(1, NP, D), cc(y[NP:]).reshape(NB, NQ, D),
            cc(k[:NP]).reshape(1, 1, NP, NH, HD), cc(v[:NP]).reshape(1, 1, NP, NH, HD), cc(pl[:1]).reshape(1, 1, HIST, PW),
            cc(k[NP:]).reshape(1, NB, NQ, NH, HD), cc(v[NP:]).reshape(1, NB, NQ, NH, HD), cc(pl[1:]).reshape(1, NB, HIST, PW))
```

```python
import concourse.bass as bass
from concourse import mybir
from contextlib import ExitStack
import numpy as np

D = 1024
NP, NB, NQ = 512, 8, 8
NS = NB * NQ
NT = NP + NS
KT = D // 128
NSEQ = 1 + NB
PW, AW, HD, NH = 512, 512, 64, 8
HIST = 15
PAST, PAGE, BLK, TOPK = 4096, 128, 256, 3
NBLK = PAST // BLK
CH = 512
NCH = PAST // CH
PPC = CH // PAGE
NE, FF = 32, 512
RB = 64
MAXBLK = NE + 2 * NT // RB
NOV = MAXBLK - NE
TT = (NT + 127) // 128
EPS = 1e-6
OFF = -1e30
U = 4096
US = HIST + NQ
UW = HIST + NP + NB * US


def const_layout():
    at, out = 0, {}
    for name, width in (("ident", 128), ("sel", NSEQ), ("heads", 128), ("before", 128), ("causal", NP),
                        ("jbias", BLK), ("blockoff", NBLK), ("newbias", NB * NS), ("iota", 64),
                        ("share", 4 * 16), ("valid", TT), ("payload", TT * 4), ("thr", 16),
                        ("slopes", NH), ("eps", 1), ("two", 16), ("ovid", NOV), ("half", 1), ("dump", 1)):
        out[name] = (at, width)
        at += width
    return out, at


def build_kernel(nc, d, o):
    f32, i32, u32 = mybir.dt.float32, mybir.dt.int32, mybir.dt.uint32
    ALU, ACT, AX = mybir.AluOpType, mybir.ActivationFunctionType, mybir.AxisListType
    ds = bass.ds
    ctx = ExitStack()
    with ctx:
        def sb(name, shape, dt=f32):
            return ctx.enter_context(nc.sbuf_tensor(name, shape, dt))

        def sem(name):
            return ctx.enter_context(nc.semaphore(name))

        ring = sb("ring", [128, 6 * U])
        wbuf = sb("wbuf", [128, U])
        xP = wbuf[:, :].rearrange("p (k t) -> p k t", k=KT)
        uxr = sb("uxr", [128, 4 * UW])
        uX = uxr[:, :].rearrange("p (g t) -> p g t", g=4)
        rstd = uxr[:, 0:NT]
        xS = uxr[:, NT:NT + KT * NS].rearrange("p (k t) -> p k t", k=KT)
        hP, hS = sb("hP", [128, KT, NP]), sb("hS", [128, KT, NS])
        mP, mS = hP, hS
        qP, kP = sb("qP", [128, 4, NP]), sb("kP", [128, 4, NP])
        vP = sb("vP", [128, NP // 128, AW])
        qS, kS = sb("qS", [128, 4, NS]), sb("kS", [128, 4, NS])
        vS = sb("vS", [128, AW])
        modT = sb("modT", [128, 6 * KT, NSEQ])
        big = sb("big", [128, PAST + 128 + 33 * 64])
        L = big[:, 0:PAST + 128]
        PT = big[:, PAST + 128:PAST + 128 + 33 * 64].rearrange("p (t c) -> p t c", c=64)
        unused = [big[:, PAST + 128 + BLK * i:PAST + 128 + BLK * (i + 1)] for i in range(8)]
        sq = big[:, 0:KT * NT].rearrange("p (k t) -> p k t", t=NT)
        CL, CW = const_layout()
        cst = sb("cst", [128, CW])
        C = {n: cst[:, a:a + w] for n, (a, w) in CL.items()}
        ones = sb("ones", [128, 128])
        cT = ring[:, 4 * U + 512:4 * U + 512 + KT * NSEQ].rearrange("p (k s) -> p k s", s=NSEQ)
        scT = qS[:, :, :].rearrange("p j t -> p (j t)").rearrange("p (k c) -> p k c", k=KT)
        part = sb("part", [128, 512])
        coef = part[:, 256:256 + KT * NSEQ].rearrange("p (k s) -> p k s", s=NSEQ)
        gcols = sb("gcols", [128, 2 * KT + 2 + 4])
        g1, g2 = gcols[:, 0:KT], gcols[:, KT:2 * KT]
        gq, gk = gcols[:, 2 * KT:2 * KT + 1], gcols[:, 2 * KT + 1:2 * KT + 2]
        pscale = gcols[:, 2 * KT + 2:2 * KT + 6]
        pages = sb("pages", [1, NB * PAST // PAGE], i32)
        gsum, bmax, pen, ebias = (sb(n, [128, NBLK]) for n in ("gsum", "bmax", "pen", "ebias"))
        top8, topf = sb("top8", [128, 8]), sb("topf", [128, 8])
        topi = sb("topi", [128, 8], u32)
        st = sb("st", [128, 8])
        nmax, gmax_, negm, tot, rinv = (st[:, i:i + 1] for i in range(5))
        esum = sb("esum", [128, NBLK + 1])
        On = part[:, 0:128]
        qst = part[:, 128:256].rearrange("p (j c) -> p j c", j=4)
        wrt = uxr[:, 1536:1536 + KT * 64].rearrange("p (k n) -> p k n", k=KT)
        brt = uxr[:, 2048:2084]
        zr, halves = uxr[:, 2176:2176 + NT], uxr[:, 2176 + NT:2212 + NT]

        bT = ring[:, 5 * U:5 * U + 6 * KT * NSEQ].rearrange("p (c s) -> p c s", s=NSEQ)
        wpool = hP[:, 4, :].rearrange("p (g n) -> p g n", g=4)
        win1, win2 = (vP[:, :, :].rearrange("p a b -> p (a b)")[:, i * UW:(i + 1) * UW] for i in range(2))
        part2 = big[:, 5 * 1024:5 * 1024 + 512]
        zoS = big[:, 9 * 512:10 * 512]
        addS = [big[:, (20 + i) * 256:(21 + i) * 256] for i in range(2)]
        spread = big[:, 22 * 256:22 * 256 + TT * 128]
        rms2 = st[:, 0:TT]
        zst = [big[:, i * 512:(i + 1) * 512] for i in range(2)]

        B = [ctx.enter_context(nc.psum_tensor(f"bank{i}", [128, 512], f32)) for i in range(8)]

        h2d = nc.dram_tensor("h2d", (2 * NT, 512), f32, kind="Internal").ap()
        y2 = nc.dram_tensor("y2", (2 * (2 * NT + RB), 512), f32, kind="Internal").ap()

        s = {n: sem(n) for n in (
            "small", "x_in", "late_in", "wpool_in", "zeroed", "silu", "ada_part", "ada_copied", "ada_cols",
            "ada_done", "squared", "sums", "rooted", "h_scaled", "h_ready", "zP", "zS", "zS_copied", "zS_turned", "zP_out", "zS_out",
            "hsq", "hsum", "hroot", "normed", "pooled", "ypool", "ypool_out",
            "q_staged", "new_scored", "new_out", "k_used", "s_out", "g_summed", "exp_bias", "probs", "turned", "turned_out",
            "newT", "newT_out", "v_used", "o_sum", "rinv_ready", "o_scaled", "oT", "oT_out", "w2_full", "x_back",
            "staged", "p_scores", "p_logits", "p_neg", "p_exp", "p_prob", "p_turned", "p_turned_out", "p_out", "p_stored",
            "wo_full0", "wo_full1", "mixP", "mixS", "mixS_copied", "mixS_turned", "res1", "res1S", "squared2",
            "sq_summed", "sums2", "rooted2", "rms_spread", "rms_out", "h_scaled2", "h2_ready", "h2_turn",
            "h2_out", "h2_stored", "route_parts", "route_copied", "route_scores", "g_exp_in", "g_exp", "hot", "ranked", "listed", "lists_summed",
            "listed_rows", "list_staged", "x_turned", "xT_ready", "gate_done", "gate_up", "count_ready", "silu_ready", "act_ready", "a_turned",
            "aT_ready", "down", "y_out", "weighted", "combined", "c_turned", "final", "stored",
            "dve", "choice", "sum_ready", "pool", "settle")}
        w_full = [sem(f"w_full{i}") for i in range(4)]
        k_full = [sem(f"k_full{i}") for i in range(4)]
        v_full = [sem(f"v_full{i}") for i in range(8)]
        gathered = [sem(f"gathered{i}") for i in range(2)]
        y_back = [sem(f"y_back{i}") for i in range(TT)]
        y_scat = [sem(f"y_scattered{i}") for i in range(2)]
        e_full = [[sem(f"e_full{p}{i}") for i in range(3)] for p in range(2)]

        slot = [ring[:, i * U:(i + 1) * U].rearrange("p (k n) -> p k n", k=KT) for i in range(6)]
        kslot = [ring[:, i * 2048:(i + 1) * 2048].rearrange("p (g j s) -> p g j s", g=PPC, j=4) for i in range(4)]
        vslot = [ring[:, 2 * U + i * 2048:2 * U + (i + 1) * 2048].rearrange("p (g n) -> p g n", g=PPC)
                 for i in range(8)]
        eslot = [[ring[:, ((3 - 3 * p) + i) * U:((3 - 3 * p) + i + 1) * U] for i in range(3)] for p in range(2)]

        def chain(eng, sm, start=0):
            n = [0]

            def then(ins):
                n[0] += 1
                ins.then_inc(sm, 1)
                eng.wait_ge(sm, start + n[0])
            return then, n

        pq, pk = uxr[:, 0:512], uxr[:, 512:1024]
        pv = uxr[:, 1024:1536].rearrange("p (t n) -> p t n", t=4)
        plog = [uxr[:, 1536 + 512 * i:2048 + 512 * i] for i in range(2)]
        pslope, pst = uxr[:, 2560:2562], uxr[:, 2564:2572]
        pPT = [wbuf[:, 2048 * i:2048 * (i + 1)].rearrange("p (t q) -> p t q", t=4) for i in range(2)]
        w2 = wbuf[:, :].rearrange("p (k n) -> p k n", k=KT)

        h2tok = big[:, 0:TT * D].rearrange("p (t n) -> p t n", t=TT)
        rs = qP[:, :, :].rearrange("p a b -> p (a b)")
        ri = kP[:, :, :].rearrange("p a b -> p (a b)")
        at = [0]

        def cut(n):
            a = at[0]
            at[0] += n
            assert at[0] <= 2048
            return rs[:, a:a + n]
        lg = cut(TT * 36).rearrange("p (t n) -> p t n", t=TT)
        lg8 = cut(TT * 8).rearrange("p (t n) -> p t n", t=TT)
        gtop = cut(TT * 8).rearrange("p (t n) -> p t n", t=TT)
        etop = cut(TT * 8).rearrange("p (t n) -> p t n", t=TT)
        ein = cut(TT * 8).rearrange("p (t n) -> p t n", t=TT)
        gif = cut(TT)
        gexp = cut(TT * 4).rearrange("p (t n) -> p t n", t=TT)
        gw = cut(TT)
        goh = cut(TT * 4).rearrange("p (t n) -> p t n", t=TT)
        gtmp = cut(TT * 32)
        edif = cut(TT)
        eex = cut(TT)
        eden = cut(TT)
        wts = sb("wts", [128, 2, TT])
        ek = cut(TT * 2)
        hot = cut(TT * 2 * 32)
        hotm = cut(TT * 32).rearrange("p (t e) -> p t e", t=TT)
        cum = cut((TT + 1) * 32).rearrange("p (t e) -> p t e", t=TT + 1)
        cnt = vP[:, 3, 256:256 + (TT + 1) * 32].rearrange("p (t e) -> p t e", t=TT + 1)
        over, incl, base2 = cut(32), cut(32), cut(32)
        pos, ost, bno, far, blk_ = (cut(TT * 2) for _ in range(5))
        ovt = ri[:, 0:NOV * 32]
        ovn = hP[:, 0:2, :].rearrange("p k t -> p (k t)")[:, 0:NOV * 32]
        prod = ri[:, 576:576 + TT * 2 * 32]
        past = ri[:, 1400:1400 + TT * 2 * 8]
        ti = ri[:, 1024:1024 + 300].bitcast(u32)
        gidx = ti[:, 0:TT * 8].rearrange("p (t n) -> p t n", t=TT)
        eidx = ti[:, 40:40 + TT * 8].rearrange("p (t n) -> p t n", t=TT)
        oveif = cut(NOV)
        npf = cut(2)
        nint = sb("nint", [1, 3 + NOV], i32)
        rows = vP[:, :, :].rearrange("p a b -> p (a b)")[:, 0:2 * TT * 128].rearrange("p (x h r) -> p x h r", h=2, r=RB)
        blks = ri[:, 0:2 * TT * 3 * MAXBLK].rearrange("p (x c b) -> p x c b", c=3, b=MAXBLK)
        first = sb("first", [1, 4])
        tblS = sb("tblS", [128, 2, MAXBLK + 3], u32)

        o_ = [0]

        def mo(n):
            a = o_[0]
            o_[0] += n
            assert o_[0] <= PAST + 128 + 33 * 64
            return big[:, a:a + n]
        Xg = [mo(512) for _ in range(2)]
        XT = [mo(512) for _ in range(2)]
        gs = [mo(256) for _ in range(2)]
        aa = [mo(256) for _ in range(2)]
        aT = [mo(256) for _ in range(2)]
        Yo = [mo(512) for _ in range(2)]
        gix = [sb(f"gix{i}", [128, 1], u32) for i in range(2)]
        six = [sb(f"six{i}", [128, 1], u32) for i in range(2)]
        yb = [[ring[:, (2 * i + j) * 1024:(2 * i + j + 1) * 1024] for j in range(2)] for i in range(TT)]
        yc = [ring[:, (2 * TT + i) * 1024:(2 * TT + 1 + i) * 1024] for i in range(2)]

        def sp_pages(ap):
            return nc.values_load_multi_w_load_instructions(
                ap, engines=(mybir.EngineType.SP,), min_val=0, max_val=d["v"].shape[0] - 1,
                skip_runtime_bounds_check_because="a page table names pages of the pool")[1]

        block = ctx.enter_context(nc.Block())

        @block.sync
        def _(sp):
            sp.sem_inc(s["k_used"], 4)
            sp.sem_inc(s["v_used"], 8)
            sp.dma_start(cT, d["cT"].rearrange("(k p) s -> p k s", p=128)).then_inc(s["small"], 16)
            sp.dma_start(cst[:, :], d["consts"]).then_inc(s["small"], 16)
            sp.dma_start(bT, d["b_ada"]).then_inc(s["small"], 16)
            sp.dma_start(gcols[:, :], d["gcols"]).then_inc(s["small"], 16)
            sp.dma_start(pages[:, :], d["pages"]).then_inc(s["small"], 16)
            xT = d["xT"].rearrange("(k p) t -> p k t", p=128)
            sp.dma_start(xP[:, :, :], xT[:, :, 0:NP]).then_inc(s["x_in"], 16)
            sp.dma_start(xS[:, :, :], xT[:, :, NP:NT]).then_inc(s["x_in"], 16)
            w_ada = d["w_ada"].rearrange("(k p) n -> p k n", p=128)
            with sp.Fori(0, 3) as it:
                for u in range(4):
                    sp.wait_ge(s["ada_part"], 4 * it + u + 1)
                    sp.dma_start(slot[u], w_ada[:, :, ds((4 * it + u) * 512, 512)]).then_inc(w_full[u], 16)
            w_in = d["w_in"].rearrange("(k p) n -> p k n", p=128)
            for u in range(4):
                sp.wait_ge(s["ada_part"], 4 + 9 + u)
                sp.dma_start(slot[u], w_in[:, :, u * 512:(u + 1) * 512]).then_inc(w_full[u], 16)
            sp.wait_ge(s["small"], 80)

            def batch_loads(b, unit):
                def chunk_pages(c):
                    return sp_pages(pages[0:1, ds(PPC * NCH * b + PPC * c, PPC)])
                for c in range(NCH):
                    at_ = chunk_pages(c)
                    if unit == 0 and c == 0:
                        sp.wait_ge(s["zS"], 1)
                    sp.wait_ge(s["k_used"], NCH * b + c + 1)
                    for g, pg in enumerate(at_):
                        sp.dma_start(kslot[c % 4][:, g, :, :], d["kT"][ds(pg, 1), :, :, :].rearrange("a p j s -> (a p) j s"))\
                            .then_inc(k_full[c % 4], 16)
                    if unit is not None and c == 3:
                        if unit == 0:
                            sp.wait_ge(s["h_scaled"], 1 + KT)
                        else:
                            sp.wait_ge(s["zP"], 4 * unit)
                        sp.dma_start(w2, w_in[:, :, unit * 512:(unit + 1) * 512]).then_inc(s["w2_full"], 16)
                for c in range(NCH):
                    at_ = chunk_pages(c)
                    if unit == 0 and c == 0:
                        sp.wait_ge(s["zS"], 2)
                    sp.wait_ge(s["v_used"], NCH * b + c + 1)
                    for g, pg in enumerate(at_):
                        sp.dma_start(vslot[c][:, g, :], d["v"][ds(pg, 1), :, :].rearrange("a p n -> (a p) n"))\
                            .then_inc(v_full[c], 16)
            for b in range(4):
                batch_loads(b, b)
            with sp.Fori(4, NB) as b:
                batch_loads(b, None)
            w_out = d["w_out"].rearrange("(k p) n -> p k n", p=128)
            sp.wait_ge(s["k_used"], 4 + NB * NCH)
            for u in range(2):
                sp.dma_start(slot[u], w_out[:, :, u * 512:(u + 1) * 512]).then_inc(s[f"wo_full{u}"], 16)
            sp.wait_ge(s["mixP"], 1 + 4)
            sp.wait_ge(s["p_stored"], 1 + 4)
            sp.dma_start(xP[:, :, :], xT[:, :, 0:NP]).then_inc(s["x_back"], 16)
            sp.dma_start(xS[:, :, :], xT[:, :, NP:NT]).then_inc(s["x_back"], 16)
            sp.dma_start(wrt, d["w_route"].rearrange("(k p) n -> p k n", p=128)).then_inc(s["x_back"], 16)
            sp.dma_start(brt, d["b_route"]).then_inc(s["x_back"], 16)
            wg = d["w_gate"].rearrange("e (k p) n -> e p k n", p=128)
            wu = d["w_up"].rearrange("e (k p) n -> e p k n", p=128)
            wd = d["w_down"].rearrange("e (k p) n -> e p k n", p=128)

            def load_expert(e, p, blk=None):
                for i, (w, k) in enumerate(((wg, KT), (wu, KT), (wd, FF // 128))):
                    if blk is not None:
                        sp.wait_ge(s[("gate_done", "gate_up", "down")[i]], blk + 1)
                    sp.dma_start(eslot[p][i].rearrange("q (k n) -> q k n", k=k),
                                 w[ds(e, 1), :, :, :].rearrange("a q k n -> (a q) k n")).then_inc(e_full[p][i], 16)
            sp.wait_ge(s["v_used"], 8 + NB * NCH)
            load_expert(0, 0)
            sp.wait_ge(s["mixP"], 1 + 4 + KT)
            sp.wait_ge(s["mixS"], 1)
            load_expert(1, 1)
            with sp.Fori(1, NE // 2 - 1) as i:
                for p in range(2):
                    load_expert(2 * i + p, p, 2 * i + p - 2)
            sp.wait_ge(s["count_ready"], 1)
            n_pair = sp.value_load(nint[0:1, 0:1], min_val=NE // 2, max_val=MAXBLK // 2)
            with sp.Fori(0, n_pair - (NE // 2 - 1)) as i:
                for p in range(2):
                    e = sp.value_load(nint[0:1, ds(1 + 2 * i + p, 1)], min_val=0, max_val=NE - 1)
                    load_expert(e, p, 2 * i + (NE + p - 4))
            for p in range(2):
                sp.wait_ge(y_scat[p], 16 * n_pair + 16)
            for p in range(2):
                sp.sem_inc(s["settle"], 1)
                sp.wait_ge(gathered[p], 16 * n_pair + 16 * (2 - p))
            for t in range(TT):
                r = min(128, NT - 128 * t)
                for k in range(2):
                    a = 2 * (k * NT + 128 * t)
                    sp.dma_start(yb[t][k][0:r, :], y2[a:a + 2 * r, :].rearrange("(p h) n -> p (h n)", h=2))\
                        .then_inc(y_back[t], 16)
            yT = o["yT"].rearrange("(k p) t -> p k t", p=128)
            for t in range(TT - 1):
                sp.wait_ge(s["final"], KT * (t + 1))
                sp.dma_start(yT[:, :, 128 * t:128 * t + 128], xP[:, :, 128 * t:128 * t + 128]).then_inc(s["stored"], 16)
            sp.wait_ge(s["final"], KT * (TT - 1) + 2)
            sp.dma_start(yT[:, :, NP:NT], xS[:, :, :]).then_inc(s["stored"], 16)
            sp.wait_ge(s["stored"], (9 + TT) * 16)

        @block.gpsimd
        def _(pool):
            pool.memset(ones[:, :], 1.0).then_inc(s["zeroed"], 1)
            pool.wait_ge(s["zeroed"], 1)
            pool.memset(scT[:, :, :], 0.0).then_inc(s["zeroed"], 1)
            pool.wait_ge(s["zeroed"], 2)
            pool.memset(vS[64:128, :], 0.0).then_inc(s["zeroed"], 1)
            pool.wait_ge(s["zeroed"], 3)
            pool.memset(tblS[:, :, :], 0).then_inc(s["zeroed"], 1)
            pool.wait_ge(s["zeroed"], 4)
            pool.wait_ge(s["h_scaled"], 1 + KT)
            pool.memset(uX[:, :, 0:HIST], 0.0).then_inc(s["zeroed"], 1)
            pool.wait_ge(s["zeroed"], 5)
            then, n = chain(pool, s["pool"])
            pool.wait_ge(s["late_in"], 4 * 16)
            pool.wait_ge(s["normed"], 2)
            pool.wait_ge(s["zP_out"], 4)
            pool.wait_ge(s["zS_out"], 4)
            for g in range(4):
                src = uX[:, g, :]
                for a in range(g + 1):
                    k = 1 << a
                    dst = (win1, win2)[a % 2]
                    lo = 2 * k - 1
                    if a == 0 and g:
                        pool.wait_ge(s["pooled"], g)
                    then(pool.tensor_tensor(dst[:, lo:UW], src[:, lo:UW], src[:, lo - k:UW - k], ALU.add))
                    src = dst
            pool.wait_ge(s["normed"], 10)
            pool.wait_ge(s["zP_out"], 16)
            pool.wait_ge(s["ypool"], 4)
            with pool.Fori(0, 4) as j:
                pool.wait_ge(s["p_logits"], 8 * j + 1)
                pool.sem_inc(s["settle"], 1)
                for k, (dst, src) in enumerate(((pslope, C["slopes"][:, ds(2 * j, 2)]),
                                                (pq, qP[:, ds(j, 1), :].rearrange("p a n -> p (a n)")),
                                                (pk, kP[:, ds(j, 1), :].rearrange("p a n -> p (a n)")),
                                                (pv, vP[:, :, ds(128 * j, 128)]))):
                    if k == 3:
                        pool.wait_ge(s["mixP"], j + 1)
                        pool.sem_inc(s["settle"], 1)
                    pool.tensor_copy(dst, src).then_inc(s["staged"], 1)
                    pool.wait_ge(s["staged"], 4 * j + k + 1)
                    pool.sem_inc(s["settle"], 1)
            pool.wait_ge(s["count_ready"], 1)
            n_pair = pool.value_load(nint[0:1, 0:1], min_val=NE // 2, max_val=MAXBLK // 2)
            pool.wait_ge(s["h2_stored"], 16 * TT)

            def gather(p):
                pool.indirect_dma_start(Xg[p], None, h2d, bass.IndirectOffsetOnAxis(gix[p][:, :], 0)).then_inc(gathered[p], 16)
            def stage(dst, column, at):
                pool.sem_inc(s["settle"], 1)
                pool.tensor_copy(dst, column).then_inc(s["list_staged"], 1)
                pool.wait_ge(s["list_staged"], at)
            pool.wait_ge(s["listed_rows"], 1)
            for n in range(3):
                if n == 2:
                    pool.wait_ge(s["x_turned"], 1)
                stage(gix[n % 2][:, :], tblS[:, 0, n:n + 1], n + 1)
                gather(n % 2)
            for p in range(2):
                pool.dma_start(first[:, 2 * p:2 * p + 2], d["consts"][p:p + 1, 0:2]).then_inc(y_scat[p], 16)
            with pool.Fori(0, n_pair) as i:
                for p in range(2):
                    q = 1 - p
                    pool.wait_ge(gathered[q], 16 * i + 16 * (p + 1))
                    stage(gix[q][:, :], tblS[:, 0, ds(2 * i + (p + 3), 1)], 4 * i + (2 * p + 4))
                    pool.wait_ge(s["x_turned"], 2 * i + p + 2)
                    pool.sem_inc(s["settle"], 1)
                    gather(q)
                    pool.wait_ge(y_scat[p], 16 * i + 16)
                    stage(six[p][:, :], tblS[:, 1, ds(2 * i + p, 1)], 4 * i + (2 * p + 5))
                    pool.wait_ge(s["y_out"], 2 * i + p + 3)
                    pool.wait_ge(y_scat[1 - p], 16 * i + 16 * (p + 1))
                    pool.sem_inc(s["settle"], 1)
                    pool.indirect_dma_start(y2, bass.IndirectOffsetOnAxis(six[p][:, :], 0), Yo[p], None)\
                        .then_inc(y_scat[p], 16)

        def norm_roots(act, sq_s, sum_s, root_s):
            for k in range(KT):
                act.activation(sq[:, k, 0:NP], xP[:, k, :], ACT.Square)
                act.activation(sq[:, k, NP:NT], xS[:, k, :], ACT.Square).then_inc(sq_s, 1)
            act.wait_ge(sum_s, 2)
            act.activation(rstd[:, 0:NP], B[4][:, :], ACT.Sqrt, scale=1.0 / D, bias=C["eps"])
            act.activation(rstd[:, NP:NT], B[5][:, 0:NS], ACT.Sqrt, scale=1.0 / D, bias=C["eps"]).then_inc(root_s, 1)

        def norm_shift(act, scaled_s, ready_s, shift):
            for k in range(KT):
                act.wait_ge(scaled_s, k + 2)
                act.activation(hP[:, k, :], hP[:, k, :], ACT.Identity, bias=modT[:, shift * KT + k, 0:1])\
                    .then_inc(ready_s, 1)

        def norm_pe(pe, sq_s, sum_s):
            for k in range(KT):
                pe.wait_ge(sq_s, k + 1)
                p_ = pe.matmul(B[4][:, :], ones[:, :], sq[:, k, 0:NP], start=k == 0, stop=k == KT - 1)
                s_ = pe.matmul(B[5][:, 0:NS], ones[:, :], sq[:, k, NP:NT], start=k == 0, stop=k == KT - 1)
            p_.then_inc(sum_s, 1)
            s_.then_inc(sum_s, 1)

        def norm_coef(dve, then, g, scale):
            then(dve.scalar_tensor_tensor(coef, modT[:, scale * KT:(scale + 1) * KT, :], 1.0,
                                          g.unsqueeze(2).to_broadcast([128, KT, NSEQ]), ALU.add, ALU.mult))

        def norm_scale(dve, then, scaled_s, rP, rS, shift):
            h4_ = hS[:, :, :].rearrange("p k (b q) -> p k b q", b=NB)
            then(dve.tensor_tensor(h4_, xS.rearrange("p k (b q) -> p k b q", b=NB),
                                   coef[:, :, 1:NSEQ].unsqueeze(3).to_broadcast([128, KT, NB, NQ]), ALU.mult))
            then(dve.tensor_tensor(hS[:, :, :], hS[:, :, :], rS.unsqueeze(1).to_broadcast([128, KT, NS]), ALU.mult))
            dve.tensor_tensor(h4_, h4_, modT[:, shift * KT:(shift + 1) * KT, 1:NSEQ].unsqueeze(3)
                              .to_broadcast([128, KT, NB, NQ]), ALU.add).then_inc(scaled_s, 1)
            for k in range(KT):
                dve.scalar_tensor_tensor(hP[:, k, :], xP[:, k, :], coef[:, k, 0:1], rP,
                                         ALU.mult, ALU.mult).then_inc(scaled_s, 1)

        uxs = uX[:, :, HIST + NP:UW].rearrange("p g (b t) -> p g b t", b=NB)
        pieces = [(qS[:, :, :].rearrange("p j t -> p (j t)"), 0), (kS[:, :, :].rearrange("p j t -> p (j t)"), 1)]
        pieces += [(qP[:, m, :], 0) for m in range(4)] + [(kP[:, m, :], 1) for m in range(4)]
        hsq, hrt = ([(kP if 2 <= i < 6 else vP)[:, i % 2 + a, :] for i in range(10)] for a in (0, 2))
        square_at = {(n, "v", c): 4 * n - 2 + i for n in (1, 2) for i, c in enumerate((0, 1, 3, 4))}
        sum_at = {(n + (i > 2), k_, c): 4 * n - 2 + i for n in (1, 2)
                  for i, (k_, c) in enumerate((("v", 1), ("v", 2), ("v", 4), ("q", 0)))}
        root_at = {(n + (i > 0), k_, c): 4 * n - 2 + i for n in (1, 2)
                   for i, (k_, c) in enumerate((("v", 2), ("q", 0), ("q", 1), ("q", 3)))}
        hbank = [B[3]] * 2 + [B[5], B[6], B[7], B[3]] * 2
        pool_at = {("q", 2): 0, ("q", 6): 1, ("v", 0): 2, ("v", 4): 3}
        steps = [(h, i) for i in range(4) for h in range(2)]
        zbank = [B[5], B[6], B[7], B[5]]
        z_at = [{("q", 3): (0,), ("q", 5): (1,), ("q", 6): (2,), ("q", 7): (3,)}] * 2
        z_at += [{("q", 1): (0,), ("q", 3): (1,), ("q", 5): (2,), ("q", 7): (3,)}] * 2
        z_out_at = {("q", 4): (0,), ("q", 6): (1,), ("q", 7): (2,), ("s", 0): (3,)}
        points = [("q", c) for c in range(NCH)] + [("v", c) for c in range(NCH)]
        start_at = [0, 1, 3, 5, 7, 9, 11, 13]
        score_of = {points[x]: e for e, x in enumerate(start_at)}
        scale_of = {points[x + 1]: e for e, x in enumerate(start_at)}
        turn_of = {points[min(x + 3, 15)]: e for e, x in enumerate(start_at)}
        act_points = points[0:7] + [None, ("s", 0)] + points[8:] + [("e", 0)]
        exp_of = {act_points[x + (x >= 7) + (x >= 8)]: e for e, x in enumerate(start_at)}
        turned_of = {act_points[y + (y >= 7) + (y >= 8)]: e for y, e in ((points.index(p_), e) for p_, e in turn_of.items())}

        @block.scalar
        def _(act):
            act.wait_ge(s["small"], 80)
            act.wait_ge(s["zeroed"], 4)
            act.activation(scT[:, :, 0:NSEQ], cT, ACT.Silu).then_inc(s["silu"], 1)
            act.wait_ge(s["x_in"], 32)
            norm_roots(act, s["squared"], s["sums"], s["rooted"])
            with act.Fori(0, 6) as u:
                for i in range(2):
                    act.wait_ge(s["ada_part"], 2 * u + i + 5)
                    act.activation((part[:, :], part2)[i], B[i][:, :], ACT.Copy).then_inc(s["ada_copied"], 1)
            norm_shift(act, s["h_scaled"], s["h_ready"], 0)
            for g in range(4):
                act.dma_start(uxs[:, g, :, 0:HIST], d["histT"][g * 128:(g + 1) * 128, :, :]).then_inc(s["late_in"], 16)

            def head_square(i):
                x = pieces[i][0]
                if i >= 2:
                    act.wait_ge(s["hsum"], i - 1)
                act.activation(hsq[i][:, 0:x.shape[1]], x, ACT.Square).then_inc(s["hsq"], 1)

            def head_root(i):
                w = pieces[i][0].shape[1]
                act.wait_ge(s["hsum"], i + 1)
                if i >= 2:
                    act.wait_ge(s["normed"], i - 1)
                act.activation(hrt[i][:, 0:w], hbank[i][:, 0:w], ACT.Sqrt, scale=1.0 / HD, bias=C["eps"])\
                    .then_inc(s["hroot"], 1)
            act.wait_ge(s["zS_out"], 4)
            head_square(0)
            head_square(1)
            head_root(0)
            head_root(1)
            act.wait_ge(s["normed"], 2)
            act.dma_start(o["kT"].rearrange("(j p) t -> p j t", p=128)[:, :, NP:NT], kS[:, :, :]).then_inc(s["stored"], 16)
            act.dma_start(o["v"][NP:NT, :], vS[0:NS, :]).then_inc(s["stored"], 16)

            def act_batch(b, extra):
                act.wait_ge(s["o_sum"], b + 1)
                for c in range(NCH):
                    act.wait_ge(s["s_out"], NCH * b + c + 3)
                    if c >= 4:
                        act.wait_ge(s["g_summed"], NCH * b + c - 1)
                    for n in range(2):
                        ins = act.activation(unused[2 * (c % 4) + n], B[c % 2][:, BLK * n:BLK * (n + 1)], ACT.Copy,
                                             accum_out=gsum[:, 2 * c + n:2 * c + n + 1])
                    ins.then_inc(s["g_summed"], 1)
                    extra("q", c)
                act.wait_ge(s["exp_bias"], b + 1)

                def turned_out(g):
                    act.wait_ge(s["turned"], 8 * b + g + 2)
                    act.activation(PT[:, 4 * g:4 * g + 4, :].rearrange("p t (j c) -> p (t j) c", j=4),
                                   B[g % 2][:, :].rearrange("p (x c) -> p x c", c=32)[:, :, 0:16],
                                   ACT.Copy).then_inc(s["turned_out"], 1)
                    if g == 0:
                        extra("s", 0)
                    else:
                        extra("v", g - 1)
                for g in range(NCH):
                    for n in range(2 * g, 2 * g + 2):
                        act.activation(L[:, BLK * n:BLK * (n + 1)], L[:, BLK * n:BLK * (n + 1)], ACT.Exp,
                                       bias=ebias[:, n:n + 1], accum_out=esum[:, n:n + 1]).then_inc(s["probs"], 1)
                    if g:
                        if g == NCH - 1:
                            act.activation(L[:, PAST:PAST + NS], L[:, PAST:PAST + NS], ACT.Exp, bias=negm,
                                           accum_out=esum[:, NBLK:NBLK + 1]).then_inc(s["probs"], 1)
                        turned_out(g - 1)
                turned_out(NCH - 1)
                act.wait_ge(s["newT"], b + 2)
                act.activation(PT[:, 32, :].rearrange("p (j c) -> p j c", j=4),
                               B[2][:, 128:256].rearrange("p (x c) -> p x c", c=32)[:, :, 0:16],
                               ACT.Copy).then_inc(s["newT_out"], 1)
                extra("v", 7)
                act.wait_ge(s["o_sum"], b + 2)
                act.wait_ge(s["rinv_ready"], b + 1)
                act.activation(On, B[4][:, 0:128], ACT.Copy, scale=rinv).then_inc(s["o_scaled"], 1)
                extra("e", 0)
                act.wait_ge(s["oT"], b + 1)
                act.sem_inc(s["settle"], 1)
                oT = B[2][:, 256:384].rearrange("p (j c) -> p j c", j=4)
                for h in range(2):
                    act.activation(mS[64 * h:64 * h + 64, 4:8, ds(NQ * b, NQ)],
                                   oT[64 * h:64 * h + 64, :, NQ * h:NQ * h + NQ], ACT.Copy).then_inc(s["oT_out"], 1)

            for b in range(4):
                def tiles_out(kind, c):
                    if (b, kind, c) in root_at:
                        head_root(root_at[b, kind, c])
                    if (b, kind, c) in square_at:
                        if c == 0:
                            act.wait_ge(s["zP_out"], 4 * (b + 1))
                            if b == 2:
                                act.wait_ge(s["pooled"], 4)
                        head_square(square_at[b, kind, c])
                    if b == 3 and kind == "v" and 3 <= c < 7:
                        g = c - 3
                        act.wait_ge(s["ypool"], g + 1)
                        act.activation(mP[:, g, :], B[5 + g % 2][:, :], ACT.Copy, scale=pscale[:, g:g + 1])
                        act.activation(mS[:, g, :], B[7 - 4 * (g % 2)][:, 0:NS], ACT.Copy, scale=pscale[:, g:g + 1])\
                            .then_inc(s["ypool_out"], 1)
                    for m in z_out_at.get((kind, c), ()):
                        act.wait_ge(s["zP"], 4 * b + m + 1)
                        if b >= 2 and m == 0:
                            act.wait_ge(s["normed"], 4 * b - 2)
                        dst = (uX[:, m, HIST:HIST + NP], qP[:, m, :], kP[:, m, :], vP[:, m, :])[b]
                        act.activation(dst, zbank[m][:, :], ACT.Copy).then_inc(s["zP_out"], 1)
                        if b == 3 and m == 3:
                            act.dma_start(wpool, d["w_pool"].rearrange("g p n -> p g n")).then_inc(s["wpool_in"], 16)
                act_batch(b, tiles_out)
                if b == 0:
                    act.wait_ge(s["zP_out"], 4)
                    act.wait_ge(s["zS_out"], 4)
                    act.wait_ge(s["late_in"], 4 * 16)
                    act.dma_start(o["poolT"].rearrange("(g p) b t -> p g b t", p=128)[:, :, 0, :],
                                  uX[:, :, NP:NP + HIST]).then_inc(s["stored"], 16)
                    for g in range(4):
                        act.dma_start(o["poolT"][g * 128:(g + 1) * 128, 1:NSEQ, :], uxs[:, g, :, NQ:US])\
                            .then_inc(s["stored"], 16)
            act.wait_ge(s["zP_out"], 16)
            act.wait_ge(s["normed"], 10)
            act.dma_start(o["kT"].rearrange("(j p) t -> p j t", p=128)[:, :, 0:NP], kP[:, :, :]).then_inc(s["stored"], 16)
            act.dma_start(o["v"][0:NP, :].rearrange("(r p) n -> p r n", p=128), vP[:, :, :]).then_inc(s["stored"], 16)
            with act.Fori(4, NB) as b:
                def prompt_step(kind, c):
                    n = 8 * (b - 4)
                    if (kind, c) in turned_of:
                        e = turned_of[kind, c]
                        h, i = steps[e]
                        act.wait_ge(s["p_turned"], n + e + 1)
                        act.activation(pPT[h][:, 0:i + 1, 128 * i:128 * i + 128],
                                       B[6][:, 0:128 * (i + 1)].rearrange("p (t q) -> p t q", q=128), ACT.Copy)\
                            .then_inc(s["p_turned_out"], 1)
                    if (kind, c) in exp_of:
                        e = exp_of[kind, c]
                        h, i = steps[e]
                        act.wait_ge(s["p_neg"], n + e + 1)
                        act.activation(plog[h][:, 0:128 * (i + 1)], plog[h][:, 0:128 * (i + 1)], ACT.Exp,
                                       bias=pst[:, h:h + 1], accum_out=pst[:, 2 + h:3 + h]).then_inc(s["p_exp"], 1)
                    if kind == "e":
                        act.wait_ge(s["mixP"], b - 4 + 2)
                        act.sem_inc(s["settle"], 1)
                        act.activation(mP[:, ds(b, 1), :].rearrange("p a t -> p (a t)"), B[7][:, :], ACT.Copy)\
                            .then_inc(s["p_stored"], 1)
                act_batch(b, prompt_step)
            for k in range(KT):
                act.wait_ge(s["res1"], k + 1)
                act.activation(sq[:, k, 0:NP], xP[:, k, :], ACT.Square).then_inc(s["squared2"], 1)
                if k == 3:
                    act.wait_ge(s["mixS"], 1)
                    act.activation(zoS, B[2][:, :], ACT.Copy).then_inc(s["mixS_copied"], 1)
                if k == 4:
                    act.wait_ge(s["res1S"], 2)
                    act.activation(sq[:, :, NP:NT], xS, ACT.Square).then_inc(s["squared2"], 1)
            act.wait_ge(s["sums2"], 1)
            act.activation(rms2, B[4][:, 0:TT], ACT.Sqrt, scale=1.0 / D, bias=C["eps"]).then_inc(s["rooted2"], 1)
            norm_shift(act, s["h_scaled2"], s["h2_ready"], 3)
            act.wait_ge(s["route_parts"], 1)
            act.activation(zr[:, 0:NP], B[6][:, :], ACT.Copy)
            act.activation(zr[:, NP:NT], B[7][:, 0:NS], ACT.Copy).then_inc(s["route_copied"], 1)
            for t in range(2 * TT):
                r = min(128, NT - 128 * (t // 2))
                act.wait_ge(s["h2_turn"], t + 1)
                act.activation(h2tok[0:r, t // 2, 512 * (t % 2):512 * (t % 2) + 512], B[t % 2][0:r, :], ACT.Copy)\
                    .then_inc(s["h2_out"], 1)
            for t in range(TT):
                r = min(128, NT - 128 * t)
                act.wait_ge(s["h2_out"], 2 * t + 2)
                act.dma_start(h2d[256 * t:256 * t + 2 * r, :].rearrange("(p h) n -> p (h n)", h=2),
                              h2tok[0:r, t, :]).then_inc(s["h2_stored"], 16)
            act.wait_ge(s["g_exp_in"], 1)
            act.activation(gexp, gexp, ACT.Exp).then_inc(s["g_exp"], 1)
            act.wait_ge(s["g_exp_in"], 2)
            act.activation(eex, edif, ACT.Exp).then_inc(s["g_exp"], 1)
            act.wait_ge(s["count_ready"], 1)
            n_pair = act.value_load(nint[0:1, 0:1], min_val=NE // 2, max_val=MAXBLK // 2)
            act.wait_ge(s["x_turned"], 1)
            act.activation(XT[0], B[0][:, :], ACT.Copy).then_inc(s["xT_ready"], 1)
            with act.Fori(0, n_pair) as i:
                for p in range(2):
                    act.wait_ge(s["gate_up"], 2 * i + p + 1)
                    act.activation(gs[p], B[1][:, 0:256], ACT.Silu).then_inc(s["silu_ready"], 1)
                    act.wait_ge(s["a_turned"], 2 * i + p + 1)
                    act.activation(aT[p], B[3][:, 0:256], ACT.Copy).then_inc(s["aT_ready"], 1)
                    act.wait_ge(s["x_turned"], 2 * i + p + 2)
                    act.activation(XT[1 - p], B[0][:, :], ACT.Copy).then_inc(s["xT_ready"], 1)
            for t in range(TT):
                r = min(128, NT - 128 * t)
                act.wait_ge(y_back[t], 32)
                if t >= 2:
                    act.wait_ge(s["c_turned"], 2 * t - 2)
                act.activation(yc[t % 2][0:r, :], yb[t][0][0:r, :], ACT.Copy, scale=wts[0:r, 0, t:t + 1])\
                    .then_inc(s["weighted"], 1)

        @block.vector
        def _(dve):
            then, n = chain(dve, s["dve"])
            dve.wait_ge(s["small"], 80)
            dve.wait_ge(s["rooted"], 1)
            then(dve.reciprocal(rstd, rstd))
            with dve.Fori(0, 6) as u:
                for i in range(2):
                    dve.wait_ge(s["ada_cols"], 2 * u + i + 1)
                    dve.tensor_tensor(modT[:, ds(8 * u + 4 * i, 4), :],
                                      B[2 + i][:, 0:4 * NSEQ].rearrange("p (c s) -> p c s", s=NSEQ),
                                      bT[:, ds(8 * u + 4 * i, 4), :], ALU.add).then_inc(s["ada_done"], 1)
            dve.wait_ge(s["ada_done"], 14)
            norm_coef(dve, then, g1, 1)
            norm_scale(dve, then, s["h_scaled"], rstd[:, 0:NP], rstd[:, NP:NT], 0)
            dve.wait_ge(s["h_scaled"], 1 + KT)
            for n_ in range(2):
                dve.wait_ge(s["zS"], n_ + 1)
                dve.tensor_copy(zst[n_], B[5 + n_][:, :]).then_inc(s["zS_copied"], 1)
            dve.tensor_copy(vS[0:NS, :], B[6][0:NS, :]).then_inc(s["zS_out"], 1)
            for n_, dst in enumerate((qS, kS)):
                dve.wait_ge(s["zS_turned"], n_ + 1)
                zt = B[n_][:, :].rearrange("p (c h t) -> p c h t", c=4, h=2)
                if n_ == 0:
                    dve.tensor_copy(uxs[:, :, :, HIST:US], zt[:, :, 0, :].rearrange("p c (b q) -> p c b q", b=NB))\
                        .then_inc(s["zS_out"], 1)
                dve.tensor_copy(dst[:, :, :], zt[:, :, 1, :]).then_inc(s["zS_out"], 1)
            then(dve.tensor_scalar(gq, gq, HD ** -0.5, None, ALU.mult))

            def head_norm(i):
                x, which = pieces[i]
                r = hrt[i][:, 0:x.shape[1]]
                dve.wait_ge(s["hroot"], i + 1)
                then(dve.reciprocal(r, r))
                dve.scalar_tensor_tensor(x, x, (gq, gk)[which], r, ALU.mult, ALU.mult).then_inc(s["normed"], 1)
            head_norm(0)
            head_norm(1)
            then(dve.memset(qst, 0.0))
            then(dve.memset(L[:, PAST:PAST + 128], 0.0))
            dve.wait_ge(s["normed"], 2)
            jb = C["jbias"].unsqueeze(1).to_broadcast([128, CH // BLK, BLK])
            PER = 11
            nb = C["newbias"].rearrange("p (b t) -> p b t", b=NB)

            def dve_batch(b, extra):
                then2, n2 = chain(dve, s["choice"], PER * b)
                dve.wait_ge(s["k_used"], NCH * b + 4)
                for h in range(2):
                    ins = dve.tensor_scalar(qst[64 * h:64 * h + 64, :, NQ * h:NQ * h + NQ],
                                            qS[64 * h:64 * h + 64, :, ds(NQ * b, NQ)], 1.0, None, ALU.mult)
                ins.then_inc(s["q_staged"], 1)
                dve.wait_ge(s["new_scored"], b + 1)
                dve.wait_ge(s["newT"], b + 1)
                dve.wait_ge(s["turned"], 8 * b + 1)
                dve.tensor_tensor(L[:, PAST:PAST + NS], B[3][:, 0:NS], nb[:, ds(b, 1), :].rearrange("p a t -> p (a t)"),
                                  ALU.add).then_inc(s["new_out"], 1)
                dve.wait_ge(s["new_out"], b + 1)
                dve.tensor_reduce(nmax, L[:, PAST:PAST + NS], AX.X, ALU.max)
                for c in range(NCH):
                    dve.wait_ge(s["k_used"], NCH * b + c + 5)
                    sc = B[c % 2][:, :].rearrange("p (n k) -> p n k", n=2)
                    dve.tensor_tensor(L[:, CH * c:CH * (c + 1)].rearrange("p (n k) -> p n k", n=2), sc, jb, ALU.add)\
                        .then_inc(s["s_out"], 1)
                    dve.wait_ge(s["s_out"], NCH * b + c + 3)
                    ins = dve.tensor_reduce(bmax[:, 2 * c:2 * c + 2], L[:, CH * c:CH * (c + 1)].rearrange("p (n k) -> p n k", n=2),
                                            AX.X, ALU.max)
                    if c < NCH - 1:
                        extra("q", c)
                dve.wait_ge(s["g_summed"], NCH * b + NCH + 2)
                then2(ins)
                dve.sem_inc(s["settle"], 1)
                then2(dve.max(top8[:, :], gsum[:, :]))
                dve.sem_inc(s["settle"], 1)
                then2(dve.max_index(topi[:, :], top8[:, :], gsum[:, :]))
                then2(dve.tensor_scalar(topf[:, :], topi[:, :], 1.0, None, ALU.mult))
                io = C["iota"][:, 0:NBLK]
                then2(dve.tensor_scalar(pen[:, :], io, topf[:, 0:1], None, ALU.not_equal))
                for x in range(1, TOPK):
                    then2(dve.scalar_tensor_tensor(pen[:, :], io, topf[:, x:x + 1], pen[:, :], ALU.not_equal, ALU.mult))
                then2(dve.scalar_tensor_tensor(pen[:, :], pen[:, :], OFF, C["blockoff"], ALU.mult, ALU.add))
                then2(dve.tensor_tensor(bmax[:, :], bmax[:, :], pen[:, :], ALU.add))
                then2(dve.tensor_reduce(gmax_, bmax[:, :], AX.X, ALU.max))
                then2(dve.tensor_scalar(negm, gmax_, nmax, -1.0, ALU.max, ALU.mult))
                assert n2[0] == PER
                dve.tensor_scalar(ebias[:, :], pen[:, :], negm, None, ALU.add).then_inc(s["exp_bias"], 1)
                extra("q", NCH - 1)
                for c in range(NCH - 2):
                    extra("v", c)
                dve.wait_ge(s["probs"], 17 * b + 17)
                dve.tensor_reduce(tot, esum[:, :], AX.X, ALU.add).then_inc(s["sum_ready"], 1)
                dve.wait_ge(s["sum_ready"], b + 1)
                dve.wait_ge(s["o_scaled"], b + 1)
                dve.reciprocal(rinv, tot).then_inc(s["rinv_ready"], 1)
                for c in range(NCH - 2, NCH):
                    extra("v", c)

            def pooling(g):
                w = 2 << g
                src = (win1, win2)[g % 2]
                dve.wait_ge(s["pool"], sum(range(1, g + 2)))
                start = part[:, 384:400]
                then(dve.tensor_tensor(start, src[:, HIST:HIST + 16], C["share"][:, 16 * g:16 * g + 16], ALU.mult))
                then(dve.tensor_tensor(start, start, uX[:, g, HIST:HIST + 16], ALU.subtract))
                then(dve.scalar_tensor_tensor(uX[:, g, HIST:HIST + NP], src[:, HIST:HIST + NP], 1.0 / w,
                                              uX[:, g, HIST:HIST + NP], ALU.mult, ALU.subtract))
                then(dve.tensor_copy(uX[:, g, HIST:HIST + 16], start))
                sw = src[:, HIST + NP:UW].rearrange("p (b t) -> p b t", b=NB)
                dve.scalar_tensor_tensor(uxs[:, g, :, HIST:US], sw[:, :, HIST:US], 1.0 / w,
                                         uxs[:, g, :, HIST:US], ALU.mult, ALU.subtract).then_inc(s["pooled"], 1)
            for b in range(4):
                def beside(kind, c):
                    if b == 1 and (kind, c) in pool_at:
                        if (kind, c) == ("q", 2):
                            dve.wait_ge(s["stored"], 7 * 16)
                        pooling(pool_at[kind, c])
                    if (b, kind, c) in root_at:
                        head_norm(root_at[b, kind, c])
                dve_batch(b, beside)
            with dve.Fori(4, NB) as b:
                def prompt_step(kind, c):
                    n = 8 * (b - 4)
                    if (kind, c) in scale_of:
                        e = scale_of[kind, c]
                        h, i = steps[e]
                        dve.wait_ge(s["p_exp"], n + e + 1)
                        dve.reciprocal(pst[:, 4 + h:5 + h], pst[:, 2 + h:3 + h]).then_inc(s["p_out"], 1)
                        dve.wait_ge(s["p_out"], n + e + 1)
                        dve.tensor_scalar(plog[h][:, 0:128 * (i + 1)], plog[h][:, 0:128 * (i + 1)], pst[:, 4 + h:5 + h], None,
                                          ALU.mult).then_inc(s["p_prob"], 1)
                    if (kind, c) in score_of:
                        e = score_of[kind, c]
                        h, i = steps[e]
                        w = 128 * (i + 1)
                        dve.wait_ge(s["p_scores"], n + e + 1)
                        if e > 1:
                            dve.wait_ge(s["p_turned"], n + e - 1)
                        dve.scalar_tensor_tensor(plog[h][:, 0:w], C["causal"][:, NP - w:NP], pslope[:, h:h + 1], B[5][:, 0:w],
                                                 ALU.mult, ALU.add).then_inc(s["p_logits"], 1)
                        dve.wait_ge(s["p_logits"], n + e + 2)
                        dve.tensor_reduce(pst[:, h:h + 1], plog[h][:, 0:w], AX.X, ALU.max, negate=True).then_inc(s["p_neg"], 1)
                dve_batch(b, prompt_step)
            dve.wait_ge(s["x_back"], 64)
            then(dve.tensor_tensor(halves, C["ident"][:, 0:36], C["ident"][:, 64:100], ALU.add))

            def sum_squares(k):
                dve.wait_ge(s["squared2"], max(6, k + 2))
                dve.wait_ge(s["sq_summed"], k)
                dve.tensor_tensor(sq[:, 0, :], sq[:, 0, :], sq[:, k, :], ALU.add).then_inc(s["sq_summed"], 1)
            for m in range(KT):
                dve.wait_ge(s["mixP"], 5 + m + 1)
                dve.scalar_tensor_tensor(xP[:, m, :], B[m % 2][:, :], modT[:, 2 * KT + m, 0:1], xP[:, m, :], ALU.mult, ALU.add)\
                    .then_inc(s["res1"], 1)
                if m == 4:
                    dve.wait_ge(s["mixS_turned"], 1)
                    zt = B[3][:, :].rearrange("p (c h b q) -> p c h b q", c=4, h=2, b=NB)
                    for h in range(2):
                        then(dve.tensor_tensor(
                            addS[h].rearrange("p (c b q) -> p c b q", c=4, b=NB), zt[:, :, h, :, :],
                            modT[:, 2 * KT + 4 * h:2 * KT + 4 * h + 4, 1:NSEQ].unsqueeze(3).to_broadcast([128, 4, NB, NQ]), ALU.mult))
                        dve.tensor_tensor(xS[:, 4 * h:4 * h + 4, :], xS[:, 4 * h:4 * h + 4, :],
                                          addS[h].rearrange("p (c t) -> p c t", c=4), ALU.add).then_inc(s["res1S"], 1)
                for k in {5: (1, 2, 3), 6: (4, 5), 7: (6, 7)}.get(m, ()):
                    sum_squares(k)
            norm_coef(dve, then, g2, 4)
            dve.wait_ge(s["rooted2"], 1)
            then(dve.reciprocal(rms2, rms2))
            dve.tensor_tensor(spread.rearrange("p (t n) -> p t n", t=TT), C["ident"].unsqueeze(1).to_broadcast([128, TT, 128]),
                              rms2.unsqueeze(2).to_broadcast([128, TT, 128]), ALU.mult).then_inc(s["rms_spread"], 1)
            dve.wait_ge(s["rms_out"], 1)
            norm_scale(dve, then, s["h_scaled2"], B[5][:, :], B[7][:, 0:NS], 3)

            dve.wait_ge(s["stored"], 9 * 16)
            then(dve.memset(lg8, OFF))
            then(dve.memset(lg, 0.0))
            then(dve.memset(cnt, 0.0))
            dve.wait_ge(s["route_scores"], 1)
            dve.tensor_tensor(lg[:, 0:TT - 1, :], B[4][:, 0:(TT - 1) * 36].rearrange("p (t n) -> p t n", n=36),
                              brt[:, :].unsqueeze(1).to_broadcast([128, TT - 1, 36]), ALU.add)
            then(dve.tensor_tensor(lg[0:NS, TT - 1, :], B[4][0:NS, (TT - 1) * 36:TT * 36], brt[0:NS, :], ALU.add))
            then(dve.tensor_copy(lg8[:, :, 0:4], lg[:, :, 0:4]))
            for t in range(TT):
                ins = dve.max(gtop[:, t, :], lg8[:, t, :])
            then(ins)
            for t in range(TT):
                ins = dve.max_index(gidx[:, t, :], gtop[:, t, :], lg8[:, t, :])
            then(ins)
            then(dve.tensor_copy(gif, gidx[:, :, 0]))
            dve.tensor_tensor(gexp, lg[:, :, 0:4], gtop[:, :, 0:1].to_broadcast([128, TT, 4]), ALU.subtract)\
                .then_inc(s["g_exp_in"], 1)
            then(dve.tensor_tensor(goh, C["iota"][:, 0:4].unsqueeze(1).to_broadcast([128, TT, 4]),
                                   gif.unsqueeze(2).to_broadcast([128, TT, 4]), ALU.is_equal))
            g4 = gtmp.rearrange("p (t g e) -> p t g e", t=TT, g=4)
            then(dve.tensor_tensor(g4, lg[:, :, 4:36].rearrange("p t (g e) -> p t g e", g=4),
                                   goh.unsqueeze(3).to_broadcast([128, TT, 4, 8]), ALU.mult))
            then(dve.tensor_reduce(ein, g4.rearrange("p t g e -> p t e g"), AX.X, ALU.add))
            for t in range(TT):
                ins = dve.max(etop[:, t, :], ein[:, t, :])
            then(ins)
            for t in range(TT):
                ins = dve.max_index(eidx[:, t, :], etop[:, t, :], ein[:, t, :])
            then(ins)
            dve.tensor_tensor(edif, etop[:, :, 1], etop[:, :, 0], ALU.subtract).then_inc(s["g_exp_in"], 1)
            ek2 = ek.rearrange("p (t k) -> p t k", k=2)
            then(dve.tensor_copy(ek2, eidx[:, :, 0:2]))
            then(dve.scalar_tensor_tensor(ek2, gif.unsqueeze(2).to_broadcast([128, TT, 2]), 8.0, ek2, ALU.mult, ALU.add))
            hotv = hot.rearrange("p (x e) -> p x e", e=32)
            then(dve.tensor_tensor(hotv, C["iota"][:, 0:NE].unsqueeze(1).to_broadcast([128, 2 * TT, 32]),
                                   ek.unsqueeze(2).to_broadcast([128, 2 * TT, 32]), ALU.is_equal))
            h4 = hot.rearrange("p (t k e) -> p t k e", t=TT, k=2)
            then(dve.tensor_tensor(hotm, h4[:, :, 0, :], h4[:, :, 1, :], ALU.add))
            then(dve.tensor_tensor(hotm, hotm, C["valid"].unsqueeze(2).to_broadcast([128, TT, 32]), ALU.mult))
            for t in range(TT):
                then(dve.tensor_tensor(cnt[:, t + 1, :], cnt[:, t, :], hotm[:, t, :], ALU.add))
            dve.sem_inc(s["hot"], 1)
            dve.wait_ge(s["ranked"], 1)
            then(dve.tensor_copy(cum, B[7][:, 0:(TT + 1) * 32].rearrange("p (t e) -> p t e", t=TT + 1)))
            NTH = 9
            ovv = ovt[:, 0:32 * NTH].rearrange("p (e i) -> p e i", i=NTH)
            then(dve.tensor_tensor(ovv, cum[:, TT, :].unsqueeze(2).to_broadcast([128, 32, NTH]),
                                   C["thr"][:, 0:NTH].unsqueeze(1).to_broadcast([128, 32, NTH]), ALU.is_gt))
            then(dve.tensor_reduce(over, ovv, AX.X, ALU.add))
            then(dve.tensor_tensor_scan(incl, ones[:, 0:32], over, 0.0, ALU.mult, ALU.add))
            then(dve.tensor_tensor(base2, incl, over, ALU.subtract))
            then(dve.tensor_scalar(base2, base2, float(NE - 1), None, ALU.add))
            pr = prod.rearrange("p (t k e) -> p t k e", t=TT, k=2)
            then(dve.tensor_tensor(pr, h4, cum[:, 0:TT, :].unsqueeze(2).to_broadcast([128, TT, 2, 32]), ALU.mult))
            prv = prod.rearrange("p (x e) -> p x e", e=32)
            then(dve.tensor_reduce(pos, prv, AX.X, ALU.add))
            then(dve.tensor_tensor(prv, hotv, base2.unsqueeze(1).to_broadcast([128, 2 * TT, 32]), ALU.mult))
            then(dve.tensor_reduce(ost, prv, AX.X, ALU.add))
            pv8 = past.rearrange("p (x i) -> p x i", i=8)
            then(dve.tensor_tensor(pv8, pos.unsqueeze(2).to_broadcast([128, 2 * TT, 8]),
                                   C["thr"][:, 0:8].unsqueeze(1).to_broadcast([128, 2 * TT, 8]), ALU.is_ge))
            then(dve.tensor_reduce(bno, pv8, AX.X, ALU.add))
            then(dve.scalar_tensor_tensor(pos, bno, -float(RB), pos, ALU.mult, ALU.add))
            then(dve.tensor_scalar(far, bno, 1.0, None, ALU.is_ge))
            then(dve.tensor_tensor(ost, ost, bno, ALU.add))
            then(dve.tensor_tensor(ost, ost, ek, ALU.subtract))
            then(dve.tensor_tensor(ost, ost, far, ALU.mult))
            then(dve.tensor_tensor(blk_, ost, ek, ALU.add))
            blk2 = blk_.rearrange("p (t k) -> p t k", k=2)
            then(dve.scalar_tensor_tensor(blk2, blk2, 1.0, C["valid"].unsqueeze(2).to_broadcast([128, TT, 2]), ALU.add, ALU.mult))
            then(dve.tensor_tensor(rows, C["iota"].unsqueeze(1).unsqueeze(1).to_broadcast([128, 2 * TT, 2, RB]),
                                   pos.unsqueeze(2).unsqueeze(2).to_broadcast([128, 2 * TT, 2, RB]), ALU.is_equal))
            then(dve.tensor_tensor(blks[:, :, 0, :], C["iota"][:, 1:MAXBLK + 1].unsqueeze(1).to_broadcast([128, 2 * TT, MAXBLK]),
                                   blk_.unsqueeze(2).to_broadcast([128, 2 * TT, MAXBLK]), ALU.is_equal))
            pay = C["payload"].rearrange("p (x c) -> p x c", c=2)
            for c in range(2):
                ins = dve.tensor_tensor(blks[:, :, 1 + c, :], blks[:, :, 0, :],
                                        pay[:, :, c:c + 1].to_broadcast([128, 2 * TT, MAXBLK]), ALU.mult)
                ins.then_inc(s["listed"], 1)
            nv = ovn[0:1, 0:NOV * 32].rearrange("p (o e) -> p o e", e=32)
            then(dve.tensor_tensor(nv, C["ovid"][0:1, :].unsqueeze(2).to_broadcast([1, NOV, 32]),
                                   incl[0:1, :].unsqueeze(1).to_broadcast([1, NOV, 32]), ALU.is_ge))
            then(dve.tensor_reduce(oveif[0:1, :], nv, AX.X, ALU.add))
            then(dve.tensor_scalar(oveif[0:1, :], oveif[0:1, :], float(NE - 1), None, ALU.min))
            then(dve.tensor_scalar(ovn[0:1, 0:NOV // 2], C["two"][0:1, 0:NOV // 2], incl[0:1, 31:32], None, ALU.is_lt))
            then(dve.tensor_reduce(npf[0:1, 1:2], ovn[0:1, 0:NOV // 2], AX.X, ALU.add))
            then(dve.tensor_scalar(nint[0:1, 0:1], npf[0:1, 1:2], float(NE // 2), None, ALU.add))
            then(dve.tensor_copy(nint[0:1, 1:3], C["iota"][0:1, NE - 2:NE]))
            then(dve.tensor_copy(nint[0:1, 3:3 + NOV], oveif[0:1, :]))
            dve.sem_inc(s["count_ready"], 1)
            dve.wait_ge(s["g_exp"], 1)
            then(dve.tensor_reduce(gw, gexp, AX.X, ALU.add))
            dve.wait_ge(s["g_exp"], 2)
            then(dve.scalar_tensor_tensor(eden, eex, 1.0, gw, ALU.add, ALU.mult))
            then(dve.reciprocal(wts[:, 0, :], eden))
            then(dve.tensor_tensor(wts[:, 1, :], wts[:, 0, :], eex, ALU.mult))
            n_pair = dve.value_load(nint[0:1, 0:1], min_val=NE // 2, max_val=MAXBLK // 2)
            dve.wait_ge(s["lists_summed"], 1)
            dve.wait_ge(s["zeroed"], 4)
            ls = B[5][:, 0:3 * MAXBLK].rearrange("p (c b) -> p c b", c=3)
            free = ovt[:, 0:MAXBLK]
            then(dve.tensor_scalar(free, ls[:, 0, :], -1.0, 1.0, ALU.mult, ALU.add))
            then(dve.scalar_tensor_tensor(free, free, C["dump"], ls[:, 2, :], ALU.mult, ALU.add))
            then(dve.tensor_scalar(tblS[:, 0, 0:MAXBLK], ls[:, 1, :], C["half"], None, ALU.add))
            then(dve.tensor_scalar(tblS[:, 1, 0:MAXBLK], free, C["half"], None, ALU.add))

            dve.sem_inc(s["listed_rows"], 1)
            with dve.Fori(0, n_pair) as i:
                for p in range(2):
                    dve.wait_ge(s["silu_ready"], 2 * i + p + 1)
                    dve.tensor_tensor(aa[p], gs[p], B[2][:, 0:256], ALU.mult).then_inc(s["act_ready"], 1)
                    dve.wait_ge(s["down"], 2 * i + p + 1)
                    dve.wait_ge(y_scat[p], 16 * i + 16)
                    dve.tensor_copy(Yo[p], B[4 + p][:, :]).then_inc(s["y_out"], 1)
            def combine(t):
                r = min(128, NT - 128 * t)
                dve.wait_ge(y_back[t], 32)
                dve.wait_ge(s["weighted"], t + 1)
                dve.scalar_tensor_tensor(yc[t % 2][0:r, :], yb[t][1][0:r, :], wts[0:r, 1, t:t + 1], yc[t % 2][0:r, :],
                                         ALU.mult, ALU.add).then_inc(s["combined"], 1)
            combine(0)
            for t in range(TT):
                if t < TT - 1:
                    combine(t + 1)
                for f in range(2):
                    dve.wait_ge(s["c_turned"], 2 * t + f + 1)
                    bank = B[2 * (t % 2) + f]
                    if t < TT - 1:
                        for k in range(4 * f, 4 * f + 4):
                            x = xP[:, k, 128 * t:128 * t + 128]
                            dve.scalar_tensor_tensor(x, bank[:, (k % 4) * 128:(k % 4) * 128 + 128], modT[:, 5 * KT + k, 0:1], x,
                                                     ALU.mult, ALU.add).then_inc(s["final"], 1)
                    else:
                        if f:
                            dve.wait_ge(s["final"], KT * t + f)
                        add = part[:, 0:4 * NS].rearrange("p (k b q) -> p k b q", k=4, b=NB)
                        then(dve.tensor_tensor(
                            add, bank[:, :].rearrange("p (k t) -> p k t", k=4)[:, :, 0:NS].rearrange("p k (b q) -> p k b q", b=NB),
                            modT[:, 5 * KT + 4 * f:5 * KT + 4 * f + 4, 1:NSEQ].unsqueeze(3).to_broadcast([128, 4, NB, NQ]), ALU.mult))
                        dve.tensor_tensor(xS[:, 4 * f:4 * f + 4, :], xS[:, 4 * f:4 * f + 4, :],
                                          part[:, 0:4 * NS].rearrange("p (k t) -> p k t", k=4), ALU.add).then_inc(s["final"], 1)

        @block.tensor
        def _(pe):
            pe.sem_inc(s["ada_part"], 4)
            pe.sem_inc(s["sq_summed"], 1)
            pe.sem_inc(s["ada_done"], 2)
            pe.sem_inc(s["s_out"], 2)
            pe.sem_inc(s["g_summed"], 2)
            pe.sem_inc(s["turned"], 1)
            pe.sem_inc(s["turned_out"], 1)
            pe.sem_inc(s["newT"], 1)
            pe.sem_inc(s["o_sum"], 1)
            pe.sem_inc(s["o_scaled"], 1)
            pe.sem_inc(s["oT_out"], 1)
            pe.sem_inc(s["mixP"], 1)
            pe.sem_inc(s["p_stored"], 1)
            pe.sem_inc(s["p_logits"], 1)
            pe.sem_inc(s["p_turned_out"], 1)
            pe.sem_inc(s["y_out"], 2)
            pe.wait_ge(s["zeroed"], 4)
            pe.wait_ge(s["silu"], 1)
            norm_pe(pe, s["squared"], s["sums"])
            with pe.Fori(0, 3) as it:
                def columns(u):
                    pe.wait_ge(s["ada_copied"], 4 * it + u + 1)
                    pe.wait_ge(s["ada_done"], 4 * it + u + 1)
                    for c in range(4):
                        last = pe.matmul(B[2 + u % 2][:, NSEQ * c:NSEQ * (c + 1)], (part[:, :], part2)[u % 2][:, 128 * c:128 * c + 128],
                                         C["sel"], start=True, stop=True)
                    last.then_inc(s["ada_cols"], 1)
                for u in range(4):
                    pe.wait_ge(w_full[u], 16 * it + 16)
                    for k in range(KT):
                        j = k % 4
                        last = pe.matmul(B[u % 2][32 * j:32 * j + 32, :], scT[:, k, :], slot[u][:, k, :], start=k < 4, stop=k >= 4)
                    last.then_inc(s["ada_part"], 1)
                    if u:
                        columns(u - 1)
                columns(3)
            pe.wait_ge(s["h_scaled"], 1)
            for n, units in enumerate(((0, 1), (3, 2))):
                for i in units:
                    pe.wait_ge(w_full[i], 16 * 4)
                for k in range(KT):
                    for h, i in enumerate(units):
                        last = pe.matmul(B[5 + n][64 * h:64 * h + 64, :], hS[:, k, :], slot[i][:, k, :],
                                         start=k == 0, stop=k == KT - 1)
                last.then_inc(s["zS"], 1)
            for n in range(2):
                pe.wait_ge(s["zS_copied"], n + 1)
                for c in range(4):
                    last = pe.transpose(B[n][:, 128 * c:128 * c + 128], zst[n][:, 128 * c:128 * c + 128], C["ident"])
                last.then_inc(s["zS_turned"], 1)
            pe.wait_ge(s["zS_out"], 4)

            def head_sum(i):
                w = pieces[i][0].shape[1]
                pe.wait_ge(s["hsq"], i + 1)
                if i == 1:
                    pe.wait_ge(s["hroot"], 1)
                pe.matmul(hbank[i][:, 0:w], C["heads"], hsq[i][:, 0:w], start=True, stop=True).then_inc(s["hsum"], 1)
            head_sum(0)
            head_sum(1)

            def pe_batch(b, extra):
                pe.wait_ge(s["q_staged"], b + 1)
                for j in range(4):
                    last = pe.matmul(B[3][32 * j:32 * j + 32, 0:NS], qst[:, j, :], kS[:, j, :], start=True, stop=True)
                last.then_inc(s["new_scored"], 1)
                for c in range(NCH):
                    pe.wait_ge(k_full[c % 4], 16 * PPC * (2 * b + c // 4 + 1))
                    pe.wait_ge(s["g_summed"], NCH * b + c + 1)
                    for j in range(4):
                        last = pe.matmul(B[c % 2][32 * j:32 * j + 32, :], qst[:, j, :], kslot[c % 4][:, :, j, :],
                                         start=True, stop=True)
                    last.then_inc(s["k_used"], 1)
                    extra("q", c)

                def values(t):
                    for j in range(4):
                        rhs = vslot[t // 4][:, t % 4, 128 * j:128 * j + 128] if t < 32 else vS[:, 128 * j:128 * j + 128]
                        last = pe.matmul(B[4][32 * j:32 * j + 16, 0:128], PT[:, t, 16 * j:16 * j + 16], rhs,
                                         start=t == 0, stop=t == 32)
                    return last

                def chunk_values(g):
                    if g == 0:
                        pe.wait_ge(s["o_scaled"], b + 1)
                    pe.wait_ge(s["turned_out"], 8 * b + g + 2)
                    pe.wait_ge(v_full[g], 16 * PPC * (b + 1))
                    for t in range(4 * g, 4 * g + 4):
                        last = values(t)
                    last.then_inc(s["v_used"], 1)
                    extra("v", g)
                for g in range(8):
                    pe.wait_ge(s["probs"], 17 * b + 2 * g + 2)
                    if g >= 2:
                        pe.wait_ge(s["turned_out"], 8 * b + g)
                    for t in range(4):
                        a = (4 * g + t) * 128
                        last = pe.transpose(B[g % 2][:, 128 * t:128 * t + 128], L[:, a:a + 128], C["ident"])
                    last.then_inc(s["turned"], 1)
                    if g:
                        chunk_values(g - 1)
                pe.wait_ge(s["probs"], 17 * b + 17)
                pe.wait_ge(s["oT_out"], 2 * b + 1)
                pe.transpose(B[2][:, 128:256], L[:, PAST:PAST + 128], C["ident"]).then_inc(s["newT"], 1)
                chunk_values(7)
                pe.wait_ge(s["newT_out"], b + 1)
                values(32).then_inc(s["o_sum"], 1)
                extra("e", 0)
                pe.wait_ge(s["o_scaled"], b + 2)
                pe.transpose(B[2][:, 256:384], On, C["ident"]).then_inc(s["oT"], 1)

            pe.wait_ge(s["h_ready"], KT)
            for b in range(4):
                def tiles(kind, c):
                    if (b, kind, c) in sum_at:
                        if kind == "v" and c == 1:
                            pe.wait_ge(s["zP_out"], 4 * (b + 1))
                        if kind == "q":
                            pe.wait_ge(s["new_out"], b + 1)
                        head_sum(sum_at[b, kind, c])
                    if b == 3 and kind == "v" and 2 <= c < 6:
                        g = c - 2
                        if g == 0:
                            pe.wait_ge(s["pooled"], 4)
                            pe.wait_ge(s["zP_out"], 16)
                            pe.wait_ge(s["wpool_in"], 16)
                        if g >= 2:
                            pe.wait_ge(s["ypool_out"], g - 1)
                        pe.matmul(B[5 + g % 2][:, :], wpool[:, g, :], uX[:, g, HIST:HIST + NP], start=True, stop=True)
                        pe.matmul(B[7 - 4 * (g % 2)][:, 0:NS], wpool[:, g, :], uxs[:, g, :, HIST:US], start=True, stop=True)\
                            .then_inc(s["ypool"], 1)
                    for m in z_at[b].get((kind, c), ()):
                        if m == 0:
                            pe.wait_ge(s["w2_full"], 16 * (b + 1))
                            if b:
                                pe.wait_ge(s["zP_out"], 4 * b)
                        if m in (1, 2) and b >= 2:
                            pe.wait_ge(s["hroot"], 4 * b - 5 + m)
                        if m == 3:
                            pe.wait_ge(s["zP_out"], 4 * b + 1)
                        for k in range(KT):
                            if b < 3:
                                last = pe.matmul(zbank[m][:, :], w2[:, k, 128 * m:128 * m + 128], hP[:, k, :],
                                                 start=k == 0, stop=k == KT - 1)
                            else:
                                last = pe.matmul(zbank[m][:, :], hP[:, k, 128 * m:128 * m + 128], w2[:, k, :],
                                                 start=k == 0, stop=k == KT - 1)
                        last.then_inc(s["zP"], 1)
                pe_batch(b, tiles)
            pe.wait_ge(s["ypool_out"], 4)
            with pe.Fori(4, NB) as b:
                def prompt_step(kind, c):
                    n = 8 * (b - 4)
                    if (kind, c) in turn_of:
                        e = turn_of[kind, c]
                        h, i = steps[e]
                        pe.wait_ge(s["p_prob"], n + e + 1)
                        pe.wait_ge(s["p_turned_out"], n + e + 1)
                        for t in range(i + 1):
                            last = pe.transpose(B[6][:, 128 * t:128 * t + 128], plog[h][:, 128 * t:128 * t + 128], C["ident"])
                        last.then_inc(s["p_turned"], 1)
                    if (kind, c) in score_of:
                        e = score_of[kind, c]
                        h, i = steps[e]
                        if e == 0:
                            pe.wait_ge(s["staged"], 4 * (b - 4) + 3)
                        pe.wait_ge(s["p_logits"], n + e + 1)
                        pe.matmul(B[5][:, 0:128 * (i + 1)], pq[64 * h:64 * h + 64, 128 * i:128 * i + 128],
                                  pk[64 * h:64 * h + 64, 0:128 * (i + 1)], start=True, stop=True).then_inc(s["p_scores"], 1)
                    if kind == "e":
                        pe.wait_ge(s["staged"], 4 * (b - 4) + 4)
                        pe.wait_ge(s["p_turned_out"], n + 9)
                        pe.wait_ge(s["p_stored"], b - 4 + 1)
                        for t in range(4):
                            for h in range(2):
                                last = pe.matmul(B[7][64 * h:64 * h + 64, 128 * t:NP], pv[:, t, 64 * h:64 * h + 64],
                                                 pPT[h][:, t, 128 * t:NP], start=t == 0, stop=t == 3)
                        last.then_inc(s["mixP"], 1)
                pe_batch(b, prompt_step)
            pe.wait_ge(s["oT_out"], 1 + 2 * NB)
            pe.wait_ge(s["p_stored"], 5)
            for m in range(KT):
                if m % 4 == 0:
                    pe.wait_ge(s[f"wo_full{m // 4}"], 16)
                if m >= 2:
                    pe.wait_ge(s["res1"], m - 1)
                for k in range(KT):
                    last = pe.matmul(B[m % 2][:, :], slot[m // 4][:, k, 128 * (m % 4):128 * (m % 4) + 128], mP[:, k, :],
                                     start=k == 0, stop=k == KT - 1)
                last.then_inc(s["mixP"], 1)
                if m == 3:
                    pe.wait_ge(s["wo_full1"], 16)
                    for k in range(KT):
                        for h in range(2):
                            last = pe.matmul(B[2][64 * h:64 * h + 64, :], mS[:, k, :], slot[h][:, k, :],
                                             start=k == 0, stop=k == KT - 1)
                    last.then_inc(s["mixS"], 1)
                if m == 4:
                    pe.wait_ge(s["mixS_copied"], 1)
                    for c in range(4):
                        last = pe.transpose(B[3][:, 128 * c:128 * c + 128], zoS[:, 128 * c:128 * c + 128], C["ident"])
                    last.then_inc(s["mixS_turned"], 1)
            pe.wait_ge(s["sq_summed"], KT)
            for x in range(TT):
                last = pe.matmul(B[4][:, x:x + 1], big[:, 128 * x:128 * x + 128], ones[:, 0:1], start=True, stop=True)
            last.then_inc(s["sums2"], 1)
            pe.wait_ge(s["rms_spread"], 1)
            pe.matmul(B[5][:, :], ones[:, :], spread[:, 0:NP], start=True, stop=True)
            pe.matmul(B[7][:, 0:NS], ones[:, :], spread[:, NP:NT], start=True, stop=True).then_inc(s["rms_out"], 1)

            def tok(k, t):
                return hP[:, k, 128 * t:128 * t + 128] if t < 4 else hS[:, k, :]
            pe.wait_ge(s["h_scaled2"], 1)
            for k in range(KT):
                pe.wait_ge(s["h2_ready"], k + 1)
                h = k % 2
                pe.matmul(B[6][64 * h:64 * h + 64, :], wrt[:, k, :], hP[:, k, :], start=k < 2, stop=k >= KT - 2)
                last = pe.matmul(B[7][64 * h:64 * h + 64, 0:NS], wrt[:, k, :], hS[:, k, :], start=k < 2, stop=k >= KT - 2)
            last.then_inc(s["route_parts"], 1)
            pe.wait_ge(s["route_copied"], 1)
            for t in range(TT):
                r = min(128, NT - 128 * t)
                last = pe.matmul(B[4][0:r, 36 * t:36 * t + 36], zr[:, 128 * t:128 * t + r], halves, start=True, stop=True)
            last.then_inc(s["route_scores"], 1)
            for t in range(2 * TT):
                r = min(128, NT - 128 * (t // 2))
                if t >= 2:
                    pe.wait_ge(s["h2_out"], t - 1)
                for k in range(4):
                    last = pe.transpose(B[t % 2][0:r, 128 * k:128 * k + 128], tok(4 * (t % 2) + k, t // 2), C["ident"])
                last.then_inc(s["h2_turn"], 1)
            pe.wait_ge(s["hot"], 1)
            pe.matmul(B[7][:, 0:32 * TT], ones[:, :], cnt[:, 0:TT, :].rearrange("p t e -> p (t e)"), start=True, stop=False)
            pe.matmul(B[7][:, 0:32 * TT], C["before"], hotm.rearrange("p t e -> p (t e)"), start=False, stop=True)
            pe.matmul(B[7][:, 32 * TT:32 * TT + 32], ones[:, :], cnt[:, TT, :], start=True, stop=True).then_inc(s["ranked"], 1)
            pe.wait_ge(s["listed"], 2)
            for x in range(2 * TT):
                last = pe.matmul(B[5][:, 0:3 * MAXBLK], rows[:, x, :, :].rearrange("p h r -> p (h r)"),
                                 blks[:, x, :, :].rearrange("p c b -> p (c b)"), start=x == 0, stop=x == 2 * TT - 1)
            last.then_inc(s["lists_summed"], 1)
            pe.wait_ge(s["count_ready"], 1)
            n_pair = pe.value_load(nint[0:1, 0:1], min_val=NE // 2, max_val=MAXBLK // 2)

            def turn_rows(p):
                for c in range(4):
                    last = pe.transpose(B[0][:, 128 * c:128 * c + 128], Xg[p][:, 128 * c:128 * c + 128], C["ident"])
                last.then_inc(s["x_turned"], 1)
            pe.wait_ge(gathered[0], 16)
            turn_rows(0)
            with pe.Fori(0, n_pair) as i:
                for p in range(2):
                    xv = XT[p].rearrange("q (c h r) -> q c h r", c=4, h=2)
                    pe.wait_ge(s["xT_ready"], 2 * i + p + 1)
                    for w in range(2):
                        pe.wait_ge(e_full[p][w], 16 * i + 16)
                        wv = eslot[p][w].rearrange("q (k n) -> q k n", k=KT)
                        for k in range(KT):
                            h, c = divmod(k, 4)
                            for f in range(2):
                                last = pe.matmul(B[1 + w][64 * f:64 * f + 64, 0:256], xv[:, c, h, :],
                                                 wv[:, k, 256 * f:256 * f + 256], start=k == 0, stop=k == KT - 1)
                        if w == 0:
                            last.then_inc(s["gate_done"], 1)
                    last.then_inc(s["gate_up"], 1)
                    pe.wait_ge(gathered[1 - p], 16 * i + 16 * (p + 1))
                    turn_rows(1 - p)
                    pe.wait_ge(s["act_ready"], 2 * i + p + 1)
                    for c in range(2):
                        last = pe.transpose(B[3][:, 128 * c:128 * c + 128], aa[p][:, 128 * c:128 * c + 128], C["ident"])
                    last.then_inc(s["a_turned"], 1)
                    pe.wait_ge(s["aT_ready"], 2 * i + p + 1)
                    pe.wait_ge(e_full[p][2], 16 * i + 16)
                    pe.wait_ge(s["y_out"], 2 * i + p + 1)
                    av = aT[p].rearrange("q (c f r) -> q c f r", c=2, f=2)
                    wv = eslot[p][2].rearrange("q (k n) -> q k n", k=FF // 128)
                    for k in range(FF // 128):
                        f, c = divmod(k, 2)
                        for h in range(2):
                            last = pe.matmul(B[4 + p][64 * h:64 * h + 64, :], av[:, c, f, :], wv[:, k, 512 * h:512 * h + 512],
                                             start=k == 0, stop=k == FF // 128 - 1)
                    last.then_inc(s["down"], 1)
            for t in range(TT):
                r = min(128, NT - 128 * t)
                pe.wait_ge(s["combined"], t + 1)
                if t >= 2:
                    pe.wait_ge(s["final"], KT * (t - 1))
                for k in range(KT):
                    last = pe.transpose(B[2 * (t % 2) + k // 4][:, 128 * (k % 4):128 * (k % 4) + r],
                                        yc[t % 2][0:r, 128 * k:128 * k + 128], C["ident"][0:r, 0:r])
                    if k % 4 == 3:
                        last.then_inc(s["c_turned"], 1)


def constants():
    lay, width = const_layout()
    c = np.zeros((128, width), np.float32)

    def put(name, a):
        at, w = lay[name]
        c[:a.shape[0], at:at + w] = a.reshape(a.shape[0], -1)
    p = np.arange(128)
    put("ident", np.eye(128))
    put("sel", (p[:, None] % 32 == np.arange(NSEQ)[None]) * 1.0)
    put("heads", (p[:, None] // 64 == p[None] // 64) * 1.0)
    put("before", (p[:, None] < p[None]) * 1.0)
    rel = (np.arange(NP) - (NP - 128))[None] - p[:, None]
    put("causal", np.where(rel <= 0, rel, -1e32))
    r = p % 32
    live = r < 2 * NQ
    head = 2 * (p // 32) + r // NQ
    slope = np.where(live, 2.0 ** -(head + 1.0), 0.0)[:, None]
    q = (r % NQ)[:, None]
    put("jbias", slope * np.arange(BLK)[None])
    put("blockoff", slope * (BLK * np.arange(NBLK)[None] - PAST - q))
    sb_, si = np.arange(NS) // NQ, np.arange(NS) % NQ
    ok = (sb_[None, None] == np.arange(NB)[None, :, None]) & (si[None, None] <= q[:, :, None])
    nbias = np.where(ok, slope[:, :, None] * (si[None, None] - q[:, :, None]), OFF)
    put("newbias", np.where(live[:, None, None], nbias, 0.0))
    put("iota", np.tile(np.arange(64), (128, 1)))
    t = np.arange(16)
    put("share", np.tile(np.concatenate([1.0 / np.minimum(t + 1, 2 << g) for g in range(4)]), (128, 1)))
    tok = 128 * np.arange(TT)[None] + p[:, None]
    put("valid", (tok < NT) * 1.0)
    put("payload", np.stack([np.stack([2 * tok, 2 * (k * NT + tok)], -1) for k in range(2)], 2))
    put("thr", np.tile(RB * (np.arange(16) + 1), (128, 1)))
    put("slopes", np.tile(2.0 ** -(np.arange(NH) + 1.0), (128, 1)))
    put("eps", np.full((128, 1), EPS))
    put("two", np.tile(2 * np.arange(16), (128, 1)))
    put("half", p[:, None] // RB)
    put("dump", 2 * (2 * NT + p[:, None] % RB))
    put("ovid", np.tile(np.arange(NOV), (128, 1)))
    return c


def kernel(**inputs):
    import numpy as _np
    import concourse.bacc as _bacc
    from concourse import mybir as _mybir
    from concourse.bass_utils import run_bass_kernel_spmd as _run

    a = {k: _np.asarray(v) for k, v in inputs.items()}
    cc = _np.ascontiguousarray
    cols = lambda v: v.reshape(-1, 128).T
    x = _np.concatenate([a["x_prompt"].reshape(NP, D), a["x_sample"].reshape(NS, D)])
    c9 = _np.concatenate([a["c_prompt"], a["c_sample"]])
    nph = a["cache_k"].shape[1]
    gq, gk = (_np.concatenate([a[n][0], a[n][0]])[:, None] for n in ("g_q", "g_k"))
    arr = {
        "xT": cc(x.T), "cT": cc(c9.T), "consts": constants(), "pages": a["page_table"].reshape(1, -1),
        "b_ada": cc(_np.broadcast_to(cols(a["b_ada"][0])[:, :, None], (128, 6 * KT, NSEQ))),
        "gcols": cc(_np.concatenate([cols(a["g_attn_norm"][0]), cols(a["g_ffn_norm"][0]), gq, gk, cols(a["pool_scale"][0])], 1)),
        "w_ada": a["w_ada"][0], "w_in": a["w_in"][0], "w_out": a["w_out"][0], "w_pool": a["w_pool"][0],
        "histT": cc(a["state_pool"][0].transpose(2, 0, 1)),
        "kT": cc(a["cache_k"][0].reshape(nph, PAGE, 4, 128).transpose(0, 3, 2, 1)),
        "v": a["cache_v"][0].reshape(nph, PAGE, AW),
        "w_route": cc(_np.concatenate([a["w_group"][0], a["w_expert"][0], _np.zeros((D, 28), _np.float32)], 1)),
        "b_route": cc(_np.broadcast_to(_np.concatenate([a["b_group"][0], a["b_expert"][0]])[None], (128, 36))),
        "w_gate": a["w_gate"][0], "w_up": a["w_up"][0], "w_down": a["w_down"][0],
    }
    outs = {"yT": (D, NT), "kT": (AW, NT), "v": (NT, AW), "poolT": (PW, NSEQ, HIST)}
    nc = _bacc.Bacc("TRN2", target_bir_lowering=False, num_devices=1)
    d = {n: nc.dram_tensor(f"in_{n}", v.shape, _mybir.dt.from_np(v.dtype), kind="ExternalInput").ap() for n, v in arr.items()}
    o = {n: nc.dram_tensor(f"out_{n}", sh, _mybir.dt.float32, kind="ExternalOutput").ap() for n, sh in outs.items()}
    build_kernel(nc, d, o)
    r = _run(nc, [{f"in_{n}": cc(v) for n, v in arr.items()}], core_ids=[0]).results[0]
    y, k, v, pl = (_np.asarray(r[f"out_{n}"]) for n in ("yT", "kT", "v", "poolT"))
    y, k, pl = y.T, k.T, pl.transpose(1, 2, 0)
    return (cc(y[:NP]).reshape(1, NP, D), cc(y[NP:]).reshape(NB, NQ, D),
            cc(k[:NP]).reshape(1, 1, NP, NH, HD), cc(v[:NP]).reshape(1, 1, NP, NH, HD), cc(pl[:1]).reshape(1, 1, HIST, PW),
            cc(k[NP:]).reshape(1, NB, NQ, NH, HD), cc(v[NP:]).reshape(1, NB, NQ, NH, HD), cc(pl[1:]).reshape(1, NB, HIST, PW))
```
